# Optimizing a Trainium2 kernel written in Bass

```python
import math
import jax, jax.numpy as jnp
from jax import lax
import numpy as np

D_MODEL = 2048
BATCH = 1
SEQ = 1024
DEPTH = 1
DEC_BATCH = 8
DEC_SEQ = 16
PAST_LEN = 256

CHUNK = 64
Q_BLOCK = 128
D_ATTN = 1024
N_HEADS = 8
N_KV_HEADS = 2
HEAD_DIM = 128
KV_DIM = N_KV_HEADS * HEAD_DIM
N_IDX_HEADS = 16
IDX_DIM = 64
TOPK_MAX = 256
D_SSM = 1024
SSM_GROUP = 16
N_SSM_GROUPS = D_SSM // SSM_GROUP
SSM_STATE = 64
D_MIX = D_ATTN + D_SSM
RMS_EPS = 1e-6
IN_SIZES = (D_ATTN, KV_DIM, KV_DIM, N_IDX_HEADS * IDX_DIM, IDX_DIM, N_IDX_HEADS, D_ATTN, D_SSM, D_SSM)
IN_COLS = sum(IN_SIZES)

kernel_name = "hymba_dsa_s5_streaming_step"

def _rmsnorm(x, g):
    xf = x.astype(jnp.float32)
    y = xf * lax.rsqrt(jnp.mean(xf * xf, axis=-1, keepdims=True) + RMS_EPS)
    return (y * g.astype(jnp.float32)).astype(x.dtype)

def _split_cols(z):
    offs = []
    acc = 0
    for s in IN_SIZES[:-1]:
        acc += s
        offs.append(acc)
    return jnp.split(z, offs, axis=-1)

def _dsa_block(q, iq, iw, k, v, ik, limit, topk):
    f32 = jnp.float32
    bsz, nq = q.shape[:2]
    n_keys = k.shape[1]
    s = jnp.einsum('bqhd,bsd->bqhs', iq.astype(f32), ik.astype(f32)) * (IDX_DIM ** -0.5)
    score = jnp.einsum('bqhs,bqh->bqs', jax.nn.relu(s), iw.astype(f32))
    visible = jnp.arange(n_keys, dtype=jnp.int32)[None, :] < limit[:, None]
    score = jnp.where(visible[None], score, -jnp.inf)
    _, idx = lax.top_k(score, topk)
    valid = idx < limit[None, :, None]
    kg = jax.vmap(lambda a, i: a[i])(k, idx)
    vg = jax.vmap(lambda a, i: a[i])(v, idx)
    qg = q.reshape(bsz, nq, N_KV_HEADS, N_HEADS // N_KV_HEADS, HEAD_DIM).astype(f32)
    logits = jnp.einsum('bqhgd,bqnhd->bqhgn', qg, kg.astype(f32)) * (HEAD_DIM ** -0.5)
    logits = jnp.where(valid[:, :, None, None, :], logits, -jnp.inf)
    p = jax.nn.softmax(logits, axis=-1)
    o = jnp.einsum('bqhgn,bqnhd->bqhgd', p, vg.astype(f32))
    return o.reshape(bsz, nq, D_ATTN).astype(q.dtype)

def _dsa_prompt(q, k, v, iq, ik, iw):
    bsz, s = q.shape[:2]
    nb = s // Q_BLOCK
    topk = min(TOPK_MAX, s // 4)
    lim = (((jnp.arange(s, dtype=jnp.int32) // CHUNK) + 1) * CHUNK).reshape(nb, Q_BLOCK)

    def blocks(a):
        return jnp.moveaxis(a.reshape((bsz, nb, Q_BLOCK) + a.shape[2:]), 1, 0)

    def one(args):
        qb, iqb, iwb, lb = args
        return _dsa_block(qb, iqb, iwb, k, v, ik, lb, topk)

    out = lax.map(one, (blocks(q), blocks(iq), blocks(iw), lim))
    return jnp.moveaxis(out, 0, 1).reshape(bsz, s, D_ATTN)

def _s5(u, h0, lam_re, lam_im, log_dt, b_re, b_im, c_re, c_im, d_skip):
    f32 = jnp.float32
    bsz, s, _ = u.shape
    t_len = CHUNK if s % CHUNK == 0 else s
    n_chunks = s // t_len
    lam = lax.complex(lam_re.astype(f32), lam_im.astype(f32))
    lam_dt = lam * jnp.exp(log_dt.astype(f32))[:, None]
    lam_bar = jnp.exp(lam_dt)
    b_bar = ((lam_bar - 1.0) / lam)[..., None] * lax.complex(b_re.astype(f32), b_im.astype(f32))
    decay = jnp.exp(lam_dt[None] * jnp.arange(1, t_len + 1, dtype=f32)[:, None, None])
    cr = c_re.astype(f32)
    ci = c_im.astype(f32)
    uc = jnp.moveaxis(u.astype(f32).reshape(bsz, n_chunks, t_len, N_SSM_GROUPS, SSM_GROUP), 1, 0)

    def combine(l, r):
        a_l, b_l = l
        a_r, b_r = r
        return a_r * a_l, a_r * b_l + b_r

    def step(h, u_blk):
        bu = jnp.einsum('gpc,btgc->btgp', b_bar, u_blk.astype(jnp.complex64))
        a = jnp.broadcast_to(lam_bar, bu.shape)
        _, hs = lax.associative_scan(combine, (a, bu), axis=1)
        hs = hs + decay[None] * h[:, None]
        y = jnp.einsum('gcp,btgp->btgc', cr, hs.real) - jnp.einsum('gcp,btgp->btgc', ci, hs.imag)
        return hs[:, -1], y

    h_last, ys = lax.scan(step, h0, uc)
    y = jnp.moveaxis(ys, 0, 1).reshape(bsz, s, D_SSM) + d_skip.astype(f32) * u.astype(f32)
    return y, h_last

def _layer(x, c, past, w_ada, b_ada, g_pre, g_post, w_in, lam_re, lam_im, log_dt,
           b_re, b_im, c_re, c_im, d_skip, w_glu, b_glu, w_out):
    bsz, s, _ = x.shape
    mod = c @ w_ada + b_ada
    shift, scale, gate = jnp.split(mod[:, None, :], 3, axis=-1)
    h = _rmsnorm(x, g_pre) * (1.0 + scale) + shift
    z = h @ w_in
    q, k, v, iq, ik, iw, za, u, zs = _split_cols(z)
    q = q.reshape(bsz, s, N_HEADS, HEAD_DIM)
    k = k.reshape(bsz, s, N_KV_HEADS, HEAD_DIM)
    v = v.reshape(bsz, s, N_KV_HEADS, HEAD_DIM)
    iq = iq.reshape(bsz, s, N_IDX_HEADS, IDX_DIM)
    iw = iw * (N_IDX_HEADS ** -0.5)
    if past is None:
        attn = _dsa_prompt(q, k, v, iq, ik, iw)
        h0 = jnp.zeros((bsz, N_SSM_GROUPS, SSM_STATE), jnp.complex64)
    else:
        ck, cv, cik, sre, sim = past
        k_all = jnp.concatenate([ck.astype(k.dtype), k], axis=1)
        v_all = jnp.concatenate([cv.astype(v.dtype), v], axis=1)
        ik_all = jnp.concatenate([cik.astype(ik.dtype), ik], axis=1)
        n_keys = k_all.shape[1]
        topk = min(TOPK_MAX, n_keys // 4)
        lim = jnp.full((s,), n_keys, dtype=jnp.int32)
        attn = _dsa_block(q, iq, iw, k_all, v_all, ik_all, lim, topk)
        h0 = lax.complex(sre.astype(jnp.float32), sim.astype(jnp.float32))
    attn = attn * jax.nn.silu(za)
    y_ssm, h_last = _s5(u, h0, lam_re, lam_im, log_dt, b_re, b_im, c_re, c_im, d_skip)
    y_ssm = jax.nn.gelu(y_ssm.astype(x.dtype))
    y_ssm = y_ssm * jax.nn.sigmoid(y_ssm @ w_glu + b_glu)
    y_ssm = y_ssm * jax.nn.silu(zs)
    out = jnp.concatenate([attn, y_ssm], axis=-1) @ w_out
    y = x + gate * _rmsnorm(out, g_post)
    return y, (k, v, ik, h_last.real.astype(x.dtype), h_last.imag.astype(x.dtype))

def setup_inputs(seed: int = 0) -> dict:
    key = jax.random.key(seed)
    ks = jax.random.split(key, 32)
    f32 = jnp.float32

    def nrm(k, shape, sd):
        return sd * jax.random.normal(k, shape, f32)

    G, P, Cg = N_SSM_GROUPS, SSM_STATE, SSM_GROUP
    b_ada = jnp.concatenate([nrm(ks[20], (DEPTH, 2 * D_MODEL), 0.02),
                             1.0 + nrm(ks[21], (DEPTH, D_MODEL), 0.02)], axis=-1)
    return {
        "x_prompt": nrm(ks[0], (BATCH, SEQ, D_MODEL), 1.0),
        "x_sample": nrm(ks[1], (DEC_BATCH, DEC_SEQ, D_MODEL), 1.0),
        "c_prompt": nrm(ks[2], (BATCH, D_MODEL), 1.0),
        "c_sample": nrm(ks[3], (DEC_BATCH, D_MODEL), 1.0),
        "cache_k": nrm(ks[4], (DEPTH, DEC_BATCH, PAST_LEN, N_KV_HEADS, HEAD_DIM), 1.0),
        "cache_v": nrm(ks[5], (DEPTH, DEC_BATCH, PAST_LEN, N_KV_HEADS, HEAD_DIM), 1.0),
        "cache_idx_k": nrm(ks[6], (DEPTH, DEC_BATCH, PAST_LEN, IDX_DIM), 1.0),
        "state_ssm_re": nrm(ks[7], (DEPTH, DEC_BATCH, G, P), 0.1),
        "state_ssm_im": nrm(ks[8], (DEPTH, DEC_BATCH, G, P), 0.1),
        "w_ada": nrm(ks[9], (DEPTH, D_MODEL, 3 * D_MODEL), 0.1 * D_MODEL ** -0.5),
        "b_ada": b_ada,
        "g_pre": 1.0 + nrm(ks[10], (DEPTH, D_MODEL), 0.02),
        "g_post": 1.0 + nrm(ks[11], (DEPTH, D_MODEL), 0.02),
        "w_in": nrm(ks[12], (DEPTH, D_MODEL, IN_COLS), D_MODEL ** -0.5),
        "lambda_re": -0.5 + nrm(ks[13], (DEPTH, G, P), 0.01),
        "lambda_im": jnp.pi * jnp.arange(P, dtype=f32)[None, None, :] + nrm(ks[14], (DEPTH, G, P), 0.01),
        "log_dt": jax.random.uniform(ks[15], (DEPTH, G), f32, math.log(1e-3), math.log(1e-1)),
        "b_re": nrm(ks[16], (DEPTH, G, P, Cg), (0.5 / Cg) ** 0.5),
        "b_im": nrm(ks[17], (DEPTH, G, P, Cg), (0.5 / Cg) ** 0.5),
        "c_re": nrm(ks[18], (DEPTH, G, Cg, P), (0.5 / P) ** 0.5),
        "c_im": nrm(ks[19], (DEPTH, G, Cg, P), (0.5 / P) ** 0.5),
        "d_skip": nrm(ks[22], (DEPTH, D_SSM), 1.0),
        "w_glu": nrm(ks[23], (DEPTH, D_SSM, D_SSM), D_SSM ** -0.5),
        "b_glu": nrm(ks[24], (DEPTH, D_SSM), 0.01),
        "w_out": nrm(ks[25], (DEPTH, D_MIX, D_MODEL), D_MIX ** -0.5),
    }

def reference(x_prompt, x_sample, c_prompt, c_sample, cache_k, cache_v, cache_idx_k,
              state_ssm_re, state_ssm_im, w_ada, b_ada, g_pre, g_post, w_in,
              lambda_re, lambda_im, log_dt, b_re, b_im, c_re, c_im, d_skip,
              w_glu, b_glu, w_out):
    yp, ys = x_prompt, x_sample
    kp, vp, ikp, srp, sip = [], [], [], [], []
    kd, vd, ikd, srd, sid = [], [], [], [], []
    for l in range(DEPTH):
        lw = (w_ada[l], b_ada[l], g_pre[l], g_post[l], w_in[l], lambda_re[l], lambda_im[l],
              log_dt[l], b_re[l], b_im[l], c_re[l], c_im[l], d_skip[l], w_glu[l], b_glu[l], w_out[l])
        yp, (k1, v1, ik1, r1, i1) = _layer(yp, c_prompt, None, *lw)
        past = (cache_k[l], cache_v[l], cache_idx_k[l], state_ssm_re[l], state_ssm_im[l])
        ys, (k2, v2, ik2, r2, i2) = _layer(ys, c_sample, past, *lw)
        kp.append(k1); vp.append(v1); ikp.append(ik1); srp.append(r1); sip.append(i1)
        kd.append(k2); vd.append(v2); ikd.append(ik2); srd.append(r2); sid.append(i2)
    return (yp, ys,
            jnp.stack(kp), jnp.stack(vp), jnp.stack(ikp), jnp.stack(srp), jnp.stack(sip),
            jnp.stack(kd), jnp.stack(vd), jnp.stack(ikd), jnp.stack(srd), jnp.stack(sid))


_drawn_inputs = setup_inputs


def setup_inputs(seed=0):
    import zlib

    import numpy as np

    out = dict(_drawn_inputs(seed))
    spreads = {}
    factors = {'g_post': 4.104, 'lambda_re': 3.687, 'b_glu': 8.0}
    for name, (base, spread) in spreads.items():
        noise = np.random.default_rng([zlib.crc32(name.encode()), seed]).standard_normal(out[name].shape)
        drawn = base * np.exp(spread * noise) if base else spread * noise
        out[name] = __import__('jax').numpy.asarray(drawn.astype(out[name].dtype))
    for name, factor in factors.items():
        out[name] = (out[name] * factor).astype(out[name].dtype)
    return out
```

```python
from contextlib import ExitStack

import concourse.bass as bass
import concourse.mybir as mybir
from concourse.alu_op_type import AluOpType as ALU

ACT = mybir.ActivationFunctionType
AX_X = mybir.AxisListType.X
F32 = mybir.dt.float32
F32R = mybir.dt.float32r
BF16 = mybir.dt.bfloat16
I32 = mybir.dt.int32

P = 128
D_MODEL = 2048
KB = D_MODEL // P
SEQ = 1024
DEC_B, DEC_S, PAST = 8, 16, 256
TOK = SEQ + DEC_B * DEC_S
NT = TOK // P
TC, NTC = 384, 3
COND = 1 + DEC_B
CHUNK = 64
TOPK = 256
DEC_KEYS = PAST + DEC_S
DEC_TOPK = min(256, DEC_KEYS // 4)
HEADS, KV_HEADS, HD = 8, 2, 128
IDX_HEADS, IDX_DIM = 16, 64
GROUPS, CH, STATE = 64, 16, 64
PAIRS = GROUPS // 2
STEP = 8
NSTEP = TOK // STEP
PSTEP = SEQ // STEP
TAPS = 2 * STEP - 1
EPS = 1e-6
COLS = 5712
Q0, K0, V0, IQ0, IK0, IW0, ZA0, U0, ZS0 = 0, 1024, 1280, 1536, 2560, 2624, 2640, 3664, 4688
PAIR_BATCH = 4
BATCHES = PAIRS // PAIR_BATCH
HALF = KB // 2

PI = 3.141592653589793
LN2 = 0.6931471805599453
TWO_PI_PARTS = (6.28125, 0.0019350051879882812, 3.019916050561733e-07)
LN2_PARTS = (0.693359375, -0.00021219444005469057)
ROUND = 12582912.0


def bc(ap, axis, n):
    u = ap.unsqueeze(axis)
    shape = list(u.shape)
    shape[axis] = n
    return u.broadcast_to(shape)


def cleared_after(nc, ctx):
    signals = []

    def clear():
        nc.clear_and_free_semaphores(signals)
        nc.all_engine_barrier()

    ctx.callback(clear)
    return signals


def new_signal(nc, signals, name):
    signals.append(nc.alloc_semaphore(name=name))
    return signals[-1]


def prepare(nc, io, keep, scr):
    xT, shared, ident, vecT, mod = keep["xT"], keep["shared_base"], keep["ident"], keep["vecT"], keep["mod"]
    with ExitStack() as ctx:
        signals = cleared_after(nc, ctx)

        def sb(name, shape, dt=F32):
            return ctx.enter_context(nc.sbuf_tensor(name, shape, dt))

        def sem(name):
            return new_signal(nc, signals, name)

        wada = [sb(f"wada{i}", [P, KB, P]) for i in range(4)]
        xs = [sb(f"xs{i}", [P, D_MODEL]) for i in range(2)]
        offset = [shared]

        def at(name, shape, dt=F32):
            size = 4
            for s in shape[1:]:
                size *= s
            if dt == BF16:
                size //= 2
            t = nc.alloc_sbuf_tensor_at(name, shape, dt, offset=offset[0])
            offset[0] += (size + 31) // 32 * 32
            assert offset[0] <= shared + KB * TOK * 4
            return t

        crows = at("crows", [COND, D_MODEL])
        square = at("square", [P, D_MODEL], BF16)
        vrows = at("vrows", [72, P])
        lam_rows = at("lam_rows", [PAIRS, 3, P])
        dt_rows = at("dt_rows", [PAIRS, 2])
        bmat = at("bmat", [P, 2, PAIRS, CH])
        bbar = at("bbar", [P, 2, PAIRS, CH])
        crow = at("crow", [P, 2, 4, P])
        cmat = at("cmat", [P, 2, PAIRS, CH])
        skip = at("skip", [CH, GROUPS, CH])
        lam = at("lam", [P, 3, PAIRS])
        tiny = at("tiny", [P, 24, PAIRS])
        ang = at("ang", [P, 8, 2, PAIRS])
        powr = at("powr", [P, 2, STEP + 1, PAIRS])
        prev = at("prev", [P, 2, STEP, PAIRS])
        wmat = at("wmat", [P, PAIR_BATCH, 2, STEP + 1, CH])
        wtmp = at("wtmp", [P, PAIR_BATCH, STEP + 1, CH])
        pmat = at("pmat", [P, PAIR_BATCH, 2, STEP, CH])
        ptmp = at("ptmp", [P, PAIR_BATCH, STEP, CH])
        bslot = at("bslot", [P, 2, PAIR_BATCH, CH])
        pout = at("pout", [P, PAIR_BATCH, 2, P])
        taps = at("taps", [CH, 2 * PAIR_BATCH, TAPS, CH])
        cT = sb("cT", [P, KB, COND])
        stat = sb("stat", [P, 6, 2])

        ps_x = [ctx.enter_context(nc.psum_tensor(f"ps_x{i}", [P, 512], F32)) for i in range(2)]
        ps_ada = [ctx.enter_context(nc.psum_tensor(f"ps_ada{i}", [P, 512], F32)) for i in range(2)]
        ps_v = ctx.enter_context(nc.psum_tensor("ps_v", [P, 512], F32))
        ps_p = ctx.enter_context(nc.psum_tensor("ps_p", [P, 512], F32))
        ps_k = ctx.enter_context(nc.psum_tensor("ps_k", [P, 2, 512], F32))

        rows_in, s5_in = sem("rows_in"), sem("s5_in")
        ada_in = [sem(f"ada_in{i}") for i in range(4)]
        x_in = [sem(f"x_in{i}") for i in range(2)]
        ident_ok, c_copied = sem("ident_ok"), sem("c_copied")
        vec_T, vec_copied = sem("vec_T"), sem("vec_copied")
        squared, var_ok, root_ok, x_scaled = sem("squared"), sem("var_ok"), sem("root_ok"), sem("x_scaled")
        x_T, x_copied = sem("x_T"), [sem("x_copied0"), sem("x_copied1")]
        ada_ok, ada_read = [sem(f"ada_ok{i}") for i in range(4)], [sem("ada_read0"), sem("ada_read1")]
        norm_step, s5_step, pool_step = sem("norm_step"), sem("s5_step"), sem("pool_step")
        lam_T, lam_copied, c_mat_T, c_mat_copied = sem("lam_T"), sem("lam_copied"), sem("c_mat_T"), sem("c_mat_copied")
        dt_ok, consts_ok = sem("dt_ok"), sem("consts_ok")
        w_ok, p_ok, p_T, p_copied, k_mm, k_copied = (sem(n) for n in ("w_ok", "p_ok", "p_T", "p_copied", "k_mm", "k_copied"))
        taps_ok, taps_out, p_out, q_out, tabs_out = sem("taps_ok"), sem("taps_out"), sem("p_out"), sem("q_out"), sem("tabs_out")
        skip_ok, bbar_ok, pow_ok = sem("skip_ok"), sem("bbar_ok"), sem("pow_ok")
        taps_zero, bslot_ok, w_step, passed = sem("taps_zero"), sem("bslot_ok"), sem("w_step"), sem("passed")

        block = ctx.enter_context(nc.Block())
        xp = io["x_prompt"].rearrange("b s d -> (b s) d")
        xd = io["x_sample"].rearrange("b s d -> (b s) d")
        w_ada = io["w_ada"][0].rearrange("(k p) n -> p k n", p=P)

        @block.sync
        def _(sp):
            sp.dma_start(crows[0:1, :], io["c_prompt"]).then_inc(rows_in, 16)
            sp.dma_start(crows[1:COND, :], io["c_sample"]).then_inc(rows_in, 16)
            sp.dma_start(vrows[0:48, :], io["b_ada"].rearrange("a (r c) -> (a r) c", c=P)).then_inc(rows_in, 16)
            sp.dma_start(vrows[48:64, :], io["g_pre"].rearrange("a (r c) -> (a r) c", c=P)).then_inc(rows_in, 16)
            sp.dma_start(vrows[64:72, :], io["b_glu"].rearrange("a (r c) -> (a r) c", c=P)).then_inc(rows_in, 16)
            sp.dma_start(xs[0][:], xd).then_inc(x_in[0], 16)
            for i, name in enumerate(("lambda_re", "lambda_im")):
                sp.dma_start(lam_rows[:, i, :], io[name][0].rearrange("(j g) p -> j (g p)", g=2)).then_inc(s5_in, 16)
            sp.dma_start(dt_rows[:], io["log_dt"][0].rearrange("(j g) -> j g", g=2)).then_inc(s5_in, 16)
            for i, name in enumerate(("b_re", "b_im")):
                sp.dma_start(bmat[:, i], io[name][0].rearrange("(j g) p c -> (g p) j c", g=2)).then_inc(s5_in, 16)
            for i, name in enumerate(("c_re", "c_im")):
                for r in range(4):
                    src = io[name][0, 16 * r:16 * r + 16].rearrange("(j g) c p -> j c g p", g=2)
                    for j in range(8):
                        sp.dma_start(crow[16 * j:16 * j + 16, i, r, :].rearrange("c (g p) -> c g p", g=2),
                                     src[j]).then_inc(s5_in, 16)
            sp.dma_start(skip[:].rearrange("a g c -> a (g c)"), io["d_skip"].broadcast_to([CH, GROUPS * CH])).then_inc(s5_in, 16)

            with sp.Fori(0, 4) as i:
                for u in range(2):
                    s = (u + 1) % 2
                    sp.wait_ge(x_T, i * 8 + 4 * u)
                    sp.dma_start(xs[s][:], xp[bass.ds(i * 256 + u * P, P), :]).then_inc(x_in[s], 16)
                    for v in range(4):
                        sp.wait_ge(ada_ok[v], i * 2 + u)
                        sp.dma_start(wada[v][:], w_ada[:, :, bass.ds(i * 1024 + (4 * u + v) * P, P)]).then_inc(ada_in[v], 16)

        @block.gpsimd
        def _(pool):
            nc.gpsimd.memset(ident[:], 0.0).then_inc(pool_step, 1)
            pool.wait_ge(pool_step, 1)
            nc.gpsimd.affine_select(out=ident[:], in_=ident[:], compare_op=ALU.not_equal, fill=1.0, base=0,
                                    pattern=[[-1, P]], channel_multiplier=1).then_inc(ident_ok, 1)
            nc.gpsimd.memset(taps[:], 0.0).then_inc(taps_zero, 1)
            pool.wait_ge(bbar_ok, 2)
            pool.wait_ge(pow_ok, 1)
            with pool.Fori(0, BATCHES) as b:
                js = bass.ds(b * PAIR_BATCH, PAIR_BATCH)
                pr = bc(prev[:, 0, :, js].rearrange("p s j -> p j s"), 3, CH)
                pi = bc(prev[:, 1, :, js].rearrange("p s j -> p j s"), 3, CH)
                pool.wait_ge(p_T, b * (2 * PAIR_BATCH))
                pool.sem_inc(passed, 1)
                for ri in range(2):
                    first, second = bc(bbar[:, ri, js, :], 2, STEP), bc(bbar[:, 1 - ri, js, :], 2, STEP)
                    nc.gpsimd.tensor_tensor(pmat[:, :, ri], pr, first, ALU.mult).then_inc(pool_step, 1)
                    nc.gpsimd.tensor_tensor(ptmp[:], pi, second, ALU.mult).then_inc(pool_step, 1)
                    pool.wait_ge(pool_step, b * 4 + 2 * ri + 3)
                    nc.gpsimd.tensor_tensor(pmat[:, :, ri], pmat[:, :, ri], ptmp[:],
                                            ALU.add if ri else ALU.subtract).then_inc(p_ok, 1)
                    pool.wait_ge(p_ok, b * 2 + ri + 1)
                    pool.sem_inc(passed, 1)

        @block.scalar
        def _(act):
            def root_of_mean(slot, landed, n):
                act.wait_ge(x_in[slot], landed)
                nc.scalar.activation(square[:], xs[slot][:], ACT.Square, accum_out=stat[:, 0, slot:slot + 1]).then_inc(squared, 1)
                act.wait_ge(var_ok, n)
                nc.scalar.activation(stat[:, 2, slot:slot + 1], stat[:, 1, slot:slot + 1], ACT.Sqrt).then_inc(root_ok, 1)

            root_of_mean(0, 16, 1)
            act.wait_ge(taps_zero, 1)
            with act.Fori(0, 4) as i:
                for u in range(2):
                    b = i * 2 + u
                    root_of_mean((u + 1) % 2, i * 16 + (32 if u else 16), b + 2)
                    js = bass.ds(b * PAIR_BATCH, PAIR_BATCH)
                    for h in range(2):
                        if h == 0:
                            act.wait_ge(p_out, b * 16)
                        act.wait_ge(p_T, b * 8 + 4 * h + 4)
                        nc.scalar.activation(pout[:, 2 * h:2 * h + 2].rearrange("p j r q -> p (j r q)"), ps_p[:],
                                             ACT.Copy).then_inc(p_copied, 1)
                    act.wait_ge(p_copied, b * 2 + 2)
                    act.dma_start(scr["s5_in"][:, js], pout[:]).then_inc(p_out, 16)
                    act.wait_ge(w_ok, b + 1)
                    act.dma_start(scr["s5_out"][:, js],
                                  wmat[:, :, :, 1:].rearrange("p j r t c -> p j r (t c)")).then_inc(q_out, 16)
                    act.wait_ge(taps_out, b * 16)
                    act.sem_inc(passed, 1)
                    act.wait_ge(k_mm, b + 1)
                    nc.scalar.activation(taps[:, :, STEP - 1:, :].rearrange("c (j a) t o -> c a j (t o)", a=2),
                                         ps_k[0:CH].rearrange("p a (j n) -> p a j n", j=4), ACT.Copy).then_inc(k_copied, 1)
                    act.wait_ge(taps_ok, b + 1)
                    act.dma_start(scr["taps"][bass.ds(b * (2 * PAIR_BATCH), 2 * PAIR_BATCH)].rearrange("g c t -> c g t"),
                                  taps[:].rearrange("c g t o -> c g (t o)")).then_inc(taps_out, 16)
            act.wait_ge(taps_out, 16 * BATCHES)
            act.wait_ge(p_out, 16 * BATCHES)
            act.wait_ge(q_out, 16 * BATCHES)

        @block.vector
        def _(dve):
            count = [0]

            def step(ins):
                count[0] += 1
                ins.then_inc(s5_step, 1)
                dve.wait_ge(s5_step, count[0])

            V = nc.vector
            dve.wait_ge(vec_T, 1)
            V.tensor_copy(cT[:].rearrange("p k c -> p (k c)"), ps_v[:, 0:KB * COND]).then_inc(c_copied, 1)
            V.tensor_copy(vecT[:], ps_v[:, 256:256 + 72]).then_inc(vec_copied, 1)

            def normalise(slot, n):
                s = lambda r: stat[:, r, slot:slot + 1]
                dve.wait_ge(squared, n + 1)
                V.tensor_scalar(s(1), s(0), 1.0 / D_MODEL, EPS, ALU.mult, ALU.add).then_inc(var_ok, 1)
                dve.wait_ge(root_ok, n + 1)
                V.reciprocal(s(3), s(2)).then_inc(norm_step, 1)
                dve.wait_ge(norm_step, n * 5 + 1)
                V.tensor_tensor(s(4), s(3), s(3), ALU.mult).then_inc(norm_step, 1)
                dve.wait_ge(norm_step, n * 5 + 2)
                V.tensor_tensor(s(4), s(4), s(1), ALU.mult).then_inc(norm_step, 1)
                dve.wait_ge(norm_step, n * 5 + 3)
                V.tensor_scalar(s(4), s(4), -0.5, 1.5, ALU.mult, ALU.add).then_inc(norm_step, 1)
                dve.wait_ge(norm_step, n * 5 + 4)
                V.tensor_tensor(s(5), s(3), s(4), ALU.mult).then_inc(norm_step, 1)
                dve.wait_ge(norm_step, n * 5 + 5)
                V.tensor_scalar(xs[slot][:], xs[slot][:], s(5), None, ALU.mult).then_inc(x_scaled, 1)

            def copy_x(column, n):
                for g in range(4):
                    dve.wait_ge(x_T, n * 4 + g + 1)
                    dve.sem_inc(passed, 1)
                    V.tensor_copy(xT[:, 4 * g:4 * g + 4, bass.ds(column, P)],
                                  ps_x[g % 2][:].rearrange("p (k t) -> p k t", k=4)).then_inc(x_copied[g % 2], 1)

            def keep_modulation(i, c):
                dve.wait_ge(ada_ok[c % 4], i * 2 + c // 4 + 1)
                V.tensor_tensor(mod[:, bass.ds(i * 8 + c, 1), :], ps_ada[c % 2][:, 0:COND].unsqueeze(1),
                                vecT[:, bass.ds(i * 8 + c, 1)].unsqueeze(2).broadcast_to([P, 1, COND]),
                                ALU.add).then_inc(ada_read[c % 2], 1)

            normalise(0, 0)
            copy_x(SEQ, 0)

            def exp_of(out, x, k, r, acc):
                step(V.tensor_scalar(k, x, 1.0 / LN2, -126.0, ALU.mult, ALU.max))
                step(V.tensor_scalar(k, k, 127.0, ROUND, ALU.min, ALU.add))
                step(V.tensor_scalar(k, k, -ROUND, None, ALU.add))
                step(V.scalar_tensor_tensor(r, k, -LN2_PARTS[0], x, ALU.mult, ALU.add))
                step(V.scalar_tensor_tensor(r, k, -LN2_PARTS[1], r, ALU.mult, ALU.add))
                step(V.tensor_scalar(r, r, -1.0, 1.0, ALU.max, ALU.min))
                step(V.tensor_scalar(acc, r, 1.0 / 5040, 1.0 / 720, ALU.mult, ALU.add))
                for c in (1.0 / 120, 1.0 / 24, 1.0 / 6, 0.5, 1.0, 1.0):
                    step(V.tensor_tensor(acc, acc, r, ALU.mult))
                    step(V.tensor_scalar(acc, acc, c, None, ALU.add))
                step(V.tensor_scalar(k, k, 127.0, 8388608.0, ALU.add, ALU.mult))
                step(V.tensor_copy(r.bitcast(I32), k))
                step(V.tensor_tensor(out, acc, r, ALU.mult))

            def sincos(cos, sin, y, k, z, zz):
                step(V.tensor_scalar(k, y, 0.5 / PI, ROUND, ALU.mult, ALU.add))
                step(V.tensor_scalar(k, k, -ROUND, None, ALU.add))
                step(V.scalar_tensor_tensor(z, k, -TWO_PI_PARTS[0], y, ALU.mult, ALU.add))
                step(V.scalar_tensor_tensor(z, k, -TWO_PI_PARTS[1], z, ALU.mult, ALU.add))
                step(V.scalar_tensor_tensor(z, k, -TWO_PI_PARTS[2], z, ALU.mult, ALU.add))
                step(V.tensor_scalar(z, z, 0.25, None, ALU.mult))
                step(V.tensor_tensor(zz, z, z, ALU.mult))
                step(V.tensor_scalar(sin, zz, 1.0 / 362880, -1.0 / 5040, ALU.mult, ALU.add))
                for c in (1.0 / 120, -1.0 / 6, 1.0):
                    step(V.tensor_tensor(sin, sin, zz, ALU.mult))
                    step(V.tensor_scalar(sin, sin, c, None, ALU.add))
                step(V.tensor_tensor(sin, sin, z, ALU.mult))
                step(V.tensor_scalar(cos, zz, -1.0 / 3628800, 1.0 / 40320, ALU.mult, ALU.add))
                for c in (-1.0 / 720, 1.0 / 24, -0.5, 1.0):
                    step(V.tensor_tensor(cos, cos, zz, ALU.mult))
                    step(V.tensor_scalar(cos, cos, c, None, ALU.add))
                for _ in range(2):
                    step(V.tensor_tensor(k, sin, sin, ALU.mult))
                    step(V.tensor_tensor(z, sin, cos, ALU.mult))
                    step(V.tensor_scalar(cos, k, -2.0, 1.0, ALU.mult, ALU.add))
                    step(V.tensor_scalar(sin, z, 2.0, None, ALU.mult))

            dve.wait_ge(s5_in, 16 * (3 + 2 + 64 + 1))
            V.tensor_copy(lam_rows[:, 2, :].rearrange("j (g p) -> j g p", g=2), bc(dt_rows[:], 2, STATE)).then_inc(dt_ok, 1)
            dve.wait_ge(lam_T, 3)
            step(V.tensor_copy(lam[:], ps_v[:, 384:384 + 96].rearrange("p (a j) -> p a j", a=3)))
            for ri in range(2):
                dve.wait_ge(c_mat_T, ri + 1)
                step(V.tensor_copy(cmat[:, ri].rearrange("p j c -> p (j c)"), ps_k[:, ri]))
            T = lambda i: tiny[:, i]
            A = lambda i: ang[:, i]
            exp_of(T(0), lam[:, 2], T(1), T(2), T(3))
            step(V.tensor_tensor(A(0)[:, 0], lam[:, 0], T(0), ALU.mult))
            step(V.tensor_tensor(A(1)[:, 0], lam[:, 1], T(0), ALU.mult))
            step(V.tensor_scalar(A(0)[:, 1], A(0)[:, 0], float(STEP), None, ALU.mult))
            step(V.tensor_scalar(A(1)[:, 1], A(1)[:, 0], float(STEP), None, ALU.mult))
            exp_of(A(2), A(0), A(3), A(4), A(5))
            sincos(A(3), A(4), A(1), A(5), A(6), A(7))
            step(V.memset(powr[:, 0, 0], 1.0))
            step(V.memset(powr[:, 1, 0], 0.0))
            step(V.tensor_tensor(powr[:, 0, 1], A(2)[:, 0], A(3)[:, 0], ALU.mult))
            step(V.tensor_tensor(powr[:, 1, 1], A(2)[:, 0], A(4)[:, 0], ALU.mult))
            for a, b in ((1, 1), (2, 1), (2, 2), (3, 2), (3, 3), (4, 3), (4, 4)):
                n = a + b
                step(V.tensor_tensor(T(4), powr[:, 0, a], powr[:, 0, b], ALU.mult))
                step(V.tensor_tensor(T(5), powr[:, 1, a], powr[:, 1, b], ALU.mult))
                step(V.tensor_tensor(powr[:, 0, n], T(4), T(5), ALU.subtract))
                step(V.tensor_tensor(T(4), powr[:, 0, a], powr[:, 1, b], ALU.mult))
                step(V.tensor_tensor(T(5), powr[:, 1, a], powr[:, 0, b], ALU.mult))
                step(V.tensor_tensor(powr[:, 1, n], T(4), T(5), ALU.add))
            for s in range(STEP):
                ins = V.tensor_copy(prev[:, :, s], powr[:, :, STEP - 1 - s])
            ins.then_inc(pow_ok, 1)
            step(V.tensor_tensor(T(6), lam[:, 0], lam[:, 0], ALU.mult))
            step(V.tensor_tensor(T(7), lam[:, 1], lam[:, 1], ALU.mult))
            step(V.tensor_tensor(T(6), T(6), T(7), ALU.add))
            step(V.reciprocal(T(6), T(6)))
            step(V.tensor_scalar(T(7), powr[:, 0, 1], -1.0, None, ALU.add))
            step(V.tensor_tensor(T(8), T(7), lam[:, 0], ALU.mult))
            step(V.tensor_tensor(T(9), powr[:, 1, 1], lam[:, 1], ALU.mult))
            step(V.tensor_tensor(T(8), T(8), T(9), ALU.add))
            step(V.tensor_tensor(T(8), T(8), T(6), ALU.mult))
            step(V.tensor_tensor(T(9), powr[:, 1, 1], lam[:, 0], ALU.mult))
            step(V.tensor_tensor(T(10), T(7), lam[:, 1], ALU.mult))
            step(V.tensor_tensor(T(9), T(9), T(10), ALU.subtract))
            step(V.tensor_tensor(T(9), T(9), T(6), ALU.mult))
            fr, fi = bc(T(8), 2, CH), bc(T(9), 2, CH)
            w0 = wmat[:].rearrange("p a b c d -> p (a b c d)")[:, 0:512].rearrange("p (j c) -> p j c", j=PAIRS)
            step(V.tensor_tensor(bbar[:, 0], fr, bmat[:, 0], ALU.mult))
            step(V.tensor_tensor(w0, fi, bmat[:, 1], ALU.mult))
            V.tensor_tensor(bbar[:, 0], bbar[:, 0], w0, ALU.subtract).then_inc(bbar_ok, 1)
            dve.wait_ge(bbar_ok, 1)
            step(V.tensor_tensor(bbar[:, 1], fr, bmat[:, 1], ALU.mult))
            step(V.tensor_tensor(w0, fi, bmat[:, 0], ALU.mult))
            V.tensor_tensor(bbar[:, 1], bbar[:, 1], w0, ALU.add).then_inc(bbar_ok, 1)
            dve.wait_ge(ident_ok, 1)
            V.tensor_tensor(skip[:], skip[:], bc(ident[0:CH, 0:CH], 1, GROUPS), ALU.mult).then_inc(skip_ok, 1)
            tabs = keep["s5_tabs"]
            step(V.tensor_copy(tabs[:, 0], A(2)[:, 1]))
            step(V.tensor_copy(tabs[:, 1], A(3)[:, 1]))
            step(V.tensor_copy(tabs[:, 2], A(4)[:, 1]))
            step(V.tensor_copy(tabs[:, 3], powr[:, 0, STEP]))
            step(V.tensor_copy(tabs[:, 4], powr[:, 1, STEP]))

            def s5_build(b):
                js = bass.ds(b * PAIR_BATCH, PAIR_BATCH)
                pr = bc(powr[:, 0, :, js].rearrange("p s j -> p j s"), 3, CH)
                pi = bc(powr[:, 1, :, js].rearrange("p s j -> p j s"), 3, CH)
                cr, ci = bc(cmat[:, 0, js], 2, STEP + 1), bc(cmat[:, 1, js], 2, STEP + 1)
                flat = lambda t: t.rearrange("p j t c -> p j (t c)")
                dve.wait_ge(k_mm, b)
                dve.sem_inc(passed, 1)
                V.tensor_copy(bslot[:], bbar[:, :, js, :]).then_inc(bslot_ok, 1)
                dve.wait_ge(q_out, b * 16)
                V.tensor_tensor(wmat[:, :, 0], pr, cr, ALU.mult).then_inc(w_step, 1)
                V.tensor_tensor(wtmp[:], pi, ci, ALU.mult).then_inc(w_step, 1)
                V.tensor_tensor(wmat[:, :, 1], pi, cr, ALU.mult).then_inc(w_step, 1)
                dve.wait_ge(w_step, b * 5 + 3)
                V.tensor_tensor(wmat[:, :, 0], wmat[:, :, 0], wtmp[:], ALU.subtract).then_inc(w_step, 1)
                dve.wait_ge(w_step, b * 5 + 4)
                V.tensor_tensor(wtmp[:], pr, ci, ALU.mult).then_inc(w_step, 1)
                dve.wait_ge(w_step, b * 5 + 5)
                V.scalar_tensor_tensor(flat(wmat[:, :, 1]), flat(wmat[:, :, 1]), -1.0, flat(wtmp[:]),
                                       ALU.mult, ALU.subtract).then_inc(w_ok, 1)

            def s5_skip(b):
                dve.wait_ge(k_copied, b + 1)
                V.tensor_tensor(taps[:, :, STEP - 1], taps[:, :, STEP - 1],
                                skip[:, bass.ds(b * (2 * PAIR_BATCH), 2 * PAIR_BATCH)], ALU.add).then_inc(taps_ok, 1)

            with dve.Fori(0, 4) as i:
                for u in range(2):
                    t = i * 2 + u
                    normalise((u + 1) % 2, t + 1)
                    s5_build(t)
                    copy_x(t * P, t + 1)
                    for v in range(4):
                        keep_modulation(i, 4 * u + v)
                    s5_skip(t)
            sc = mod[:, KB:2 * KB]
            dve.wait_ge(ada_read[0], KB)
            dve.wait_ge(ada_read[1], KB)
            step(V.tensor_scalar(sc, sc, 1.0, None, ALU.add))
            step(V.tensor_tensor(sc, sc, bc(vecT[:, 48:64], 2, COND), ALU.mult))

        @block.tensor
        def _(pe):
            M, TR = nc.tensor.matmul, nc.tensor.transpose
            pe.wait_ge(ident_ok, 1)
            pe.wait_ge(rows_in, 80)
            for k in range(KB):
                ins = TR(ps_v[:, COND * k:COND * k + COND], crows[:, k * P:k * P + P], ident[0:COND, 0:COND])
            TR(ps_v[:, 256:256 + 72], vrows[:], ident[0:72, 0:72]).then_inc(vec_T, 1)

            def turn_x(slot, n):
                pe.wait_ge(x_scaled, n + 1)
                for g in range(4):
                    if g >= 2:
                        pe.wait_ge(x_copied[g % 2], n * 2 + 1)
                    else:
                        pe.wait_ge(x_copied[g % 2], n * 2)
                    for k in range(4 * g, 4 * g + 4):
                        ins = TR(ps_x[g % 2][:, (k % 4) * P:(k % 4) * P + P], xs[slot][:, k * P:k * P + P], ident[:])
                    ins.then_inc(x_T, 1)

            def turn_s5_rows():
                pe.wait_ge(dt_ok, 1)
                pe.wait_ge(vec_copied, 1)
                pe.wait_ge(c_copied, 1)
                for a in range(3):
                    TR(ps_v[:, 384 + 32 * a:416 + 32 * a], lam_rows[:, a, :], ident[0:PAIRS, 0:PAIRS]).then_inc(lam_T, 1)
                for ri in range(2):
                    for r in range(4):
                        ins = TR(ps_k[:, ri, r * P:r * P + P], crow[:, ri, r, :], ident[:])
                    ins.then_inc(c_mat_T, 1)

            def s5_batch(b):
                pe.wait_ge(p_ok, b * 2 + 2)
                for h in range(2):
                    pe.wait_ge(p_copied, b * 2 + h)
                    for q in range(4):
                        j, ri = 2 * h + q // 2, q % 2
                        TR(ps_p[:, q * P:q * P + P], pmat[:, j, ri].rearrange("p s c -> p (s c)"), ident[:]).then_inc(p_T, 1)
                pe.wait_ge(w_ok, b + 1)
                pe.sem_inc(passed, 1)
                pe.wait_ge(bslot_ok, b + 1)
                pe.sem_inc(passed, 1)
                pe.wait_ge(k_copied, b)
                pe.sem_inc(passed, 1)
                for g in range(2 * PAIR_BATCH):
                    j, half = g // 2, slice(64 * (g % 2), 64 * (g % 2) + 64)
                    for ri in range(2):
                        ins = M(ps_k[0:CH, g % 2, j * P:j * P + P], bslot[half, ri, j, :],
                                wmat[half, j, ri, 0:STEP].rearrange("p t c -> p (t c)"), start=ri == 0, stop=ri == 1)
                ins.then_inc(k_mm, 1)

            def modulate(i, c):
                pe.wait_ge(ada_in[c % 4], i * 32 + 16 * (c // 4) + 16)
                pe.wait_ge(ada_read[c % 2], i * 4 + c // 2)
                for k in range(KB):
                    ins = M(ps_ada[c % 2][:, 0:COND], wada[c % 4][:, k, :], cT[:, k, :], start=k == 0, stop=k == KB - 1)
                ins.then_inc(ada_ok[c % 4], 1)

            turn_x(0, 0)
            turn_s5_rows()
            pe.wait_ge(c_copied, 1)
            with pe.Fori(0, 4) as i:
                for u in range(2):
                    turn_x((u + 1) % 2, i * 2 + u + 1)
                    for v in range(4):
                        modulate(i, 4 * u + v)
                    s5_batch(i * 2 + u)
CHOSEN, UNSEEN, MASKED = -3.4e38, -3.0e38, -1.0e30
SLICES = [(c, TC) for c in range(0, TOK, TC)]

SEGMENTS = [
    (Q0, 4, False, None), (Q0 + 512, 8, False, 7), (U0, 5, True, 6), (U0 + 640, 5, True, 5),
    (U0 + 1280, 6, True, 4), (ZA0, 4, False, 3), (ZA0 + 512, 4, False, 2),
]


def project_in(nc, io, keep, scr):
    ident, mod, xT, maskb = keep["ident"], keep["mod"], keep["xT"], keep["maskb"]
    with ExitStack() as ctx:
        signals = cleared_after(nc, ctx)

        def sb(name, shape, dt=F32):
            return ctx.enter_context(nc.sbuf_tensor(name, shape, dt))

        def sem(name):
            return new_signal(nc, signals, name)

        h_hi = nc.alloc_sbuf_tensor_at("h_hi", [P, KB, TOK], F32R, offset=keep["shared_base"])
        h_lo = nc.alloc_sbuf_tensor_at("h_lo", [P, KB, TOK], F32R, offset=keep["xT_base"])
        w_raw = sb("w_raw", [P, 2, HALF, P])
        w_hi = sb("w_hi", [P, 2, HALF, P], F32R)
        w_lo = sb("w_lo", [P, 2, HALF, P], F32R)
        z_sb = sb("z_sb", [P, TOK])
        iqT = sb("iqT", [P, IDX_HEADS // 2, P])
        ikT = sb("ikT", [P, SEQ])
        rel = sb("rel", [P, 2, 512])
        score = sb("score", [P, SEQ])
        iw = sb("iw", [P, SEQ // P, IDX_HEADS])
        top8 = sb("top8", [P, 8])
        ps_z = [ctx.enter_context(nc.psum_tensor(f"ps_z{i}", [P, 512], F32)) for i in range(NTC)]
        ps_s = [ctx.enter_context(nc.psum_tensor(f"ps_s{i}", [P, 512], F32)) for i in range(4)]
        ps_w = ctx.enter_context(nc.psum_tensor("ps_w", [P, 512], F32))

        affine_ok, hi_ok, lo_ok = sem("affine_ok"), sem("hi_ok"), sem("lo_ok")
        w_in = [sem("w_in0"), sem("w_in1")]
        w_hi_ok, w_lo_ok, w_used = [sem("w_hi0"), sem("w_hi1")], [sem("w_lo0"), sem("w_lo1")], sem("w_used")
        z_done, z_out = sem("z_done"), sem("z_out")
        z_read = [sem(f"z_read{i}") for i in range(NTC)]
        idx_in, iq_in, iw_T, iw_ok = sem("idx_in"), sem("iq_in"), sem("iw_T"), sem("iw_ok")
        s_mm, s_relu, s_acc, unseen_ok = sem("s_mm"), sem("s_relu"), sem("s_acc"), sem("unseen_ok")
        top, mask_ok, passed = sem("top"), sem("mask_ok"), sem("passed_b")

        wv = io["w_in"][0].rearrange("(k p) n -> p k n", p=P)
        zt = scr["zt"]
        IDX_TILES = [s[3] for s in SEGMENTS if s[3] is not None]

        def width(tile):
            keys = (tile + 1) * P
            return keys, keys if keys <= 512 else keys // 2

        def units(tile):
            keys, w = width(tile)
            return [(hp, h2, c, w) for hp in range(IDX_HEADS // 2) for c in range(0, keys, w) for h2 in range(2)]

        first_unit = {}
        total = 0
        for t in IDX_TILES:
            first_unit[t] = total
            total += len(units(t))
        base_of = []
        g = 9
        for c0, n, perm, tile in SEGMENTS:
            base_of.append(g)
            g += n
        LAST = g - 1

        block = ctx.enter_context(nc.Block())

        @block.sync
        def _(sp):
            def load(G, col, m=P):
                for h in range(2):
                    sp.wait_ge(w_lo_ok[h], G)
                    sp.dma_start(w_raw[:, h, :, 0:m], wv[:, HALF * h:HALF * h + HALF, bass.ds(col, m)]).then_inc(w_in[h], 16)

            def load_queries(tile):
                sp.dma_start(iqT[:], zt[IQ0:IQ0 + 1024, tile * P:tile * P + P].rearrange("(a q) t -> q a t", q=P)).then_inc(iq_in, 16)

            load(0, IQ0)
            with sp.Fori(1, 8) as i:
                load(i, i * P + IQ0)
            load(8, IK0, 80)
            for (c0, n, perm, tile), g0 in zip(SEGMENTS, base_of):
                if tile is not None:
                    if tile == IDX_TILES[0]:
                        sp.wait_ge(z_out, 16 * 9)
                        for half in range(2):
                            sp.dma_start(ikT[64 * half:64 * half + 64, :], zt[IK0:IK0 + IDX_DIM, 0:SEQ]).then_inc(idx_in, 16)
                        sp.dma_start(score[0:IDX_HEADS, :], zt[IW0:IW0 + IDX_HEADS, 0:SEQ]).then_inc(idx_in, 16)
                    else:
                        sp.wait_ge(s_mm, first_unit[tile])
                    load_queries(tile)
                with sp.Fori(0, n) as i:
                    load(i + g0, i * P + c0)

        @block.scalar
        def _(act):
            def high(h, G, m=P):
                act.wait_ge(w_in[h], (G + 1) * 16)
                if h == 0:
                    act.wait_ge(w_used, G)
                else:
                    act.wait_ge(z_done, G * NTC)
                nc.scalar.activation(w_hi[:, h, :, 0:m], w_raw[:, h, :, 0:m], ACT.Copy).then_inc(w_hi_ok[h], 1)

            def store(G, col, m, perm):
                for i, (c, n) in enumerate(SLICES):
                    if i == 0:
                        act.wait_ge(z_out, G * 16)
                    act.wait_ge(z_done, G * NTC + i + 1)
                    if perm:
                        out = z_sb[0:m, :].rearrange("p (s n) -> p n s", s=STEP)[:, c // STEP:(c + n) // STEP, :]
                        src = ps_z[i][0:m, 0:n].rearrange("p (n s) -> p n s", s=STEP)
                    else:
                        out, src = z_sb[0:m, c:c + n], ps_z[i][0:m, 0:n]
                    nc.scalar.activation(out, src, ACT.Copy).then_inc(z_read[i], 1)
                act.wait_ge(z_read[NTC - 1], G + 1)
                act.dma_start(zt[bass.ds(col, m), :], z_sb[0:m, :]).then_inc(z_out, 16)

            def block_(G, col, perm, m=P, next_m=P):
                high(1, G, m)
                if next_m:
                    high(0, G + 1, next_m)
                store(G, col, m, perm)

            def relus(tile):
                for u, (hp, h2, c, w) in enumerate(units(tile), first_unit[tile]):
                    act.wait_ge(s_mm, u + 1)
                    if u >= 2:
                        act.wait_ge(s_acc, u - 1)
                    nc.scalar.activation(rel[:, u % 2, 0:w], ps_s[u % 4][:, 0:w], ACT.Relu).then_inc(s_relu, 1)

            high(0, 0)
            high(1, 0)
            for k in range(KB):
                act.wait_ge(affine_ok, 2 * k + 2)
                nc.scalar.activation(h_hi[:, k], xT[:, k], ACT.Copy).then_inc(hi_ok, 1)
            high(0, 1)
            store(0, IQ0, P, False)
            with act.Fori(1, 7) as i:
                block_(i, i * P + IQ0, False)
            block_(7, IQ0 + 7 * P, False, P, 80)
            block_(8, IK0, False, 80, P)
            for (c0, n, perm, tile), g0 in zip(SEGMENTS, base_of):
                if tile is not None:
                    relus(tile)
                last = g0 + n - 1 == LAST
                with act.Fori(0, n - 1 if last else n) as i:
                    block_(i + g0, i * P + c0, perm)
                if last:
                    block_(LAST, c0 + P * (n - 1), perm, P, 0)
            act.wait_ge(z_out, 16 * (LAST + 1))

        @block.vector
        def _(dve):
            V = nc.vector

            def low(h, G, m=P):
                dve.wait_ge(w_hi_ok[h], G + 1)
                V.tensor_tensor(w_lo[:, h, :, 0:m], w_raw[:, h, :, 0:m], w_hi[:, h, :, 0:m].bitcast(F32),
                                ALU.subtract).then_inc(w_lo_ok[h], 1)

            def affine(k):
                V.tensor_scalar(xT[:, k, 0:SEQ], xT[:, k, 0:SEQ], mod[:, KB + k, 0:1], mod[:, k, 0:1],
                                ALU.mult, ALU.add).then_inc(affine_ok, 1)
                s = xT[:, k, SEQ:TOK].rearrange("p (b t) -> p b t", b=DEC_B)
                V.tensor_tensor(s, s, bc(mod[:, KB + k, 1:COND], 2, DEC_S), ALU.mult).then_inc(passed, 1)
                dve.wait_ge(passed, k + 1)
                V.tensor_tensor(s, s, bc(mod[:, k, 1:COND], 2, DEC_S), ALU.add).then_inc(affine_ok, 1)

            def h_low(k):
                dve.wait_ge(hi_ok, k + 1)
                V.tensor_tensor(h_lo[:, k], xT[:, k], h_hi[:, k].bitcast(F32), ALU.subtract).then_inc(lo_ok, 1)

            def add_scores(tile):
                keys, w_ = width(tile)
                pieces = keys // w_
                if tile != IDX_TILES[0]:
                    dve.wait_ge(mask_ok, 2 + IDX_TILES.index(tile))
                for u, (hp, h2, c, w) in enumerate(units(tile), first_unit[tile]):
                    dve.wait_ge(s_relu, u + 1)
                    wgt = iw[:, tile, 2 * hp + h2:2 * hp + h2 + 1]
                    if hp == 0 and h2 == 0:
                        V.tensor_scalar(score[:, c:c + w], rel[:, u % 2, 0:w], wgt, None, ALU.mult).then_inc(s_acc, 1)
                    else:
                        dve.wait_ge(s_acc, u if h2 else u + 1 - (2 * pieces - 1))
                        V.scalar_tensor_tensor(score[:, c:c + w], rel[:, u % 2, 0:w], wgt, score[:, c:c + w],
                                               ALU.mult, ALU.add).then_inc(s_acc, 1)
                dve.wait_ge(s_acc, first_unit[tile] + len(units(tile)))
                V.memset(score[0:64, keys - CHUNK:keys], UNSEEN).then_inc(unseen_ok, 1)
                dve.wait_ge(unseen_ok, IDX_TILES.index(tile) + 1)

            def rounds(tile, at, n):
                keys = width(tile)[0]
                for r in range(n):
                    dve.wait_ge(top, at + 2 * r)
                    dve.sem_inc(passed, 1)
                    V.max(top8[:], score[:, 0:keys]).then_inc(top, 1)
                    dve.wait_ge(top, at + 2 * r + 1)
                    dve.sem_inc(passed, 1)
                    V.match_replace(score[:, 0:keys], top8[:], score[:, 0:keys], CHOSEN).then_inc(top, 1)

            def block_(G, tile, at, m=P, next_m=P):
                low(1, G, m)
                if tile is not None:
                    rounds(tile, at, 4)
                if next_m:
                    low(0, G + 1, next_m)
                if tile is not None:
                    rounds(tile, at + 8, 4)

            affine(0)
            affine(1)
            low(0, 0)
            for k in range(KB):
                h_low(k)
                if k + 2 < KB:
                    affine(k + 2)
                if k == 4:
                    low(1, 0)
            low(0, 1)
            with dve.Fori(1, 7) as i:
                block_(i, None, 0)
            block_(7, None, 0, P, 80)
            block_(8, None, 0, 80, P)
            V.memset(maskb[:, 0:3 * P], 0.0).then_inc(mask_ok, 1)
            dve.wait_ge(mask_ok, 1)
            V.memset(maskb[0:64, CHUNK:P], MASKED).then_inc(passed, 1)
            V.memset(maskb[0:64, P + 3 * CHUNK:3 * P], MASKED).then_inc(mask_ok, 1)
            for (c0, n, perm, tile), g0 in zip(SEGMENTS, base_of):
                if tile is None:
                    with dve.Fori(0, n) as i:
                        block_(i + g0, None, 0)
                    dve.wait_ge(iw_T, 1)
                    V.tensor_scalar(iw[:].rearrange("p t h -> p (t h)"), ps_w[:, 0:P], IDX_DIM ** -0.5 * IDX_HEADS ** -0.5, None,
                                    ALU.mult).then_inc(iw_ok, 1)
                    dve.wait_ge(iw_ok, 1)
                    continue
                add_scores(tile)
                k = IDX_TILES.index(tile)
                last = g0 + n - 1 == LAST
                with dve.Fori(0, 3 if last else 4) as i:
                    block_(i + g0, tile, i * 16 + 64 * k)
                if last:
                    block_(LAST, tile, 48 + 64 * k, P, 0)
                elif n > 4:
                    with dve.Fori(4, n) as i:
                        block_(i + g0, None, 0)
                keys = width(tile)[0]
                at = P * (tile * (tile + 1) // 2)
                dve.wait_ge(top, 64 * k + 64)
                V.tensor_scalar(maskb[:, at:at + keys], score[:, 0:keys], (CHOSEN + UNSEEN) / 2, MASKED,
                                ALU.is_gt, ALU.mult).then_inc(mask_ok, 1)

        @block.tensor
        def _(pe):
            M, TR = nc.tensor.matmul, nc.tensor.transpose

            def products(i, c, n, k, h, m):
                kk, cols, out = HALF * h + k, slice(c, c + n), ps_z[i][0:m, 0:n]
                M(out, w_hi[:, h, k, 0:m], h_hi[:, kk, cols], start=kk == 0, stop=False)
                M(out, w_hi[:, h, k, 0:m], h_lo[:, kk, cols], start=False, stop=False)
                return M(out, w_lo[:, h, k, 0:m], h_hi[:, kk, cols], start=False, stop=kk == KB - 1)

            def block_(G, m=P):
                for h in range(2):
                    pe.wait_ge(w_lo_ok[h], G + 1)
                    for i, (c, n) in enumerate(SLICES):
                        if h == 0:
                            pe.wait_ge(z_read[i], G)
                        for k in range(HALF):
                            ins = products(i, c, n, k, h, m)
                        if h == 1:
                            ins.then_inc(z_done, 1)
                    if h == 0:
                        ins.then_inc(w_used, 1)

            def first_block():
                for h in range(2):
                    pe.wait_ge(w_lo_ok[h], 1)
                    for k in range(HALF):
                        pe.wait_ge(lo_ok, HALF * h + k + 1)
                        for i, (c, n) in enumerate(SLICES):
                            ins = products(i, c, n, k, h, P)
                            if h == 1 and k == HALF - 1:
                                ins.then_inc(z_done, 1)
                    if h == 0:
                        ins.then_inc(w_used, 1)

            def scores(tile):
                if tile == IDX_TILES[0]:
                    pe.wait_ge(idx_in, 48)
                    for t in range(SEQ // P):
                        ins = TR(ps_w[:, IDX_HEADS * t:IDX_HEADS * t + IDX_HEADS], score[0:IDX_HEADS, t * P:t * P + P],
                                 ident[0:IDX_HEADS, 0:IDX_HEADS])
                    ins.then_inc(iw_T, 1)
                pe.wait_ge(iq_in, 16 * (IDX_TILES.index(tile) + 1))
                for u, (hp, h2, c, w) in enumerate(units(tile), first_unit[tile]):
                    if u >= 4:
                        pe.wait_ge(s_relu, u - 3)
                    half = slice(64 * h2, 64 * h2 + 64)
                    ins = M(ps_s[u % 4][:, 0:w], iqT[half, hp, :], ikT[half, c:c + w], start=True, stop=True)
                    ins.then_inc(s_mm, 1)

            first_block()
            with pe.Fori(1, 8) as i:
                block_(i)
            block_(8, 80)
            for (c0, n, perm, tile), g0 in zip(SEGMENTS, base_of):
                if tile is not None:
                    scores(tile)
                with pe.Fori(0, n) as i:
                    block_(i + g0)


def scan_states(nc, io, out, keep, scr):
    tabs, ident = keep["s5_tabs"], keep["ident"]
    with ExitStack() as ctx:
        signals = cleared_after(nc, ctx)

        def sb(name, shape, dt=F32):
            return ctx.enter_context(nc.sbuf_tensor(name, shape, dt))

        def sem(name):
            return new_signal(nc, signals, name)

        uy = sb("uy", [P, GROUPS, NSTEP])
        p_in = sb("p_in", [P, PAIRS, 2, P])
        q_out = sb("q_out", [P, PAIRS, 2, P])
        toep = sb("toep", [P, GROUPS, P])
        rot = sb("rot", [P, 2, PAIRS, PSTEP])
        wide = sb("wide", [P, 2, PAIR_BATCH, PSTEP])
        part = sb("part", [P, 4, PAIR_BATCH, PSTEP])
        hist = sb("hist", [P, 2, 2, PAIR_BATCH, NSTEP])
        dec_b = sb("dec_b", [P, 2, 2, PAIR_BATCH, 2 * DEC_B])
        dec_t = sb("dec_t", [P, 4, PAIR_BATCH, DEC_B])
        state_rows = sb("state_rows", [P, 2, 2, P])
        h0 = sb("h0", [P, 2, DEC_B, PAIRS])
        last = sb("last", [P, 2, DEC_B + 1, PAIRS])
        ps_b = ctx.enter_context(nc.psum_tensor("ps_b", [P, 2, 2, 512], F32))
        ps_y = ctx.enter_context(nc.psum_tensor("ps_y", [P, 4, 512], F32))

        u_in, p_land, q_land, t_land, h0_in = (sem(n) for n in ("u_in", "p_land", "q_land", "t_land", "h0_in"))
        rot_dve, rot_pool, rot_ok = sem("rot_dve"), sem("rot_pool"), sem("rot_ok")
        b_mm, b_read, products, turned, scanned = (sem(n) for n in ("b_mm", "b_read", "products", "turned", "scanned"))
        backs, hist_ok, dec_copied, dec_ok, dec_step = (sem(n) for n in ("backs", "hist_ok", "dec_copied", "dec_ok", "dec_step"))
        y_mm, y_copied, y_out, zeroed, h0_T, h0_ok, stepped = (sem(n) for n in ("y_mm", "y_copied", "y_out", "zeroed", "h0_T", "h0_ok", "stepped"))
        last_T, last_copied, state_out = sem("last_T"), sem("last_copied"), sem("state_out")
        zt = scr["zt"]
        block = ctx.enter_context(nc.Block())
        DVE_PAIRS = 22

        def last_rows(ri):
            return part[0:PAIRS, ri, 0, :]

        @block.sync
        def _(sp):
            sp.dma_start(p_in[:], scr["s5_in"]).then_inc(p_land, 16)
            for s in range(STEP):
                sp.dma_start(uy[CH * s:CH * s + CH],
                             zt[U0:U0 + 1024, s * NSTEP:s * NSTEP + NSTEP].rearrange("(g c) n -> c g n", c=CH)).then_inc(u_in, 16)
            for ri, name in enumerate(("state_ssm_re", "state_ssm_im")):
                sp.dma_start(state_rows[:, ri], io[name][0].rearrange("(h b) (j g) p -> (b j) h (g p)", h=2, g=2)).then_inc(h0_in, 16)
            sp.dma_start(q_out[:], scr["s5_out"]).then_inc(q_land, 16)
            sp.wait_ge(rot_ok, 2)
            for s in range(STEP):
                at = CH * (STEP - 1 - s)
                sp.dma_start(toep[CH * s:CH * s + CH], scr["taps"][:, :, at:at + P].rearrange("g c t -> c g t")).then_inc(t_land, 16)
            for half in range(2):
                sp.wait_ge(y_copied, 2 * (BATCHES // 2) * (half + 1))
                g = slice(32 * half, 32 * half + 32)
                for s in range(STEP):
                    sp.dma_start(scr["y"].rearrange("(g c) t -> c g t", c=CH)[:, g, s * NSTEP:s * NSTEP + NSTEP],
                                 uy[CH * s:CH * s + CH, g]).then_inc(y_out, 16)
            for ri, (name_d, name_p) in enumerate((("ssm_re_sample", "ssm_re_prompt"), ("ssm_im_sample", "ssm_im_prompt"))):
                sp.wait_ge(last_copied, 2)
                sp.dma_start(out[name_d][0].rearrange("(h b) (j g) p -> (b j) h (g p)", h=2, g=2), state_rows[:, ri]).then_inc(state_out, 16)
                sp.dma_start(out[name_p][0, 0].rearrange("(j g) p -> j (g p)", g=2), last_rows(ri)).then_inc(state_out, 16)
            sp.wait_ge(y_out, 16 * 2 * STEP)
            sp.wait_ge(state_out, 64)

        def rotations(E, eng, done, pairs, work):
            count = [0]

            def step(ins):
                count[0] += 1
                ins.then_inc(done, 1)

            def settle():
                eng.wait_ge(done, count[0])

            r, i = rot[:, 0, pairs], rot[:, 1, pairs]
            n = pairs.stop - pairs.start
            step(E.memset(r[:, :, 0:1], 1.0))
            step(E.memset(i[:, :, 0:1], 0.0))
            step(E.tensor_copy(r[:, :, 1:2], tabs[:, 1, pairs].unsqueeze(2)))
            step(E.tensor_copy(i[:, :, 1:2], tabs[:, 2, pairs].unsqueeze(2)))
            m = 1
            while m < PSTEP:
                settle()
                if m > 1:
                    a, b = r[:, :, m // 2], i[:, :, m // 2]
                    t = [work[:, k, pairs, 0] for k in range(3)]
                    step(E.tensor_tensor(t[0], a, a, ALU.mult))
                    step(E.tensor_tensor(t[1], b, b, ALU.mult))
                    step(E.tensor_tensor(t[2], a, b, ALU.mult))
                    settle()
                    step(E.tensor_tensor(r[:, :, m], t[0], t[1], ALU.subtract))
                    step(E.tensor_tensor(i[:, :, m], t[2], t[2], ALU.add))
                    settle()
                    lo, hi = slice(1, m), slice(m + 1, 2 * m)
                    er, ei = (x[:, :, m:m + 1].broadcast_to([P, n, m - 1]) for x in (r, i))
                    w0, w1 = work[:, 0, pairs, 0:m - 1], work[:, 1, pairs, 0:m - 1]
                    step(E.tensor_tensor(r[:, :, hi], r[:, :, lo], er, ALU.mult))
                    step(E.tensor_tensor(w0, i[:, :, lo], ei, ALU.mult))
                    step(E.tensor_tensor(i[:, :, hi], i[:, :, lo], er, ALU.mult))
                    step(E.tensor_tensor(w1, r[:, :, lo], ei, ALU.mult))
                    settle()
                    step(E.tensor_tensor(r[:, :, hi], r[:, :, hi], w0, ALU.subtract))
                    step(E.tensor_tensor(i[:, :, hi], i[:, :, hi], w1, ALU.add))
                m *= 2
            settle()

        work = toep[:].rearrange("p g n -> p (g n)")[:, 0:3 * PAIRS * 64].rearrange("p (a j n) -> p a j n", a=3, j=PAIRS)

        @block.gpsimd
        def _(pool):
            G = nc.gpsimd
            rotations(G, pool, rot_pool, slice(DVE_PAIRS, PAIRS), work)
            G.memset(hist[:, :, :, :, 0:1], 0.0).then_inc(zeroed, 1)
            pool.wait_ge(zeroed, 1)
            pool.sem_inc(rot_ok, 1)
            pool.wait_ge(h0_ok, 4)
            n = 0
            for b in range(BATCHES):
                js, s = slice(PAIR_BATCH * b, PAIR_BATCH * b + PAIR_BATCH), b % 2
                ar, ai = (bc(tabs[:, k, js], 2, DEC_B) for k in (3, 4))
                steps = lambda ri, c: hist[:, s, ri, :, PSTEP + c::2]
                xr, xi = (h0[:, ri, :, js].rearrange("p b j -> p j b") for ri in range(2))
                pool.wait_ge(dec_copied, 2 * b + 2)
                if b >= 2:
                    pool.wait_ge(y_mm, b - 1)
                G.tensor_copy(steps(0, 0), xr).then_inc(dec_step, 1)
                G.tensor_copy(steps(1, 0), xi).then_inc(dec_step, 1)
                n += 2
                for c in range(2):
                    t = [dec_t[:, k] for k in range(4)]
                    bu = [dec_b[:, s, ri, :, c::2] for ri in range(2)]
                    if c == 0:
                        to = [steps(0, 1), steps(1, 1)]
                    else:
                        xr, xi = to
                        to = [last[:, ri, 0:DEC_B, js].rearrange("p b j -> p j b") for ri in range(2)]
                    for k, (a, x) in enumerate(((ar, xr), (ai, xi), (ar, xi), (ai, xr))):
                        G.tensor_tensor(t[k], a, x, ALU.mult).then_inc(dec_step, 1)
                    n += 4
                    pool.wait_ge(dec_step, n)
                    G.tensor_tensor(t[0], t[0], t[1], ALU.subtract).then_inc(dec_step, 1)
                    G.tensor_tensor(t[2], t[2], t[3], ALU.add).then_inc(dec_step, 1)
                    n += 2
                    pool.wait_ge(dec_step, n)
                    G.tensor_tensor(to[0], t[0], bu[0], ALU.add).then_inc(dec_step, 1)
                    ins = G.tensor_tensor(to[1], t[2], bu[1], ALU.add)
                    ins.then_inc(dec_step, 1)
                    n += 2
                    pool.wait_ge(dec_step, n)
                pool.sem_inc(dec_ok, 1)

        @block.scalar
        def _(act):
            for b in range(BATCHES):
                act.wait_ge(y_mm, b + 1)
                for e in range(2):
                    dst = uy[:, 8 * b + e:8 * b + 8:2].rearrange("p (a c) n -> p a c n", a=2)
                    src = ps_y[:, 2 * e:2 * e + 2, 0:2 * NSTEP].rearrange("p a (c n) -> p a c n", c=2)
                    nc.scalar.activation(dst, src, ACT.Copy).then_inc(y_copied, 1)
            act.wait_ge(last_T, 2)
            nc.scalar.activation(state_rows[:].rearrange("p r h q -> p (r h q)"), ps_y[:, 0], ACT.Copy).then_inc(last_copied, 1)
            nc.scalar.activation(part[0:PAIRS, 0:2, 0, :], ps_y[0:PAIRS, 1, 0:2 * P].rearrange("p (r q) -> p r q", r=2),
                                 ACT.Copy).then_inc(last_copied, 1)

        @block.vector
        def _(dve):
            V = nc.vector
            rotations(V, dve, rot_dve, slice(0, DVE_PAIRS), work)
            dve.sem_inc(rot_ok, 1)
            dve.wait_ge(h0_T, 1)
            for ri in range(2):
                for h in range(2):
                    V.tensor_copy(h0[:, ri, 4 * h:4 * h + 4].rearrange("p b j -> p (b j)"),
                                  ps_y[:, 0, (2 * ri + h) * P:(2 * ri + h + 1) * P]).then_inc(h0_ok, 1)
            dve.wait_ge(rot_ok, 2)
            for b in range(BATCHES):
                js, s = slice(PAIR_BATCH * b, PAIR_BATCH * b + PAIR_BATCH), b % 2
                er, ei = (rot[:, ri, js].rearrange("p (a c) n -> p a c n", a=2) for ri in range(2))
                br, bi = (ps_b[:, ri, :, 0:2 * NSTEP].rearrange("p a (c n) -> p a c n", c=2) for ri in range(2))
                split = lambda t: t.rearrange("p (a c) n -> p a c n", a=2)
                dve.wait_ge(b_mm, b + 1)
                if b >= 2:
                    dve.wait_ge(dec_ok, b - 1)
                for ri, x in enumerate((br, bi)):
                    V.tensor_copy(split(dec_b[:, s, ri]), x[:, :, :, PSTEP:]).then_inc(dec_copied, 1)
                if b:
                    dve.wait_ge(hist_ok, b)
                V.tensor_tensor(split(wide[:, 0]), er, br[:, :, :, 0:PSTEP], ALU.mult).then_inc(products, 1)
                V.tensor_tensor(split(part[:, 0]), ei, bi[:, :, :, 0:PSTEP], ALU.mult).then_inc(products, 1)
                V.tensor_tensor(split(wide[:, 1]), er, bi[:, :, :, 0:PSTEP], ALU.mult).then_inc(products, 1)
                V.tensor_tensor(split(part[:, 1]), ei, br[:, :, :, 0:PSTEP], ALU.mult).then_inc(b_read, 1)
                dve.wait_ge(products, 3 * b + 3)
                V.tensor_tensor(wide[:, 0], wide[:, 0], part[:, 0], ALU.add).then_inc(turned, 1)
                dve.wait_ge(b_read, b + 1)
                V.tensor_tensor(wide[:, 1], wide[:, 1], part[:, 1], ALU.subtract).then_inc(turned, 1)
                dve.wait_ge(turned, 2 * b + 2)
                for ri in range(2):
                    for j in range(PAIR_BATCH):
                        r = tabs[:, 0, PAIR_BATCH * b + j:PAIR_BATCH * b + j + 1].broadcast_to([P, PSTEP])
                        V.tensor_tensor_scan(wide[:, ri, j], r, wide[:, ri, j], 0.0, ALU.mult, ALU.add).then_inc(scanned, 1)
                dve.wait_ge(scanned, 8 * b + 8)
                E = [rot[:, ri, js] for ri in range(2)]
                for k, (e, x) in enumerate(((0, 0), (1, 1), (0, 1), (1, 0))):
                    V.tensor_tensor(part[:, k], E[e], wide[:, x], ALU.mult).then_inc(backs, 1)
                if b >= 2:
                    dve.wait_ge(y_mm, b - 1)
                dve.wait_ge(backs, 4 * b + 4)
                V.tensor_tensor(last[:, 0, DEC_B, js], part[:, 0, :, PSTEP - 1], part[:, 1, :, PSTEP - 1], ALU.subtract).then_inc(stepped, 1)
                V.tensor_tensor(last[:, 1, DEC_B, js], part[:, 2, :, PSTEP - 1], part[:, 3, :, PSTEP - 1], ALU.add).then_inc(stepped, 1)
                V.tensor_tensor(hist[:, s, 0, :, 1:PSTEP], part[:, 0, :, 0:PSTEP - 1], part[:, 1, :, 0:PSTEP - 1], ALU.subtract).then_inc(stepped, 1)
                V.tensor_tensor(hist[:, s, 1, :, 1:PSTEP], part[:, 2, :, 0:PSTEP - 1], part[:, 3, :, 0:PSTEP - 1], ALU.add).then_inc(hist_ok, 1)

        @block.tensor
        def _(pe):
            M, TR = nc.tensor.matmul, nc.tensor.transpose
            pe.wait_ge(h0_in, 32)
            for ri in range(2):
                for h in range(2):
                    ins = TR(ps_y[:, 0, (2 * ri + h) * P:(2 * ri + h + 1) * P], state_rows[:, ri, h], ident[:])
            ins.then_inc(h0_T, 1)

            def inputs(b):
                if b:
                    pe.wait_ge(b_read, b)
                for j in range(PAIR_BATCH):
                    pair = PAIR_BATCH * b + j
                    for ri in range(2):
                        for g in range(2):
                            ins = M(ps_b[64 * g:64 * g + 64, ri, j // 2, (j % 2) * NSTEP:(j % 2 + 1) * NSTEP],
                                    p_in[:, pair, ri, 64 * g:64 * g + 64], uy[:, 2 * pair + g, :], start=True, stop=True)
                ins.then_inc(b_mm, 1)

            def outputs(b):
                if b:
                    pe.wait_ge(y_copied, 2 * b)
                bank = lambda j, g: ps_y[:, 2 * g + j // 2, (j % 2) * NSTEP:(j % 2 + 1) * NSTEP]
                for g in range(2):
                    for j in range(PAIR_BATCH):
                        group = 2 * (PAIR_BATCH * b + j) + g
                        M(bank(j, g), toep[:, group, :], uy[:, group, :], start=j % 2 == 0, stop=False)
                pe.wait_ge(hist_ok, b + 1)
                pe.wait_ge(dec_ok, b + 1)
                for j in range(PAIR_BATCH):
                    for ri in range(2):
                        for g in range(2):
                            half = slice(64 * g, 64 * g + 64)
                            ins = M(bank(j, g), q_out[half, PAIR_BATCH * b + j, ri, :], hist[half, b % 2, ri, j, :],
                                    start=False, stop=ri == 1 and j % 2 == 1)
                ins.then_inc(y_mm, 1)

            pe.wait_ge(p_land, 16)
            pe.wait_ge(u_in, 16 * STEP)
            pe.wait_ge(h0_ok, 4)
            inputs(0)
            pe.wait_ge(t_land, 16 * STEP)
            pe.wait_ge(q_land, 16)
            for b in range(BATCHES):
                if b + 1 < BATCHES:
                    inputs(b + 1)
                outputs(b)
            pe.wait_ge(y_copied, 2 * BATCHES)
            for ri in range(2):
                for h in range(2):
                    ins = TR(ps_y[:, 0, (2 * ri + h) * P:(2 * ri + h + 1) * P],
                             last[:, ri, 4 * h:4 * h + 4].rearrange("p b j -> p (b j)"), ident[:])
            ins.then_inc(last_T, 1)
            for ri in range(2):
                ins = TR(ps_y[0:PAIRS, 1, ri * P:ri * P + P], last[:, ri, DEC_B, :], ident[:])
            ins.then_inc(last_T, 1)


def gate_states(nc, io, keep, scr):
    vecT, mix_hi, mix_lo = keep["vecT"], keep["ssm_hi"], keep["ssm_lo"]
    NB = 1024 // P
    QUART = NB // 2
    with ExitStack() as ctx:
        signals = cleared_after(nc, ctx)

        def sb(name, shape, dt=F32):
            return ctx.enter_context(nc.sbuf_tensor(name, shape, dt))

        def sem(name):
            return new_signal(nc, signals, name)

        v_hi, v_lo = sb("v_hi", [P, NB, TOK], F32R), sb("v_lo", [P, NB, TOK], F32R)
        y_in = sb("y_in", [P, 2, TOK])
        w_raw = sb("g_raw", [P, 2, QUART, P])
        w_hi, w_lo = sb("g_hi", [P, 2, QUART, P], F32R), sb("g_lo", [P, 2, QUART, P], F32R)
        zs = sb("zs", [P, TOK])
        s1, s2 = sb("s1", [P, TOK]), sb("s2", [P, TOK])
        ps_z = [ctx.enter_context(nc.psum_tensor(f"ps_g{i}", [P, 512], F32)) for i in range(NTC)]

        yl = [sem("yl0"), sem("yl1")]
        gelu_ok, v_hi_ok, v_lo_ok = sem("gelu_ok"), sem("v_hi_ok"), sem("v_lo_ok")
        w_in = [sem("gw_in0"), sem("gw_in1")]
        w_hi_ok, w_lo_ok = [sem("gw_hi0"), sem("gw_hi1")], [sem("gw_lo0"), sem("gw_lo1")]
        w_used, z_done, sig_ok, zs_in, zsig_ok = sem("gw_used"), sem("gz_done"), sem("sig_ok"), sem("zs_in"), sem("zsig_ok")
        v_sum, gated, gated_z, zgated, mixed, m_hi, passed = (sem(n) for n in ("v_sum", "gated", "gated_z", "zgated", "mixed", "m_hi", "passed_g"))
        wv = io["w_glu"][0].rearrange("(k p) n -> p k n", p=P)
        zt = scr["zt"]
        block = ctx.enter_context(nc.Block())

        @block.sync
        def _(sp):
            def load_w(i):
                for h in range(2):
                    sp.wait_ge(w_lo_ok[h], i)
                    sp.dma_start(w_raw[:, h], wv[:, QUART * h:QUART * h + QUART, bass.ds(i * P, P)]).then_inc(w_in[h], 16)

            for k in range(NB):
                if k >= 2:
                    sp.wait_ge(gelu_ok, k - 1)
                sp.dma_start(y_in[:, k % 2], scr["y"][k * P:k * P + P, :]).then_inc(yl[k % 2], 16)
                if k == 1:
                    load_w(0)
            with sp.Fori(0, NB) as i:
                sp.wait_ge(zgated, i)
                sp.dma_start(zs[:], zt[bass.ds(i * P + ZS0, P), :]).then_inc(zs_in, 16)

        @block.scalar
        def _(act):
            A = nc.scalar.activation

            def load_w(i):
                for h in range(2):
                    act.wait_ge(w_lo_ok[h], i)
                    act.dma_start(w_raw[:, h], wv[:, QUART * h:QUART * h + QUART, bass.ds(i * P, P)]).then_inc(w_in[h], 16)

            def high(h, i):
                act.wait_ge(w_in[h], (i + 1) * 16)
                if h == 0:
                    act.wait_ge(w_used, i)
                else:
                    act.wait_ge(z_done, i * NTC)
                A(w_hi[:, h], w_raw[:, h], ACT.Copy).then_inc(w_hi_ok[h], 1)

            high(0, 0)
            high(1, 0)
            for k in range(NB):
                act.wait_ge(yl[k % 2], 16 * (k // 2 + 1))
                if k >= 2:
                    act.wait_ge(v_lo_ok, k - 1)
                g = (s1, s2)[k % 2]
                A(g[:], y_in[:, k % 2], ACT.Gelu_apprx_tanh).then_inc(gelu_ok, 1)
                act.wait_ge(gelu_ok, k + 1)
                A(v_hi[:, k], g[:], ACT.Copy).then_inc(v_hi_ok, 1)

            def block_(i, last):
                act.wait_ge(zs_in, i * 16 + 16)
                act.wait_ge(zgated, i)
                A(s2[:], zs[:], ACT.Sigmoid).then_inc(zsig_ok, 1)
                if not last:
                    load_w(i + 1)
                    high(0, i + 1)
                for t, (c, n) in enumerate(SLICES):
                    act.wait_ge(z_done, i * NTC + t + 1)
                    if t == 0:
                        act.wait_ge(gated, i)
                    act.sem_inc(passed, 1)
                    A(s1[:, c:c + n], ps_z[t][:, 0:n], ACT.Sigmoid, bias=bias(i)).then_inc(sig_ok, 1)
                if not last:
                    high(1, i + 1)
                act.wait_ge(mixed, i + 1)
                act.sem_inc(passed, 1)
                A(mix_hi[:, bass.ds(i, 1)].rearrange("p a t -> p (a t)"), s1[:], ACT.Copy).then_inc(m_hi, 1)

            def bias(i):
                return vecT[:, bass.ds(i + 64, 1)]

            act.wait_ge(v_lo_ok, NB)
            with act.Fori(0, NB - 1) as i:
                block_(i, False)
            block_(NB - 1, True)

        @block.vector
        def _(dve):
            V = nc.vector

            def low(h, i):
                dve.wait_ge(w_hi_ok[h], i + 1)
                V.tensor_tensor(w_lo[:, h], w_raw[:, h], w_hi[:, h].bitcast(F32), ALU.subtract).then_inc(w_lo_ok[h], 1)

            low(0, 0)
            low(1, 0)
            for k in range(NB):
                dve.wait_ge(v_hi_ok, k + 1)
                V.tensor_tensor(v_lo[:, k], (s1, s2)[k % 2][:], v_hi[:, k].bitcast(F32), ALU.subtract).then_inc(v_lo_ok, 1)

            def block_(i, last):
                row = lambda t: t[:, bass.ds(i, 1)].rearrange("p a t -> p (a t)")
                dve.wait_ge(zsig_ok, i + 1)
                V.tensor_tensor(zs[:], zs[:], s2[:], ALU.mult).then_inc(v_sum, 1)
                if not last:
                    low(0, i + 1)
                dve.wait_ge(v_sum, i * 2 + 1)
                V.tensor_tensor(s2[:], row(v_hi).bitcast(F32), row(v_lo).bitcast(F32), ALU.add).then_inc(v_sum, 1)
                dve.wait_ge(v_sum, i * 2 + 2)
                V.tensor_tensor(zs[:], s2[:], zs[:], ALU.mult).then_inc(gated_z, 1)
                dve.wait_ge(sig_ok, i * NTC + NTC)
                dve.wait_ge(gated_z, i + 1)
                V.tensor_tensor(s1[:], s1[:], zs[:], ALU.mult).then_inc(mixed, 1)
                dve.wait_ge(mixed, i + 1)
                dve.sem_inc(zgated, 1)
                if not last:
                    low(1, i + 1)
                dve.wait_ge(m_hi, i + 1)
                V.tensor_tensor(row(mix_lo), s1[:], row(mix_hi).bitcast(F32), ALU.subtract).then_inc(gated, 1)

            with dve.Fori(0, NB - 1) as i:
                block_(i, False)
            block_(NB - 1, True)

        @block.tensor
        def _(pe):
            M = nc.tensor.matmul

            with pe.Fori(0, NB) as i:
                for h in range(2):
                    pe.wait_ge(w_lo_ok[h], i + 1)
                    for t, (c, n) in enumerate(SLICES):
                        if h == 0:
                            pe.wait_ge(v_lo_ok, NB)
                            pe.wait_ge(sig_ok, i * NTC)
                        for k in range(QUART):
                            kk, cols, o = QUART * h + k, slice(c, c + n), ps_z[t][:, 0:n]
                            M(o, w_hi[:, h, k], v_hi[:, kk, cols], start=kk == 0, stop=False)
                            M(o, w_hi[:, h, k], v_lo[:, kk, cols], start=False, stop=False)
                            ins = M(o, w_lo[:, h, k], v_hi[:, kk, cols], start=False, stop=kk == NB - 1)
                        if h == 1:
                            ins.then_inc(z_done, 1)
                    if h == 0:
                        ins.then_inc(w_used, 1)


def natural_keys(nc, io, out, keep, scr):
    ident, kT, v_nat = keep["ident"], keep["kT"], keep["v_nat"]
    with ExitStack() as ctx:
        signals = cleared_after(nc, ctx)

        def sb(name, shape, dt=F32):
            return ctx.enter_context(nc.sbuf_tensor(name, shape, dt))

        def sem(name):
            return new_signal(nc, signals, name)

        vT = sb("vT", [P, KV_HEADS, TOK])
        ikT = sb("ikT_n", [IDX_DIM, TOK])
        rows = sb("kv_rows", [P, 2, 2 * KV_HEADS * HD])
        ik_rows = sb("ik_rows", [P, 2, IDX_DIM])
        ps_kv = [ctx.enter_context(nc.psum_tensor(f"ps_kv{i}", [P, 512], F32)) for i in range(2)]
        ps_ik = [ctx.enter_context(nc.psum_tensor(f"ps_ik{i}", [P, 512], F32)) for i in range(2)]
        kv_in, kv_T, kv_ok, ik_ok, v_ok = (sem(n) for n in ("kv_in", "kv_T", "kv_ok", "ik_ok", "v_ok"))
        kv_out = [sem("kv_out0"), sem("kv_out1")]
        block = ctx.enter_context(nc.Block())
        W = KV_HEADS * HD

        def results(t):
            if t < NT - 1:
                rows_ = slice(t * P, t * P + P)
                return (out["k_prompt"][0, 0, rows_].rearrange("t h d -> t (h d)"),
                        out["v_prompt"][0, 0, rows_].rearrange("t h d -> t (h d)"), out["idx_k_prompt"][0, 0, rows_])
            return (out["k_sample"][0].rearrange("b t h d -> (b t) (h d)"),
                    out["v_sample"][0].rearrange("b t h d -> (b t) (h d)"),
                    out["idx_k_sample"][0].rearrange("b t d -> (b t) d"))

        @block.sync
        def _(sp):
            sp.dma_start(kT[:], scr["zt"][K0:V0].rearrange("(h d) t -> d h t", d=HD)).then_inc(kv_in, 16)
            sp.dma_start(vT[:], scr["zt"][V0:IQ0].rearrange("(h d) t -> d h t", d=HD)).then_inc(kv_in, 16)
            sp.dma_start(ikT[:], scr["zt"][IK0:IW0]).then_inc(kv_in, 16)
            for t in range(NT):
                k, v, ik = results(t)
                sp.wait_ge(kv_ok, t + 1)
                sp.wait_ge(ik_ok, t + 1)
                sp.dma_start(k, rows[:, t % 2, 0:W]).then_inc(kv_out[t % 2], 16)
                sp.dma_start(v, rows[:, t % 2, W:2 * W]).then_inc(kv_out[t % 2], 16)
                sp.dma_start(ik, ik_rows[:, t % 2]).then_inc(kv_out[t % 2], 16)
            sp.wait_ge(kv_out[0], 48 * ((NT + 1) // 2))
            sp.wait_ge(kv_out[1], 48 * (NT // 2))

        @block.scalar
        def _(act):
            for t in range(NT):
                act.wait_ge(kv_T, t + 1)
                if t >= 2:
                    act.wait_ge(kv_out[t % 2], 48 * (t // 2))
                    act.wait_ge(v_ok, t - 1)
                nc.scalar.activation(rows[:, t % 2], ps_kv[t % 2][:], ACT.Copy).then_inc(kv_ok, 1)

        @block.vector
        def _(dve):
            for t in range(NT):
                dve.wait_ge(kv_T, t + 1)
                if t >= 2:
                    dve.wait_ge(kv_out[t % 2], 48 * (t // 2))
                nc.vector.tensor_copy(ik_rows[:, t % 2], ps_ik[t % 2][:, 0:IDX_DIM]).then_inc(ik_ok, 1)
                if t < NT - 1:
                    dve.wait_ge(kv_ok, t + 1)
                    nc.vector.tensor_copy(v_nat[:, t], rows[:, t % 2, W:2 * W]).then_inc(v_ok, 1)

        @block.tensor
        def _(pe):
            pe.wait_ge(kv_in, 48)
            for t in range(NT):
                cols = slice(t * P, t * P + P)
                if t >= 2:
                    pe.wait_ge(kv_ok, t - 1)
                    pe.wait_ge(ik_ok, t - 1)
                nc.tensor.transpose(ps_ik[t % 2][:, 0:IDX_DIM], ikT[:, cols], ident[0:IDX_DIM, 0:IDX_DIM])
                for h in range(2 * KV_HEADS):
                    src = (kT if h < KV_HEADS else vT)[:, h % KV_HEADS, cols]
                    ins = nc.tensor.transpose(ps_kv[t % 2][:, h * HD:h * HD + HD], src, ident[:])
                ins.then_inc(kv_T, 1)


def attend_prompt(nc, io, keep, scr):
    ident, kT, v_nat, maskb = keep["ident"], keep["kT"], keep["v_nat"], keep["maskb"]
    mix_hi, mix_lo = keep["attn_hi"], keep["attn_lo"]
    SCALE = HD ** -0.5
    TILES = SEQ // P
    units = [(t, h) for t in range(TILES) for h in range(HEADS)]
    N = len(units)
    with ExitStack() as ctx:
        signals = cleared_after(nc, ctx)

        def sb(name, shape, dt=F32):
            return ctx.enter_context(nc.sbuf_tensor(name, shape, dt))

        def sem(name):
            return new_signal(nc, signals, name)

        q = sb("q", [P, 2, HEADS, P])
        za = sb("za", [P, HEADS, P])
        gate = sb("gate", [P, HEADS, P])
        probs = sb("probs", [P, 2, SEQ])
        pT = sb("pT", [P, 2, TILES, P])
        att = sb("att", [P, 2, P])
        stat = sb("row_stat", [P, 4, 2])
        ps_l = [ctx.enter_context(nc.psum_tensor(f"ps_l{i}", [P, 1024], F32)) for i in range(2)]
        ps_t = [ctx.enter_context(nc.psum_tensor(f"ps_t{i}", [P, 512], F32)) for i in range(2)]
        ps_o = [ctx.enter_context(nc.psum_tensor(f"ps_o{i}", [P, 512], F32)) for i in range(2)]

        q_in, za_in = [sem("q_in0"), sem("q_in1")], sem("za_in")
        sig_ok, gate_ok, gate_used = sem("asig_ok"), sem("gate_ok"), sem("gate_used")
        logits_mm, logits_ok, bias_ok, exp_ok, recip_ok, probs_ok = (
            sem(n) for n in ("logits_mm", "logits_ok", "bias_ok", "exp_ok", "recip_ok", "probs_ok"))
        turned, turned_read, av_mm, att_ok, hi_ok, lo_ok = (
            sem(n) for n in ("p_turned", "p_turned_read", "av_mm", "att_ok", "att_hi_ok", "att_lo_ok"))
        zt = scr["zt"]
        banks = lambda t: (t + 4) // 4
        before = [sum(banks(t) for t, _ in units[:n]) for n in range(N + 1)]
        fills = [[sum(banks(t) > g for t, _ in units[:n]) for n in range(N + 1)] for g in range(2)]
        block = ctx.enter_context(nc.Block())

        @block.sync
        def _(sp):
            for t in range(TILES):
                if t >= 2:
                    sp.wait_ge(logits_mm, HEADS * (t - 1))
                cols = slice(t * P, t * P + P)
                sp.dma_start(q[:, t % 2], zt[Q0:K0, cols].rearrange("(h d) t -> d h t", d=HD)).then_inc(q_in[t % 2], 16)
                if t:
                    sp.wait_ge(gate_ok, t)
                sp.dma_start(za[:], zt[ZA0:U0, cols].rearrange("(h d) t -> d h t", d=HD)).then_inc(za_in, 16)

        @block.gpsimd
        def _(pool):
            for t in range(TILES):
                pool.wait_ge(sig_ok, t + 1)
                nc.gpsimd.tensor_tensor(gate[:], gate[:], za[:], ALU.mult).then_inc(gate_ok, 1)

        @block.scalar
        def _(act):
            A = nc.scalar.activation

            def exponentials(n):
                t, h = units[n]
                keys = (t + 1) * P
                act.wait_ge(bias_ok, n + 1)
                A(probs[:, n % 2, 0:keys], probs[:, n % 2, 0:keys], ACT.Exp, bias=stat[:, 1, n % 2:n % 2 + 1],
                  scale=SCALE, accum_out=stat[:, 2, n % 2:n % 2 + 1]).then_inc(exp_ok, 1)

            def read_turned(n):
                t, h = units[n]
                if n >= 2:
                    act.wait_ge(av_mm, n - 1)
                for g in range(banks(t)):
                    act.wait_ge(turned, before[n] + g + 1)
                    k = min(4, t + 1 - 4 * g)
                    A(pT[:, n % 2, 4 * g:4 * g + k].rearrange("p b t -> p (b t)"), ps_t[g][:, 0:k * P],
                      ACT.Copy).then_inc(turned_read, 1)

            def high(n):
                t, h = units[n]
                act.wait_ge(att_ok, n + 1)
                out_ = mix_hi[:, h].rearrange("p (s n) -> p n s", s=STEP)[:, 16 * t:16 * t + 16, :]
                A(out_, att[:, n % 2].rearrange("p (n s) -> p n s", s=STEP), ACT.Copy).then_inc(hi_ok, 1)

            def sigmoid(t):
                act.wait_ge(za_in, 16 * (t + 1))
                if t:
                    act.wait_ge(att_ok, HEADS * t)
                A(gate[:], za[:], ACT.Sigmoid).then_inc(sig_ok, 1)

            for n in range(N + 3):
                if n < N:
                    exponentials(n)
                if 1 <= n <= N:
                    read_turned(n - 1)
                if n >= 3:
                    high(n - 3)
                if n == 0:
                    sigmoid(0)
                if n >= 3 and (n - 3) % HEADS == HEADS - 1 and (n - 3) // HEADS + 1 < TILES:
                    sigmoid((n - 3) // HEADS + 1)

        @block.vector
        def _(dve):
            V = nc.vector

            def logits(n):
                t, h = units[n]
                keys, at = (t + 1) * P, P * (t * (t + 1) // 2)
                dve.wait_ge(logits_mm, n + 1)
                if n >= 2:
                    dve.wait_ge(turned, before[n - 1])
                s = n % 2
                V.tensor_tensor_reduce(out=probs[:, s, 0:keys], in0=ps_l[s][:, 0:keys], in1=maskb[:, at:at + keys],
                                       scale=1.0, scalar=-3.0e38, op0=ALU.add, op1=ALU.max,
                                       accum_out=stat[:, 0, s:s + 1]).then_inc(logits_ok, 1)
                dve.wait_ge(logits_ok, n + 1)
                V.tensor_scalar(stat[:, 1, s:s + 1], stat[:, 0, s:s + 1], -SCALE, None, ALU.mult).then_inc(bias_ok, 1)

            def normalise(n):
                t, h = units[n]
                s, keys = n % 2, (t + 1) * P
                dve.wait_ge(exp_ok, n + 1)
                V.reciprocal(stat[:, 3, s:s + 1], stat[:, 2, s:s + 1]).then_inc(recip_ok, 1)
                dve.wait_ge(recip_ok, n + 1)
                V.tensor_scalar(probs[:, s, 0:keys], probs[:, s, 0:keys], stat[:, 3, s:s + 1], None, ALU.mult).then_inc(probs_ok, 1)

            def gate_it(n):
                t, h = units[n]
                dve.wait_ge(av_mm, n + 1)
                dve.wait_ge(gate_ok, t + 1)
                if n >= 2:
                    dve.wait_ge(lo_ok, n - 1)
                V.tensor_tensor(att[:, n % 2], ps_o[n % 2][:, 0:P], gate[:, h], ALU.mult).then_inc(att_ok, 1)

            def low(n):
                t, h = units[n]
                dve.wait_ge(hi_ok, n + 1)
                view = lambda m: m[:, h].rearrange("p (s n) -> p n s", s=STEP)[:, 16 * t:16 * t + 16, :]
                V.tensor_tensor(view(mix_lo), att[:, n % 2].rearrange("p (n s) -> p n s", s=STEP),
                                view(mix_hi).bitcast(F32), ALU.subtract).then_inc(lo_ok, 1)

            for n in range(N + 4):
                if n < N:
                    logits(n)
                if 1 <= n <= N:
                    normalise(n - 1)
                if n >= 4:
                    low(n - 4)
                if 3 <= n < N + 3:
                    gate_it(n - 3)

        @block.tensor
        def _(pe):
            M, TR = nc.tensor.matmul, nc.tensor.transpose

            def logits(n):
                t, h = units[n]
                s, keys = n % 2, (t + 1) * P
                pe.wait_ge(q_in[t % 2], 16 * (t // 2 + 1))
                if n >= 2:
                    pe.wait_ge(logits_ok, n - 1)
                for c in range(0, keys, 512):
                    w = min(512, keys - c)
                    ins = M(ps_l[s][:, c:c + w], q[:, t % 2, h], kT[:, h * KV_HEADS // HEADS, c:c + w], start=True, stop=True)
                ins.then_inc(logits_mm, 1)

            def turn(n):
                t, h = units[n]
                pe.wait_ge(probs_ok, n + 1)
                for g in range(banks(t)):
                    last = max((m for m in range(n) if banks(units[m][0]) > g), default=None)
                    if last is not None:
                        pe.wait_ge(turned_read, before[last] + g + 1)
                    for k in range(4 * g, min(4 * g + 4, t + 1)):
                        ins = TR(ps_t[g][:, (k % 4) * P:(k % 4) * P + P], probs[:, n % 2, k * P:k * P + P], ident[:])
                    ins.then_inc(turned, 1)

            def values(n):
                t, h = units[n]
                kv = h * KV_HEADS // HEADS
                pe.wait_ge(turned_read, before[n + 1])
                if n >= 2:
                    pe.wait_ge(att_ok, n - 1)
                for k in range(t + 1):
                    ins = M(ps_o[n % 2][:, 0:P], v_nat[:, k, kv * HD:kv * HD + HD], pT[:, n % 2, k], start=k == 0, stop=k == t)
                ins.then_inc(av_mm, 1)

            logits(0)
            for n in range(N + 1):
                if n + 1 < N:
                    logits(n + 1)
                if n < N:
                    turn(n)
                if n:
                    values(n - 1)


DUMMY = -3.2e38


def attend_samples(nc, io, out, keep, scr):
    ident, kT = keep["ident"], keep["kT"]
    mix_hi, mix_lo = keep["attn_hi"], keep["attn_lo"]
    SCALE = HD ** -0.5
    HP = IDX_HEADS // 2
    BLK = PAST // P
    W = KV_HEADS * HD
    with ExitStack() as ctx:
        signals = cleared_after(nc, ctx)

        def sb(name, shape, dt=F32):
            return ctx.enter_context(nc.sbuf_tensor(name, shape, dt))

        def sem(name):
            return new_signal(nc, signals, name)

        iq = sb("iq_s", [P, DEC_B, HP * DEC_S])
        q = sb("q_s", [P, DEC_B, HEADS * DEC_S])
        ik_new = sb("ik_new", [P, P])
        w_rows = sb("w_rows", [2 * DEC_B, HP, DEC_S])
        wcol = sb("wcol", [P, 2, DEC_B])
        pick = sb("pick", [P, 240])
        spread = sb("spread", [P, DEC_B, HEADS, DEC_S], BF16)
        ik_rows = sb("ik_cached", [P, 2, BLK, 2, IDX_DIM])
        ikT = sb("ikT_s", [P, 2, DEC_KEYS])
        rel = sb("rel_s", [P, 2, DEC_KEYS])
        score = sb("score_s", [P, DEC_KEYS + 8])
        top8 = sb("top8_s", [P, 8])
        mask = sb("mask_s", [P, DEC_KEYS], BF16)
        gate = sb("gate_s", [P, HEADS, P])
        stage = nc.alloc_sbuf_tensor_at("q_stage", [P, HEADS, P], F32, offset=keep["maskb_base"])
        za = nc.alloc_sbuf_tensor_at("za_s", [P, HEADS, P], F32, offset=keep["maskb_base"] + 4 * HEADS * P)
        k_rows, v_rows = sb("k_cached", [P, 2, BLK, W]), sb("v_cached", [P, 2, BLK, W])
        v_new = sb("v_new", [DEC_S, 2, W])
        kT_s = sb("kT_s", [P, 2, KV_HEADS, DEC_KEYS])
        probs = sb("probs_s", [P, 2, DEC_KEYS])
        pT = sb("pT_s", [P, 2, BLK + 1, P])
        att = ik_rows[:, 0].rearrange("p n a d -> p n (a d)")
        stat = sb("stat_s", [P, 4, 2])
        ps_a = [ctx.enter_context(nc.psum_tensor(f"ps_a{i}", [P, 512], F32)) for i in range(2)]
        ps_k = [ctx.enter_context(nc.psum_tensor(f"ps_ks{i}", [P, 512], F32)) for i in range(2)]
        ps_o = [ctx.enter_context(nc.psum_tensor(f"ps_os{i}", [P, 512], F32)) for i in range(2)]
        ps_p = ctx.enter_context(nc.psum_tensor("ps_pt", [P, 512], F32))
        ps_sum = ctx.enter_context(nc.psum_tensor("ps_sum", [P, 512], F32))

        once_in, w_in_, w_T = sem("once_in"), sem("wcol_in"), sem("wcol_T")
        ik_in, k_in, v_in = ([sem(f"{n}{i}") for i in range(2)] for n in ("ikc_in", "kc_in", "vc_in"))
        once_ok, q_ok = sem("once_ok"), sem("q_s_ok")
        ik_T, ik_ok, s_mm, rel_ok, sum_mm = (sem(n) for n in ("ik_T", "ikT_ok", "si_mm", "rel_ok", "sum_mm"))
        scored, top, mask_ok = sem("scored"), sem("top_s"), sem("mask_s_ok")
        sig_ok, gate_ok = sem("sig_s"), sem("gate_s_ok")
        k_T, k_ok, l_mm, max_ok, bias_ok, exp_ok, recip_ok, probs_ok = (
            sem(n) for n in ("ks_T", "ks_ok", "ls_mm", "max_s", "bias_s", "exp_s", "recip_s", "probs_s_ok"))
        p_T, pT_ok, av_mm, att_ok, hi_ok, lo_ok = (sem(n) for n in ("ps_T", "pTs_ok", "avs_mm", "atts_ok", "his_ok", "los_ok"))
        zt = scr["zt"]
        block = ctx.enter_context(nc.Block())

        @block.sync
        def _(sp):
            def cached_idx(b):
                if b >= 2:
                    sp.wait_ge(ik_T, b - 1)
                src = io["cache_idx_k"][0, b].rearrange("(n p) d -> p n d", p=P)
                for twice in range(2):
                    sp.dma_start(ik_rows[:, b % 2, :, twice], src).then_inc(ik_in[b % 2], 16)

            def cached_kv(b):
                s = b % 2
                if b >= 2:
                    sp.wait_ge(k_T, b - 1)
                sp.dma_start(k_rows[:, s], io["cache_k"][0, b].rearrange("(n p) h d -> p n (h d)", p=P)).then_inc(k_in[s], 16)
                if b >= 2:
                    sp.wait_ge(av_mm, b - 1)
                sp.dma_start(v_rows[:, s], io["cache_v"][0, b].rearrange("(n p) h d -> p n (h d)", p=P)).then_inc(v_in[s], 16)
                sp.dma_start(v_new[:, s], out["v_sample"][0, b].rearrange("t h d -> t (h d)")).then_inc(v_in[s], 16)

            cached_idx(0)
            sp.dma_start(stage[:], zt[IQ0:IK0, SEQ:TOK].rearrange("(a q) t -> q a t", q=P)).then_inc(once_in, 16)
            for half in range(2):
                sp.dma_start(ik_new[64 * half:64 * half + 64, :], zt[IK0:IW0, SEQ:TOK]).then_inc(once_in, 16)
            src = zt[IW0:IW0 + IDX_HEADS, SEQ:TOK].rearrange("(a h) (b t) -> h b a t", h=2, b=DEC_B)
            for h2 in range(2):
                sp.dma_start(w_rows[DEC_B * h2:DEC_B * h2 + DEC_B], src[h2]).then_inc(w_in_, 16)
            cached_idx(1)
            cached_kv(0)
            cached_kv(1)
            sp.wait_ge(q_ok, 1)
            sp.dma_start(stage[:], zt[Q0:K0, SEQ:TOK].rearrange("(h d) t -> d h t", d=HD)).then_inc(once_in, 16)
            sp.dma_start(za[:], zt[ZA0:U0, SEQ:TOK].rearrange("(h d) t -> d h t", d=HD)).then_inc(once_in, 16)
            for b in range(2, DEC_B):
                cached_idx(b)
            for b in range(2, DEC_B):
                cached_kv(b)

        @block.scalar
        def _(act):
            A = nc.scalar.activation

            def idx_keys(b):
                s = b % 2
                act.wait_ge(ik_T, b + 1)
                if b >= 2:
                    act.wait_ge(s_mm, 2 * b - 2)
                if b == 0:
                    act.wait_ge(once_in, 16 * 3)
                A(ikT[:, s, 0:PAST], ps_k[s][:, 0:PAST], ACT.Copy).then_inc(ik_ok, 1)
                A(ikT[:, s, PAST:DEC_KEYS], ik_new[:, DEC_S * b:DEC_S * b + DEC_S], ACT.Copy).then_inc(ik_ok, 1)

            def keys(b):
                s = b % 2
                act.wait_ge(k_T, b + 1)
                if b >= 2:
                    act.wait_ge(l_mm, b - 1)
                A(kT_s[:, s, :, 0:PAST], ps_k[s][:].rearrange("p (h n) -> p h n", h=KV_HEADS), ACT.Copy).then_inc(k_ok, 1)
                A(kT_s[:, s, :, PAST:DEC_KEYS], kT[:, :, SEQ + DEC_S * b:SEQ + DEC_S * b + DEC_S], ACT.Copy).then_inc(k_ok, 1)

            def exponentials(b):
                s = b % 2
                act.wait_ge(bias_ok, b + 1)
                if b >= 2:
                    act.wait_ge(p_T, b - 1)
                A(probs[:, s], ps_a[s][:, 0:DEC_KEYS], ACT.Exp, bias=stat[:, 1, s:s + 1], scale=SCALE,
                  accum_out=stat[:, 2, s:s + 1]).then_inc(exp_ok, 1)

            def turned(b):
                s = b % 2
                act.wait_ge(p_T, b + 1)
                if b >= 2:
                    act.wait_ge(av_mm, b - 1)
                A(pT[:, s, 0:BLK].rearrange("p n t -> p (n t)"), ps_p[:, 0:BLK * P], ACT.Copy).then_inc(pT_ok, 1)
                A(pT[0:DEC_S, s, BLK], ps_p[0:DEC_S, BLK * P:BLK * P + P], ACT.Copy).then_inc(pT_ok, 1)

            def high(b):
                act.wait_ge(att_ok, b + 1)
                view = mix_hi[:].rearrange("p h (s n) -> p h s n", s=STEP)[:, :, :, PSTEP + 2 * b:PSTEP + 2 * b + 2]
                A(view, att[:, b % 2].rearrange("p (h c s) -> p h s c", h=HEADS, c=2), ACT.Copy).then_inc(hi_ok, 1)

            for b in range(DEC_B):
                idx_keys(b)
            act.wait_ge(once_in, 16 * 5)
            A(gate[:], za[:], ACT.Sigmoid).then_inc(sig_ok, 1)
            keys(0)
            for b in range(DEC_B + 2):
                if b < DEC_B:
                    exponentials(b)
                if b + 1 < DEC_B:
                    keys(b + 1)
                if 1 <= b <= DEC_B:
                    turned(b - 1)
                if b >= 2:
                    high(b - 2)

        @block.gpsimd
        def _(pool):
            for n, to in enumerate((iq, q)):
                pool.wait_ge(once_in, 16 * (5 if n else 3))
                nc.gpsimd.tensor_copy(to[:].rearrange("p b (h t) -> p h b t", t=DEC_S),
                                      stage[:].rearrange("p h (b t) -> p h b t", t=DEC_S)).then_inc(q_ok, 1)
            pool.wait_ge(sig_ok, 1)
            nc.gpsimd.tensor_tensor(gate[:], gate[:], za[:], ALU.mult).then_inc(gate_ok, 1)

        @block.vector
        def _(dve):
            V = nc.vector
            V.memset(pick[:], 0.0).then_inc(once_ok, 1)
            dve.wait_ge(once_ok, 1)
            V.tensor_reduce(pick[:, 112:128], ident[:].rearrange("p (h t) -> p t h", t=DEC_S), AX_X, ALU.add).then_inc(once_ok, 1)
            V.tensor_copy(spread[:], bc(ident[:].rearrange("p (b t) -> p b t", t=DEC_S), 2, HEADS)).then_inc(once_ok, 1)
            V.memset(score[:, DEC_KEYS:DEC_KEYS + 8], DUMMY).then_inc(once_ok, 1)
            dve.wait_ge(w_T, 1)
            V.tensor_scalar(wcol[:].rearrange("p h b -> p (h b)"), ps_p[:, 0:2 * DEC_B], IDX_DIM ** -0.5 * IDX_HEADS ** -0.5, None, ALU.mult).then_inc(once_ok, 1)
            dve.wait_ge(once_ok, 5)
            for b in range(DEC_B):
                for h2 in range(2):
                    dve.wait_ge(s_mm, 2 * b + h2 + 1)
                    if b:
                        dve.wait_ge(sum_mm, 2 * b + h2 - 1)
                    V.tensor_scalar(rel[:, h2], ps_a[h2][:, 0:DEC_KEYS], 0.0, wcol[:, h2, b:b + 1],
                                    ALU.max, ALU.mult).then_inc(rel_ok, 1)
            dve.wait_ge(sum_mm, 2 * DEC_B)
            V.tensor_copy(score[:, 0:DEC_KEYS], ps_sum[:, 0:DEC_KEYS]).then_inc(top, 1)
            n = 1
            for r in range(DEC_TOPK // 8 + 1):
                dve.wait_ge(top, n)
                V.max(top8[:], score[:]).then_inc(top, 1)
                dve.wait_ge(top, n + 1)
                n += 2
                if r == DEC_TOPK // 8:
                    V.memset(top8[:, DEC_TOPK % 8:8], DUMMY).then_inc(top, 1)
                    dve.wait_ge(top, n)
                    n += 1
                V.match_replace(score[:], top8[:], score[:], CHOSEN).then_inc(top, 1)
            dve.wait_ge(top, n)
            V.tensor_scalar(mask[:], score[:, 0:DEC_KEYS], (CHOSEN + UNSEEN) / 2, MASKED, ALU.is_gt, ALU.mult).then_inc(mask_ok, 1)

            def largest(b):
                s = b % 2
                dve.wait_ge(l_mm, b + 1)
                V.tensor_reduce(stat[:, 0, s:s + 1], ps_a[s][:, 0:DEC_KEYS], AX_X, ALU.max).then_inc(max_ok, 1)
                dve.wait_ge(max_ok, b + 1)
                V.tensor_scalar(stat[:, 1, s:s + 1], stat[:, 0, s:s + 1], -SCALE, None, ALU.mult).then_inc(bias_ok, 1)

            def normalise(b):
                s = b % 2
                dve.wait_ge(exp_ok, b + 1)
                V.reciprocal(stat[:, 3, s:s + 1], stat[:, 2, s:s + 1]).then_inc(recip_ok, 1)
                dve.wait_ge(recip_ok, b + 1)
                V.tensor_scalar(probs[:, s], probs[:, s], stat[:, 3, s:s + 1], None, ALU.mult).then_inc(probs_ok, 1)

            def gate_it(b):
                s = b % 2
                dve.wait_ge(av_mm, b + 1)
                dve.wait_ge(gate_ok, 1)
                if b >= 2:
                    dve.wait_ge(lo_ok, b - 1)
                V.tensor_tensor(att[:, s].rearrange("p (h t) -> p h t", h=HEADS), ps_o[s][:, 0:P].rearrange("p (h t) -> p h t", h=HEADS),
                                gate[:, :, DEC_S * b:DEC_S * b + DEC_S], ALU.mult).then_inc(att_ok, 1)

            def low(b):
                dve.wait_ge(hi_ok, b + 1)
                view = lambda m: m[:].rearrange("p h (s n) -> p h s n", s=STEP)[:, :, :, PSTEP + 2 * b:PSTEP + 2 * b + 2]
                V.tensor_tensor(view(mix_lo), att[:, b % 2].rearrange("p (h c s) -> p h s c", h=HEADS, c=2),
                                view(mix_hi).bitcast(F32), ALU.subtract).then_inc(lo_ok, 1)

            for b in range(DEC_B + 3):
                if b < DEC_B:
                    largest(b)
                if 1 <= b <= DEC_B:
                    normalise(b - 1)
                if 3 <= b:
                    low(b - 3)
                if 2 <= b < DEC_B + 2:
                    gate_it(b - 2)

        @block.tensor
        def _(pe):
            M, TR = nc.tensor.matmul, nc.tensor.transpose

            def turn_idx(b):
                s = b % 2
                pe.wait_ge(ik_in[s], 32 * (b // 2 + 1))
                if b >= 2:
                    pe.wait_ge(ik_ok, 2 * b - 2)
                for n in range(BLK):
                    ins = TR(ps_k[s][:, n * P:n * P + P], ik_rows[:, s, n].rearrange("p a d -> p (a d)"), ident[:])
                ins.then_inc(ik_T, 1)

            def scores(b):
                pe.wait_ge(ik_ok, 2 * b + 2)
                for h2 in range(2):
                    half = slice(64 * h2, 64 * h2 + 64)
                    if b:
                        pe.wait_ge(rel_ok, 2 * b + h2 - 1)
                    M(ps_a[h2][:, 0:DEC_KEYS], iq[half, b], ikT[half, b % 2],
                      start=True, stop=True).then_inc(s_mm, 1)

            def sums(b):
                for h2 in range(2):
                    pe.wait_ge(rel_ok, 2 * b + h2 + 1)
                    M(ps_sum[:, 0:DEC_KEYS], pick[:, 112 - DEC_S * b:240 - DEC_S * b], rel[:, h2], start=b + h2 == 0,
                      stop=b == DEC_B - 1 and h2 == 1).then_inc(sum_mm, 1)

            turn_idx(0)
            turn_idx(1)
            pe.wait_ge(w_in_, 32)
            TR(ps_p[:, 0:2 * DEC_B], w_rows[:].rearrange("r a t -> r (a t)"), ident[0:2 * DEC_B, 0:2 * DEC_B]).then_inc(w_T, 1)
            pe.wait_ge(q_ok, 1)
            for b in range(DEC_B):
                scores(b)
                if b:
                    sums(b - 1)
                if b + 2 < DEC_B:
                    turn_idx(b + 2)
            sums(DEC_B - 1)

            def turn_keys(b):
                s = b % 2
                pe.wait_ge(k_in[s], 16 * (b // 2 + 1))
                if b < 2:
                    pe.wait_ge(ik_ok, 2 * DEC_B)
                else:
                    pe.wait_ge(k_ok, 2 * b - 2)
                for h in range(KV_HEADS):
                    for n in range(BLK):
                        c = (h * BLK + n) * P
                        ins = TR(ps_k[s][:, c:c + P], k_rows[:, s, n, h * HD:h * HD + HD], ident[:])
                ins.then_inc(k_T, 1)

            def logits(b):
                s = b % 2
                pe.wait_ge(k_ok, 2 * b + 2)
                if b == 0:
                    pe.wait_ge(mask_ok, 1)
                    pe.wait_ge(q_ok, 2)
                if b < 2:
                    pe.wait_ge(rel_ok, 2 * DEC_B)
                else:
                    pe.wait_ge(exp_ok, b - 1)
                M(ps_a[s][:, 0:DEC_KEYS], spread[:, b].rearrange("p h t -> p (h t)"), mask[:], start=True, stop=False)
                for h in range(KV_HEADS):
                    ins = M(ps_a[s][64 * h:64 * h + 64, 0:DEC_KEYS], q[:, b, 64 * h:64 * h + 64],
                            kT_s[:, s, h], start=False, stop=True)
                ins.then_inc(l_mm, 1)

            def turn(b):
                s = b % 2
                pe.wait_ge(probs_ok, b + 1)
                if b:
                    pe.wait_ge(pT_ok, 2 * b)
                for n in range(BLK + 1):
                    w = P if n < BLK else DEC_S
                    ins = TR(ps_p[0:w, n * P:n * P + P], probs[:, s, n * P:n * P + w], ident[:])
                ins.then_inc(p_T, 1)

            def values(b):
                s = b % 2
                pe.wait_ge(pT_ok, 2 * b + 2)
                pe.wait_ge(v_in[s], 32 * (b // 2 + 1))
                if b >= 2:
                    pe.wait_ge(att_ok, b - 1)
                for h in range(KV_HEADS):
                    for n in range(BLK + 1):
                        w = P if n < BLK else DEC_S
                        v = v_rows[:, s, n, h * HD:h * HD + HD] if n < BLK else v_new[:, s, h * HD:h * HD + HD]
                        ins = M(ps_o[s][:, 64 * h:64 * h + 64], v, pT[0:w, s, n, 64 * h:64 * h + 64],
                                start=n == 0 and h == 0, stop=n == BLK and h == KV_HEADS - 1)
                ins.then_inc(av_mm, 1)

            turn_keys(0)
            turn_keys(1)
            logits(0)
            for b in range(DEC_B + 1):
                if b + 1 < DEC_B:
                    logits(b + 1)
                if b < DEC_B:
                    turn(b)
                if b:
                    values(b - 1)
                if b + 2 < DEC_B:
                    turn_keys(b + 2)


OC = 512
NOC = D_MODEL // OC
ROWS = TOK // STEP
GROUP_TILES = ((0, 5), (5, 4))


def gate_rows(nc, io, keep):
    ident, gpost, sel = keep["ident"], keep["gpost"], keep["sel"]
    with ExitStack() as ctx:
        signals = cleared_after(nc, ctx)

        def sb(name, shape, dt=F32):
            return ctx.enter_context(nc.sbuf_tensor(name, shape, dt))

        def sem(name):
            return new_signal(nc, signals, name)

        HALF_D = D_MODEL // 2
        c_rows = sb("c_rows", [64, D_MODEL])
        cT = sb("cT2", [P, KB, 64])
        wg = sb("wg", [P, 2, 4, OC])
        bias, post = sb("bias_rows", [P, HALF_D]), sb("post_rows", [P, HALF_D])
        full = sb("gate_full", [P, HALF_D])
        low = sb("low_rows", [P, 1])
        ps_c = [ctx.enter_context(nc.psum_tensor(f"ps_c{i}", [P, 512], F32)) for i in range(2)]
        ps_g = [ctx.enter_context(nc.psum_tensor(f"ps_gate{i}", [P, 512], F32)) for i in range(NOC)]
        zero_ok, rows_in, c_T, cT_ok, ones_ok = (sem(n) for n in ("zero_ok", "c_rows_in", "c2_T", "cT2_ok", "ones_ok"))
        w_in, g_mm, g_step = [sem("wg_in0"), sem("wg_in1")], sem("gate_mm"), sem("gate_step")
        sel_step = sem("sel_step")
        block = ctx.enter_context(nc.Block())
        wv = io["w_ada"][0].rearrange("(k p) n -> p k n", p=P)

        @block.sync
        def _(sp):
            sp.wait_ge(zero_ok, 3)
            for r in (0, 32):
                sp.dma_start(c_rows[r:r + 1, :], io["c_prompt"]).then_inc(rows_in, 16)
                sp.dma_start(c_rows[r + 1:r + COND, :], io["c_sample"]).then_inc(rows_in, 16)
            for r in range(4):
                cols = slice(HALF_D * (r // 2), HALF_D * (r // 2) + HALF_D)
                bsrc = io["b_ada"][0:1, 2 * D_MODEL:3 * D_MODEL][:, cols]
                sp.dma_start(bias[32 * r:32 * r + COND, :], bsrc.broadcast_to([COND, HALF_D])).then_inc(rows_in, 16)
                sp.dma_start(post[32 * r:32 * r + COND, :], io["g_post"][:, cols].broadcast_to([COND, HALF_D])).then_inc(rows_in, 16)
            for n in range(4 * NOC):
                if n >= 2:
                    sp.wait_ge(g_mm, n - 1)
                c, k = n // 4, n % 4
                src = wv[:, 4 * k:4 * k + 4, 2 * D_MODEL + OC * c:2 * D_MODEL + OC * c + OC]
                sp.dma_start(wg[:, n % 2], src).then_inc(w_in[n % 2], 16)

        @block.gpsimd
        def _(pool):
            G = nc.gpsimd
            ones = keep["sel_f"]
            G.memset(ones[:], 0.0).then_inc(sel_step, 1)
            pool.wait_ge(sel_step, 1)
            n = 1
            for base in range(0, P, 32):
                for at, width in ((0, PSTEP), (ROWS, PSTEP)):
                    G.memset(ones[base:base + 1, at:at + width], 1.0).then_inc(sel_step, 1)
                    n += 1
            pool.wait_ge(sel_step, n)
            for base in range(0, P, 32):
                part = ones[base:base + COND, PSTEP:ROWS]
                G.affine_select(out=part, in_=part, compare_op=ALU.not_equal, fill=1.0, base=-2, pattern=[[-1, ROWS - PSTEP]],
                                channel_multiplier=2).then_inc(sel_step, 1)
                n += 1
            pool.wait_ge(sel_step, n)
            for base in range(0, P, 32):
                part = ones[base:base + COND, PSTEP:ROWS]
                G.affine_select(out=part, in_=part, compare_op=ALU.not_equal, fill=1.0, base=-1, pattern=[[-1, ROWS - PSTEP]],
                                channel_multiplier=2).then_inc(sel_step, 1)
                n += 1
            pool.wait_ge(sel_step, n)
            G.tensor_copy(sel[:], ones[:]).then_inc(ones_ok, 1)

        @block.scalar
        def _(act):
            for i in range(2):
                act.wait_ge(c_T, i + 1)
                nc.scalar.activation(cT[:, 8 * i:8 * i + 8].rearrange("p k c -> p (k c)"), ps_c[i][:], ACT.Copy).then_inc(cT_ok, 1)

        @block.vector
        def _(dve):
            V = nc.vector
            V.memset(c_rows[:], 0.0).then_inc(zero_ok, 1)
            V.memset(bias[:], 0.0).then_inc(zero_ok, 1)
            V.memset(post[:], 0.0).then_inc(zero_ok, 1)
            V.memset(low[:], 0.0).then_inc(g_step, 1)
            dve.wait_ge(g_step, 1)
            for r in (32, 96):
                V.memset(low[r:r + 32, :], -1.0).then_inc(g_step, 1)
            dve.wait_ge(rows_in, 16 * 12)
            n = 3
            for c in range(NOC):
                rows = slice(64 * (c // 2), 64 * (c // 2) + 64)
                cols = slice(OC * (c % 2), OC * (c % 2) + OC)
                dve.wait_ge(g_mm, 4 * c + 4)
                V.tensor_tensor(full[rows, cols], ps_g[c][rows, :], bias[rows, cols], ALU.add).then_inc(g_step, 1)
                dve.wait_ge(g_step, n + 1)
                V.tensor_tensor(full[rows, cols], full[rows, cols], post[rows, cols], ALU.mult).then_inc(g_step, 1)
                n += 2
            dve.wait_ge(g_step, n)
            V.tensor_copy(gpost[:], full[:]).then_inc(g_step, 1)
            dve.wait_ge(g_step, n + 1)
            V.scalar_tensor_tensor(bias[:], gpost[:].bitcast(F32), low[:], full[:], ALU.mult, ALU.add).then_inc(g_step, 1)
            dve.wait_ge(g_step, n + 2)
            V.tensor_copy(gpost[:], bias[:]).then_inc(g_step, 1)

        @block.tensor
        def _(pe):
            pe.wait_ge(rows_in, 16 * 12)
            for i in range(2):
                for k in range(8):
                    ins = nc.tensor.transpose(ps_c[i][:, 64 * k:64 * k + 64], c_rows[:, P * (8 * i + k):P * (8 * i + k) + P],
                                              ident[0:64, 0:64])
                ins.then_inc(c_T, 1)
            pe.wait_ge(cT_ok, 2)
            for n in range(4 * NOC):
                c, q = n // 4, n % 4
                rows = slice(64 * (c // 2), 64 * (c // 2) + 64)
                pe.wait_ge(w_in[n % 2], 16 * (n // 2 + 1))
                for k in range(4):
                    ins = nc.tensor.matmul(ps_g[c][rows, :], cT[:, 4 * q + k], wg[:, n % 2, k], start=q + k == 0, stop=q + k == 6)
                ins.then_inc(g_mm, 1)


def project_out(nc, io, out, keep, scr):
    gpost, sel = keep["gpost"], keep["sel"]
    MIX_HI, MIX_LO = (keep["attn_hi"], keep["ssm_hi"]), (keep["attn_lo"], keep["ssm_lo"])
    NB = KB // 2
    with ExitStack() as ctx:
        signals = cleared_after(nc, ctx)

        def sb(name, shape, dt=F32):
            return ctx.enter_context(nc.sbuf_tensor(name, shape, dt))

        def sem(name):
            return new_signal(nc, signals, name)

        rows = [nc.alloc_sbuf_tensor_at("out_rows0", [P, D_MODEL], F32, offset=keep["maskb_base"])]
        square = nc.alloc_sbuf_tensor_at("out_square", [P, OC], BF16, offset=keep["maskb_base"] + 4 * D_MODEL)
        rows += [sb(f"out_rows{i}", [P, D_MODEL]) for i in range(1, 5)]
        w_raw = sb("o_raw", [P, 2, OC])
        w_hi, w_lo = sb("o_hi", [P, 2, OC], F32R), sb("o_lo", [P, 2, OC], F32R)
        xs = sb("x_add", [P, 2, OC])
        ssq = sb("ssq", [P, 5, NOC])
        stat = sb("out_stat", [P, 5, 5])
        ps_o = [ctx.enter_context(nc.psum_tensor(f"ps_out{i}", [P, 512], F32)) for i in range(5)]
        ps_g = [ctx.enter_context(nc.psum_tensor(f"ps_gt{i}", [P, 512], F32)) for i in range(2)]

        w_in, x_in = [sem("ow_in0"), sem("ow_in1")], [sem("x_add0"), sem("x_add1")]
        w_hi_ok, w_lo_ok, w_used = sem("ow_hi"), sem("ow_lo"), sem("ow_used")
        out_mm, out_read, squared = sem("out_mm"), sem("out_read"), sem("out_sq")
        rstd_step, root_ok, g_mm, scaled, y_ok = (sem(n) for n in ("rstd_step", "o_root", "g_copied", "scaled", "y_ok"))
        y_out = [sem(f"y_out{i}") for i in range(5)]
        passed, passed_v, ssq_ready = sem("passed_o"), sem("passed_v"), sem("ssq_ready")
        block = ctx.enter_context(nc.Block())
        wv = io["w_out"][0].rearrange("(k p) n -> p k n", p=P)

        def pieces(tile, dram_p, dram_s):
            found = []
            c = P * tile
            while c < P * tile + P:
                s, m = divmod(c, ROWS)
                end = min(P * tile + P, ROWS * s + (PSTEP if m < PSTEP else ROWS))
                dram, m = (dram_p, m) if m < PSTEP else (dram_s, m - PSTEP)
                v = dram.rearrange("(m s) d -> s m d", s=STEP)[s, m:m + end - c]
                found.append((c - P * tile, end - c, v))
                c = end
            return found

        xv = (io["x_prompt"].rearrange("b t d -> (b t) d"), io["x_sample"].rearrange("b t d -> (b t) d"))
        yv = (out["y_prompt"].rearrange("b t d -> (b t) d"), out["y_sample"].rearrange("b t d -> (b t) d"))
        finals = [[(i, q) for i in range(n) for q in range(NOC)] for _, n in GROUP_TILES]
        n_pieces = [sum(len(pieces(t0 + i, *xv)) for i in range(n)) for t0, n in GROUP_TILES]
        before = (0, len(finals[0]))
        PIECES = KB * NOC

        def x_landed(g, f):
            total = 0
            for gg, (t0, n) in enumerate(GROUP_TILES):
                for ff, (i, q) in enumerate(finals[gg]):
                    if (before[gg] + ff) % 2 == (before[g] + f) % 2:
                        total += 16 * len(pieces(t0 + i, *xv))
                    if gg == g and ff == f:
                        return total

        def y_left(g, i):
            return sum(16 * NOC * len(pieces(t0 + i, *yv)) for gg, (t0, n) in enumerate(GROUP_TILES) if gg <= g and i < n)

        def tiles_before(g, c):
            return c * GROUP_TILES[g][1] + (NOC * GROUP_TILES[0][1] if g else 0)

        def finals_at(g, c, kb):
            if g == 0 or not isinstance(c, int) or c or kb == 0:
                return []
            return [f for f in (2 * kb - 2, 2 * kb - 1) if f < len(finals[0])]

        def chunks(eng, body):
            for g in range(2):
                body(g, 0)
                with eng.Fori(1, NOC - 1) as c:
                    body(g, c)
                body(g, NOC - 1)

        @block.sync
        def _(sp):
            def load_x(g, f):
                n = before[g] + f
                i, q = finals[g][f]
                if n >= 2:
                    sp.wait_ge(y_ok, n - 1)
                for p0, m, v in pieces(GROUP_TILES[g][0] + i, *xv):
                    sp.dma_start(xs[p0:p0 + m, n % 2], v[:, OC * q:OC * q + OC]).then_inc(x_in[n % 2], 16)

            def store_y(g, f):
                i, q = finals[g][f]
                sp.wait_ge(y_ok, before[g] + f + 1)
                for p0, m, v in pieces(GROUP_TILES[g][0] + i, *yv):
                    sp.dma_start(v[:, OC * q:OC * q + OC], rows[i][p0:p0 + m, OC * q:OC * q + OC]).then_inc(y_out[i], 16)

            def body(g, c):
                for kb in range(KB):
                    if g or kb >= 2 or not isinstance(c, int) or c:
                        sp.wait_ge(w_lo_ok, c * KB + (g * PIECES + kb - 1))
                    sp.dma_start(w_raw[:, kb % 2], wv[:, kb, bass.ds(c * OC, OC)]).then_inc(w_in[kb % 2], 16)
                    if kb:
                        for f in finals_at(g, c, kb - 1):
                            store_y(0, f)
                    for f in finals_at(g, c, kb):
                        load_x(0, f)

            chunks(sp, body)
            load_x(1, 0)
            load_x(1, 1)
            for f in range(len(finals[1])):
                store_y(1, f)
                if f + 2 < len(finals[1]):
                    load_x(1, f + 2)
            for i in range(5):
                sp.wait_ge(y_out[i], y_left(1, i))

        @block.gpsimd
        def _(pool):
            for g in range(2):
                for f, (i, q) in enumerate(finals[g]):
                    n = before[g] + f
                    part = rows[i][:, OC * q:OC * q + OC]
                    pool.wait_ge(x_in[n % 2], x_landed(g, f))
                    pool.wait_ge(scaled, n + 1)
                    nc.gpsimd.tensor_tensor(part, part, xs[:, n % 2], ALU.add).then_inc(y_ok, 1)

        @block.scalar
        def _(act):
            A = nc.scalar.activation

            def high(g, c, kb):
                act.wait_ge(w_in[kb % 2], c * (8 * KB) + 16 * (g * PIECES // 2 + kb // 2 + 1))
                if kb == 1:
                    if g or not isinstance(c, int) or c:
                        act.wait_ge(out_mm, tiles_before(g, c))
                elif not (g == 0 and isinstance(c, int) and c == 0 and kb == 0):
                    act.wait_ge(w_used, c * (KB - 1) + (g * NOC * (KB - 1) + max(kb - 1, 0)))
                A(w_hi[:, kb % 2], w_raw[:, kb % 2], ACT.Copy).then_inc(w_hi_ok, 1)

            def body(g, c):
                for kb in range(1, KB):
                    high(g, c, kb)
                last = isinstance(c, int) and c == NOC - 1
                if not last:
                    high(g, c + 1, 0)
                elif g == 0:
                    high(1, 0, 0)
                for i in range(GROUP_TILES[g][1]):
                    if g and isinstance(c, int) and c == 0:
                        act.wait_ge(y_out[i], y_left(0, i))
                    act.wait_ge(out_mm, tiles_before(g, c) + (i + 1))
                    if g or i or not isinstance(c, int) or c:
                        act.wait_ge(squared, tiles_before(g, c) + i)
                    act.sem_inc(passed, 1)
                    A(square[:], ps_o[i][:], ACT.Square, accum_out=ssq[:, i, bass.ds(c, 1)]).then_inc(squared, 1)
                    A(rows[i][:, bass.ds(c * OC, OC)], ps_o[i][:], ACT.Copy).then_inc(out_read, 1)
                if last:
                    act.wait_ge(rstd_step, 8 * g + 2)
                    A(stat[:, 2], stat[:, 1], ACT.Sqrt).then_inc(root_ok, 1)

            act.wait_ge(ssq_ready, 1)
            high(0, 0, 0)
            chunks(act, body)

        @block.vector
        def _(dve):
            V = nc.vector

            def low(g, c, kb):
                dve.wait_ge(w_hi_ok, c * KB + (g * PIECES + kb + 1))
                V.tensor_tensor(w_lo[:, kb % 2], w_raw[:, kb % 2], w_hi[:, kb % 2].bitcast(F32), ALU.subtract).then_inc(w_lo_ok, 1)

            def scale(g, f):
                i, q = finals[g][f]
                part = rows[i][:, OC * q:OC * q + OC]
                dve.wait_ge(g_mm, before[g] + f + 1)
                V.scalar_tensor_tensor(part, part, stat[:, 4, i:i + 1], ps_g[(before[g] + f) % 2][:], ALU.mult, ALU.mult).then_inc(scaled, 1)

            def rstd(g):
                n = 8 * g
                dve.wait_ge(squared, tiles_before(g, NOC))
                V.tensor_reduce(stat[:, 0], ssq[:], AX_X, ALU.add).then_inc(rstd_step, 1)
                dve.wait_ge(rstd_step, n + 1)
                V.tensor_scalar(stat[:, 1], stat[:, 0], 1.0 / D_MODEL, EPS, ALU.mult, ALU.add).then_inc(rstd_step, 1)
                dve.wait_ge(root_ok, g + 1)
                V.reciprocal(stat[:, 3], stat[:, 2]).then_inc(rstd_step, 1)
                dve.wait_ge(rstd_step, n + 3)
                V.tensor_tensor(stat[:, 4], stat[:, 3], stat[:, 3], ALU.mult).then_inc(rstd_step, 1)
                dve.wait_ge(rstd_step, n + 4)
                V.tensor_tensor(stat[:, 4], stat[:, 4], stat[:, 1], ALU.mult).then_inc(rstd_step, 1)
                dve.wait_ge(rstd_step, n + 5)
                V.tensor_scalar(stat[:, 4], stat[:, 4], -0.5, 1.5, ALU.mult, ALU.add).then_inc(rstd_step, 1)
                dve.wait_ge(rstd_step, n + 6)
                V.tensor_tensor(stat[:, 4], stat[:, 4], stat[:, 3], ALU.mult).then_inc(rstd_step, 1)
                dve.wait_ge(rstd_step, n + 7)
                dve.sem_inc(rstd_step, 1)

            def body(g, c):
                last = isinstance(c, int) and c == NOC - 1
                for kb in range(1, KB):
                    low(g, c, kb)
                    for f in finals_at(g, c, kb):
                        scale(0, f)
                if not last:
                    low(g, c + 1, 0)
                elif g == 0:
                    low(1, 0, 0)
                if last:
                    rstd(g)

            V.memset(ssq[:], 1.0).then_inc(passed_v, 1)
            dve.wait_ge(passed_v, 1)
            dve.sem_inc(ssq_ready, 1)
            low(0, 0, 0)
            chunks(dve, body)
            for f in range(len(finals[1])):
                scale(1, f)

        @block.tensor
        def _(pe):
            M = nc.tensor.matmul

            def gates(g, f):
                i, q = finals[g][f]
                n = before[g] + f
                half = slice(64 * (q // 2), 64 * (q // 2) + 64)
                c0 = P * (GROUP_TILES[g][0] + i) % ROWS
                if n >= 2:
                    pe.wait_ge(scaled, n - 1)
                M(ps_g[n % 2][:], sel[half, c0:c0 + P], gpost[half, OC * (q % 2):OC * (q % 2) + OC],
                  start=True, stop=True).then_inc(g_mm, 1)

            def body(g, c):
                t0, tiles = GROUP_TILES[g]
                for kb in range(KB):
                    hi, lo = MIX_HI[kb // NB], MIX_LO[kb // NB]
                    pe.wait_ge(w_lo_ok, c * KB + (g * PIECES + kb + 1))
                    for i in range(tiles):
                        if kb == 0 and (g or not isinstance(c, int) or c):
                            first = isinstance(c, int) and c == 0
                            pe.wait_ge(out_read, tiles_before(g, c) + (i + 1 - GROUP_TILES[0 if first else g][1]))
                            pe.wait_ge(squared, tiles_before(g, c) + (i + 1 - GROUP_TILES[0 if first else g][1]))
                        cols = slice(P * (t0 + i), P * (t0 + i) + P)
                        M(ps_o[i][:], hi[:, kb % NB, cols], w_hi[:, kb % 2], start=kb == 0, stop=False)
                        M(ps_o[i][:], hi[:, kb % NB, cols], w_lo[:, kb % 2], start=False, stop=False)
                        ins = M(ps_o[i][:], lo[:, kb % NB, cols], w_hi[:, kb % 2], start=False, stop=kb == KB - 1)
                        if kb == KB - 1:
                            ins.then_inc(out_mm, 1)
                    if kb < KB - 1:
                        ins.then_inc(w_used, 1)
                    for f in finals_at(g, c, kb):
                        gates(0, f)

            chunks(pe, body)
            for f in range(len(finals[1])):
                gates(1, f)


_INS = ("x_prompt", "x_sample", "c_prompt", "c_sample", "cache_k", "cache_v", "cache_idx_k", "state_ssm_re",
        "state_ssm_im", "w_ada", "b_ada", "g_pre", "g_post", "w_in", "lambda_re", "lambda_im", "log_dt", "b_re",
        "b_im", "c_re", "c_im", "d_skip", "w_glu", "b_glu", "w_out")
_OUTS = (
    ("y_prompt", (1, SEQ, D_MODEL)), ("y_sample", (DEC_B, DEC_S, D_MODEL)),
    ("k_prompt", (1, 1, SEQ, KV_HEADS, HD)), ("v_prompt", (1, 1, SEQ, KV_HEADS, HD)), ("idx_k_prompt", (1, 1, SEQ, IDX_DIM)),
    ("ssm_re_prompt", (1, 1, GROUPS, STATE)), ("ssm_im_prompt", (1, 1, GROUPS, STATE)),
    ("k_sample", (1, DEC_B, DEC_S, KV_HEADS, HD)), ("v_sample", (1, DEC_B, DEC_S, KV_HEADS, HD)),
    ("idx_k_sample", (1, DEC_B, DEC_S, IDX_DIM)),
    ("ssm_re_sample", (1, DEC_B, GROUPS, STATE)), ("ssm_im_sample", (1, DEC_B, GROUPS, STATE)),
)


def hybrid_layer(nc, io, out):
    scr = {name: nc.dram_tensor(name, shape, F32, kind="Internal").ap() for name, shape in (
        ("zt", [COLS, TOK]), ("s5_in", [P, PAIRS, 2, P]), ("s5_out", [P, PAIRS, 2, P]),
        ("taps", [GROUPS, CH, TAPS * CH]), ("y", [1024, TOK]))}
    with ExitStack() as ctx:
        def sb(name, shape, dt=F32):
            return ctx.enter_context(nc.sbuf_tensor(name, shape, dt))

        keep = {"ident": sb("ident", [P, P]), "vecT": sb("vecT", [P, 72])}
        mod_base = nc.sbuf_base
        keep["mod"] = sb("mod", [P, 2 * KB, COND])
        keep["s5_tabs"] = sb("s5_tabs", [P, 5, PAIRS])
        keep["maskb_base"] = nc.sbuf_base
        keep["maskb"] = sb("maskb", [P, P * (NT - 1) * NT // 2], BF16)
        with ExitStack() as early:
            keep["xT_base"] = (nc.sbuf_base + 31) // 32 * 32
            keep["xT"] = early.enter_context(nc.sbuf_tensor("xT", [P, KB, TOK], F32))
            keep["shared_base"] = (nc.sbuf_base + 31) // 32 * 32
            early.enter_context(nc.sbuf_tensor("beside_xT", [P, KB, TOK], F32))
            prepare(nc, io, keep, scr)
            project_in(nc, io, keep, scr)
        scan_states(nc, io, out, keep, scr)
        keep["ssm_hi"], keep["ssm_lo"] = sb("ssm_hi", [P, 8, TOK], F32R), sb("ssm_lo", [P, 8, TOK], F32R)
        gate_states(nc, io, keep, scr)
        keep["attn_hi"], keep["attn_lo"] = sb("attn_hi", [P, 8, TOK], F32R), sb("attn_lo", [P, 8, TOK], F32R)
        with nc.sbuf_tensor("kT", [P, KV_HEADS, TOK], F32) as kT:
            keep["kT"] = kT
            with nc.sbuf_tensor("v_nat", [P, SEQ // P, KV_HEADS * HD], F32) as v_nat:
                keep["v_nat"] = v_nat
                natural_keys(nc, io, out, keep, scr)
                attend_prompt(nc, io, keep, scr)
            attend_samples(nc, io, out, keep, scr)
        keep["gpost"] = sb("gpost", [P, D_MODEL // 2], F32R)
        keep["sel"] = nc.alloc_sbuf_tensor_at("sel", [P, ROWS + P], F32R, offset=mod_base)
        with nc.sbuf_tensor("sel_f", [P, ROWS + P], F32) as sel_f:
            keep["sel_f"] = sel_f
            gate_rows(nc, io, keep)
        project_out(nc, io, out, keep, scr)


def kernel(**inputs):
    import numpy as _np
    import concourse.bacc as _bacc
    from concourse.bass_utils import run_bass_kernel_spmd as _run

    nc = _bacc.Bacc("TRN2", target_bir_lowering=False, num_devices=1)
    arrays, io = {}, {}
    for name in _INS:
        a = _np.ascontiguousarray(inputs[name])
        arrays[f"in_{name}"] = a
        io[name] = nc.dram_tensor(f"in_{name}", a.shape, mybir.dt.from_np(a.dtype), kind="ExternalInput").ap()
    out = {name: nc.dram_tensor(f"out_{name}", list(shape), F32, kind="ExternalOutput").ap() for name, shape in _OUTS}
    hybrid_layer(nc, io, out)
    r = _run(nc, [arrays], core_ids=[0])
    return tuple(r.results[0][f"out_{name}"] for name, _ in _OUTS)
```

```python
from contextlib import ExitStack

import concourse.bass as bass
import concourse.mybir as mybir
from concourse.alu_op_type import AluOpType as ALU

ACT = mybir.ActivationFunctionType
AX_X = mybir.AxisListType.X
F32 = mybir.dt.float32
F32R = mybir.dt.float32r
BF16 = mybir.dt.bfloat16
I32 = mybir.dt.int32

P = 128
D_MODEL = 2048
KB = D_MODEL // P
SEQ = 1024
DEC_B, DEC_S, PAST = 8, 16, 256
TOK = SEQ + DEC_B * DEC_S
NT = TOK // P
TC, NTC = 384, 3
COND = 1 + DEC_B
CHUNK = 64
TOPK = 256
DEC_KEYS = PAST + DEC_S
DEC_TOPK = min(256, DEC_KEYS // 4)
HEADS, KV_HEADS, HD = 8, 2, 128
IDX_HEADS, IDX_DIM = 16, 64
GROUPS, CH, STATE = 64, 16, 64
PAIRS = GROUPS // 2
STEP = 8
NSTEP = TOK // STEP
PSTEP = SEQ // STEP
TAPS = 2 * STEP - 1
EPS = 1e-6
COLS = 5712
Q0, K0, V0, IQ0, IK0, IW0, ZA0, U0, ZS0 = 0, 1024, 1280, 1536, 2560, 2624, 2640, 3664, 4688
PAIR_BATCH = 4
BATCHES = PAIRS // PAIR_BATCH
HALF = KB // 2

PI = 3.141592653589793
LN2 = 0.6931471805599453
TWO_PI_PARTS = (6.28125, 0.0019350051879882812, 3.019916050561733e-07)
LN2_PARTS = (0.693359375, -0.00021219444005469057)
ROUND = 12582912.0


def bc(ap, axis, n):
    u = ap.unsqueeze(axis)
    shape = list(u.shape)
    shape[axis] = n
    return u.broadcast_to(shape)


def cleared_after(nc, ctx):
    signals = []

    def clear():
        nc.clear_and_free_semaphores(signals)
        nc.all_engine_barrier()

    ctx.callback(clear)
    return signals


def new_signal(nc, signals, name):
    signals.append(nc.alloc_semaphore(name=name))
    return signals[-1]


def after(eng, signal, count):
    if not isinstance(count, int) or count > 0:
        eng.wait_ge(signal, count)


def prepare(nc, io, keep, scr):
    cT = keep["cT"]
    xT, shared, ident, vecT, mod = keep["xT"], keep["shared_base"], keep["ident"], keep["vecT"], keep["mod"]
    with ExitStack() as ctx:
        signals = cleared_after(nc, ctx)

        def sb(name, shape, dt=F32):
            return ctx.enter_context(nc.sbuf_tensor(name, shape, dt))

        def sem(name):
            return new_signal(nc, signals, name)

        wada = [sb(f"wada{i}", [P, KB // 4, 4 * P]) for i in range(4)]
        xs = [sb(f"xs{i}", [P, D_MODEL]) for i in range(2)]
        offset = [shared]

        def at(name, shape, dt=F32):
            size = 4
            for s in shape[1:]:
                size *= s
            if dt == BF16:
                size //= 2
            t = nc.alloc_sbuf_tensor_at(name, shape, dt, offset=offset[0])
            offset[0] += (size + 31) // 32 * 32
            assert offset[0] <= shared + KB * TOK * 4
            return t

        crows = at("crows", [COND, D_MODEL])
        square = at("square", [P, D_MODEL], BF16)
        vrows = at("vrows", [72, P])
        lam_rows = at("lam_rows", [PAIRS, 3, P])
        dt_rows = at("dt_rows", [PAIRS, 2])
        bmat = at("bmat", [P, 2, PAIRS, CH])
        bbar = at("bbar", [P, 2, PAIRS, CH])
        cmat = at("cmat", [P, 2, PAIRS, CH])
        skip = at("skip", [CH, GROUPS, CH])
        lam = at("lam", [P, 3, PAIRS])
        tiny = at("tiny", [P, 24, PAIRS])
        ang = at("ang", [P, 8, 2, PAIRS])
        powr = at("powr", [P, 2, STEP + 1, PAIRS])
        prev = at("prev", [P, 2, STEP, PAIRS])
        wmat = at("wmat", [P, PAIR_BATCH, 2, STEP + 1, CH])
        wtmp = at("wtmp", [P, PAIR_BATCH, STEP + 1, CH])
        pmat = at("pmat", [P, PAIR_BATCH, 2, STEP, CH])
        ptmp = at("ptmp", [P, PAIR_BATCH, STEP, CH])
        bslot = at("bslot", [P, 2, PAIR_BATCH, CH])
        pout = at("pout", [P, PAIR_BATCH, 2, P])
        crow = [pout[:].rearrange("p j r q -> p (j r q)"), pmat[:].rearrange("p j r s c -> p (j r s c)")]
        crow = [v.rearrange("p (b g s) -> p b g s", b=8, g=2) for v in crow]
        taps = at("taps", [CH, 2 * PAIR_BATCH, TAPS, CH])
        add4 = sb("add4", [P, 32])
        mrows = sb("mrows", [P, 4 * P])
        stat = sb("stat", [P, 6, 2])

        ps_x = [ctx.enter_context(nc.psum_tensor(f"ps_x{i}", [P, 512], F32)) for i in range(2)]
        ps_ada = [ctx.enter_context(nc.psum_tensor(f"ps_ada{i}", [P, 512], F32)) for i in range(2)]
        ps_v = ctx.enter_context(nc.psum_tensor("ps_v", [P, 512], F32))
        ps_p = ctx.enter_context(nc.psum_tensor("ps_p", [P, 512], F32))
        ps_k = ctx.enter_context(nc.psum_tensor("ps_k", [P, 2, 512], F32))

        rows_in, s5_in, c_in = sem("rows_in"), sem("s5_in"), sem("c_in")
        ada_in = [sem(f"ada_in{i}") for i in range(4)]
        x_in = [sem(f"x_in{i}") for i in range(2)]
        ident_ok, c_copied = sem("ident_ok"), sem("c_copied")
        vec_T, vec_copied = sem("vec_T"), sem("vec_copied")
        squared, var_ok, root_ok, x_scaled = sem("squared"), sem("var_ok"), sem("root_ok"), sem("x_scaled")
        x_T, x_copied = sem("x_T"), [sem("x_copied0"), sem("x_copied1")]
        ada_ok, mrows_ok, mod_T, mod_kept = [sem(f"ada_ok{i}") for i in range(4)], sem("mrows_ok"), sem("mod_T"), sem("mod_kept")
        norm_step, s5_step, pool_step = sem("norm_step"), sem("s5_step"), sem("pool_step")
        lam_T, lam_copied, c_mat_T, c_mat_copied = sem("lam_T"), sem("lam_copied"), sem("c_mat_T"), sem("c_mat_copied")
        dt_ok, consts_ok = sem("dt_ok"), sem("consts_ok")
        w_ok, p_ok, p_T, p_copied, k_mm, k_copied = (sem(n) for n in ("w_ok", "p_ok", "p_T", "p_copied", "k_mm", "k_copied"))
        taps_ok, taps_out, p_out, q_out, tabs_out = sem("taps_ok"), sem("taps_out"), sem("p_out"), sem("q_out"), sem("tabs_out")
        skip_ok, bbar_ok, pow_ok = sem("skip_ok"), sem("bbar_ok"), sem("pow_ok")
        taps_zero, bslot_ok, w_step, passed = sem("taps_zero"), sem("bslot_ok"), sem("w_step"), sem("passed")

        block = ctx.enter_context(nc.Block())
        xp = io["x_prompt"].rearrange("b s d -> (b s) d")
        xd = io["x_sample"].rearrange("b s d -> (b s) d")
        w_ada = io["w_ada"][0].rearrange("(k p) n -> p k n", p=P)

        def turns(eng, body):
            for u in range(2):
                body(0, u)
            with eng.Fori(1, 3) as i:
                for u in range(2):
                    body(i, u)
            for u in range(2):
                body(3, u)

        def is_(i, n):
            return isinstance(i, int) and i == n

        @block.sync
        def _(sp):
            def load_ada(T):
                for v in range(4):
                    after(sp, ada_ok[v], T)
                    sp.dma_start(wada[v][:], w_ada[:, 4 * v:4 * v + 4, bass.ds(T * (4 * P), 4 * P)]).then_inc(ada_in[v], 16)

            sp.dma_start(crows[0:1, :], io["c_prompt"]).then_inc(rows_in, 16)
            sp.dma_start(crows[1:COND, :], io["c_sample"]).then_inc(rows_in, 16)
            sp.dma_start(vrows[0:48, :], io["b_ada"].rearrange("a (r c) -> (a r) c", c=P)).then_inc(rows_in, 16)
            sp.dma_start(vrows[48:64, :], io["g_pre"].rearrange("a (r c) -> (a r) c", c=P)).then_inc(rows_in, 16)
            sp.dma_start(vrows[64:72, :], io["b_glu"].rearrange("a (r c) -> (a r) c", c=P)).then_inc(rows_in, 16)
            sp.dma_start(xs[0][:], xd).then_inc(x_in[0], 16)
            sp.dma_start(xs[1][:], xp[0:P, :]).then_inc(x_in[1], 16)
            for i, name in enumerate(("lambda_re", "lambda_im")):
                sp.dma_start(lam_rows[:, i, :], io[name][0].rearrange("(j g) p -> j (g p)", g=2)).then_inc(s5_in, 16)
            sp.dma_start(dt_rows[:], io["log_dt"][0].rearrange("(j g) -> j g", g=2)).then_inc(s5_in, 16)
            for i, name in enumerate(("b_re", "b_im")):
                sp.dma_start(bmat[:, i], io[name][0].rearrange("(j g) p c -> (g p) j c", g=2)).then_inc(s5_in, 16)
            load_ada(0)
            for i, name in enumerate(("c_re", "c_im")):
                for g in range(2):
                    sp.dma_start(crow[i][:, :, g], io[name][0].rearrange("(b g) c p -> (g c) b p", g=8)).then_inc(c_in, 16)
            sp.dma_start(skip[:].rearrange("a g c -> a (g c)"), io["d_skip"].broadcast_to([CH, GROUPS * CH])).then_inc(c_in, 16)

            def body(i, u):
                t = i * 2 + u
                if not (is_(i, 3) and u == 1):
                    sp.wait_ge(x_T, t * 4 + 4)
                    sp.dma_start(xs[u][:], xp[bass.ds(t * P + P, P), :]).then_inc(x_in[u], 16)
                if not is_(i, 3):
                    load_ada(t + 2)

            load_ada(1)
            turns(sp, body)

        @block.gpsimd
        def _(pool):
            nc.gpsimd.memset(ident[:], 0.0).then_inc(pool_step, 1)
            pool.wait_ge(pool_step, 1)
            nc.gpsimd.affine_select(out=ident[:], in_=ident[:], compare_op=ALU.not_equal, fill=1.0, base=0,
                                    pattern=[[-1, P]], channel_multiplier=1).then_inc(ident_ok, 1)
            nc.gpsimd.memset(taps[:], 0.0).then_inc(taps_zero, 1)
            pool.wait_ge(bbar_ok, 2)
            pool.wait_ge(pow_ok, 1)
            pool.wait_ge(c_mat_T, 2)
            def inputs_of(b):
                js = bass.ds(b * PAIR_BATCH, PAIR_BATCH)
                pr = bc(prev[:, 0, :, js].rearrange("p s j -> p j s"), 3, CH)
                pi = bc(prev[:, 1, :, js].rearrange("p s j -> p j s"), 3, CH)
                after(pool, p_T, b * (2 * PAIR_BATCH))
                pool.sem_inc(passed, 1)
                for ri in range(2):
                    first, second = bc(bbar[:, ri, js, :], 2, STEP), bc(bbar[:, 1 - ri, js, :], 2, STEP)
                    nc.gpsimd.tensor_tensor(pmat[:, :, ri], pr, first, ALU.mult).then_inc(pool_step, 1)
                    nc.gpsimd.tensor_tensor(ptmp[:], pi, second, ALU.mult).then_inc(pool_step, 1)
                    pool.wait_ge(pool_step, b * 4 + 2 * ri + 3)
                    nc.gpsimd.tensor_tensor(pmat[:, :, ri], pmat[:, :, ri], ptmp[:],
                                            ALU.add if ri else ALU.subtract).then_inc(p_ok, 1)
                    pool.wait_ge(p_ok, b * 2 + ri + 1)
                    pool.sem_inc(passed, 1)

            inputs_of(0)
            with pool.Fori(1, BATCHES) as b:
                inputs_of(b)

        @block.scalar
        def _(act):
            def root_of_mean(slot, landed, n):
                act.wait_ge(x_in[slot], landed)
                nc.scalar.activation(square[:], xs[slot][:], ACT.Square, accum_out=stat[:, 0, slot:slot + 1]).then_inc(squared, 1)
                act.wait_ge(var_ok, n)
                nc.scalar.activation(stat[:, 2, slot:slot + 1], stat[:, 1, slot:slot + 1], ACT.Sqrt).then_inc(root_ok, 1)

            def copy_rows(u, T):
                act.wait_ge(ada_ok[3], T + 1)
                after(act, mod_T, T)
                act.sem_inc(passed, 1)
                nc.scalar.activation(mrows[:], ps_ada[u][:], ACT.Copy).then_inc(mrows_ok, 1)

            def store_taps(b):
                act.wait_ge(taps_ok, b + 1)
                act.dma_start(scr["taps"][bass.ds(b * (2 * PAIR_BATCH), 2 * PAIR_BATCH)].rearrange("g c t -> c g t"),
                              taps[:].rearrange("c g t o -> c g (t o)")).then_inc(taps_out, 16)

            def body(i, u):
                b = i * 2 + u
                last = is_(i, 3)
                if not (last and u == 1):
                    root_of_mean(u, i * 16 + 32, b + 3)
                if not last:
                    copy_rows(u, b + 2)
                js = bass.ds(b * PAIR_BATCH, PAIR_BATCH)
                for h in range(2):
                    if h == 0:
                        after(act, p_out, b * 16)
                    act.wait_ge(p_T, b * 8 + 4 * h + 4)
                    nc.scalar.activation(pout[:, 2 * h:2 * h + 2].rearrange("p j r q -> p (j r q)"), ps_p[:],
                                         ACT.Copy).then_inc(p_copied, 1)
                act.wait_ge(p_copied, b * 2 + 2)
                act.dma_start(scr["s5_in"][:, js], pout[:]).then_inc(p_out, 16)
                if not (is_(i, 0) and u == 0):
                    store_taps(b - 1)
                act.wait_ge(w_ok, b + 1)
                act.dma_start(scr["s5_out"][:, js],
                              wmat[:, :, :, 1:].rearrange("p j r t c -> p j r (t c)")).then_inc(q_out, 16)
                after(act, taps_out, b * 16)
                act.sem_inc(passed, 1)
                act.wait_ge(k_mm, b + 1)
                nc.scalar.activation(taps[:, :, STEP - 1:, :].rearrange("c (j a) t o -> c a j (t o)", a=2),
                                     ps_k[0:CH].rearrange("p a (j n) -> p a j n", j=4), ACT.Copy).then_inc(k_copied, 1)

            root_of_mean(0, 16, 1)
            root_of_mean(1, 16, 2)
            copy_rows(0, 0)
            copy_rows(1, 1)
            act.wait_ge(taps_zero, 1)
            turns(act, body)
            store_taps(7)
            act.wait_ge(taps_out, 16 * BATCHES)
            act.wait_ge(p_out, 16 * BATCHES)
            act.wait_ge(q_out, 16 * BATCHES)

        @block.vector
        def _(dve):
            count = [0]

            def step(ins):
                count[0] += 1
                ins.then_inc(s5_step, 1)
                dve.wait_ge(s5_step, count[0])

            V = nc.vector
            V.memset(cT[:], 0.0).then_inc(c_copied, 1)
            dve.wait_ge(c_copied, 1)
            dve.wait_ge(ident_ok, 1)
            V.tensor_reduce(add4[:], ident[:].rearrange("p (a c) -> p c a", a=4), AX_X, ALU.add).then_inc(c_copied, 1)
            dve.wait_ge(vec_T, 1)
            V.tensor_copy(cT[:, :, 0:COND], ps_v[:, 0:KB * COND].rearrange("p (k c) -> p k c", c=COND)).then_inc(c_copied, 1)
            V.tensor_copy(vecT[:], ps_v[:, 256:256 + 72]).then_inc(vec_copied, 1)

            def normalise(slot, n):
                s = lambda r: stat[:, r, slot:slot + 1]
                dve.wait_ge(squared, n + 1)
                V.tensor_scalar(s(1), s(0), 1.0 / D_MODEL, EPS, ALU.mult, ALU.add).then_inc(var_ok, 1)
                dve.wait_ge(root_ok, n + 1)
                V.reciprocal(s(3), s(2)).then_inc(norm_step, 1)
                dve.wait_ge(norm_step, n * 5 + 1)
                V.tensor_tensor(s(4), s(3), s(3), ALU.mult).then_inc(norm_step, 1)
                dve.wait_ge(norm_step, n * 5 + 2)
                V.tensor_tensor(s(4), s(4), s(1), ALU.mult).then_inc(norm_step, 1)
                dve.wait_ge(norm_step, n * 5 + 3)
                V.tensor_scalar(s(4), s(4), -0.5, 1.5, ALU.mult, ALU.add).then_inc(norm_step, 1)
                dve.wait_ge(norm_step, n * 5 + 4)
                V.tensor_tensor(s(5), s(3), s(4), ALU.mult).then_inc(norm_step, 1)
                dve.wait_ge(norm_step, n * 5 + 5)
                V.tensor_scalar(xs[slot][:], xs[slot][:], s(5), None, ALU.mult).then_inc(x_scaled, 1)

            def copy_x(column, n):
                for g in range(4):
                    dve.wait_ge(x_T, n * 4 + g + 1)
                    dve.sem_inc(passed, 1)
                    V.tensor_copy(xT[:, 4 * g:4 * g + 4, bass.ds(column, P)],
                                  ps_x[g % 2][:].rearrange("p (k t) -> p k t", k=4)).then_inc(x_copied[g % 2], 1)

            normalise(0, 0)
            copy_x(SEQ, 0)
            normalise(1, 1)

            def exp_of(out, x, k, r, acc):
                step(V.tensor_scalar(k, x, 1.0 / LN2, -126.0, ALU.mult, ALU.max))
                step(V.tensor_scalar(k, k, 127.0, ROUND, ALU.min, ALU.add))
                step(V.tensor_scalar(k, k, -ROUND, None, ALU.add))
                step(V.scalar_tensor_tensor(r, k, -LN2_PARTS[0], x, ALU.mult, ALU.add))
                step(V.scalar_tensor_tensor(r, k, -LN2_PARTS[1], r, ALU.mult, ALU.add))
                step(V.tensor_scalar(r, r, -1.0, 1.0, ALU.max, ALU.min))
                step(V.tensor_scalar(acc, r, 1.0 / 5040, 1.0 / 720, ALU.mult, ALU.add))
                for c in (1.0 / 120, 1.0 / 24, 1.0 / 6, 0.5, 1.0, 1.0):
                    step(V.tensor_tensor(acc, acc, r, ALU.mult))
                    step(V.tensor_scalar(acc, acc, c, None, ALU.add))
                step(V.tensor_scalar(k, k, 127.0, 8388608.0, ALU.add, ALU.mult))
                step(V.tensor_copy(r.bitcast(I32), k))
                step(V.tensor_tensor(out, acc, r, ALU.mult))

            def sincos(cos, sin, y, k, z, zz):
                step(V.tensor_scalar(k, y, 0.5 / PI, ROUND, ALU.mult, ALU.add))
                step(V.tensor_scalar(k, k, -ROUND, None, ALU.add))
                step(V.scalar_tensor_tensor(z, k, -TWO_PI_PARTS[0], y, ALU.mult, ALU.add))
                step(V.scalar_tensor_tensor(z, k, -TWO_PI_PARTS[1], z, ALU.mult, ALU.add))
                step(V.scalar_tensor_tensor(z, k, -TWO_PI_PARTS[2], z, ALU.mult, ALU.add))
                step(V.tensor_scalar(z, z, 0.25, None, ALU.mult))
                step(V.tensor_tensor(zz, z, z, ALU.mult))
                step(V.tensor_scalar(sin, zz, 1.0 / 362880, -1.0 / 5040, ALU.mult, ALU.add))
                for c in (1.0 / 120, -1.0 / 6, 1.0):
                    step(V.tensor_tensor(sin, sin, zz, ALU.mult))
                    step(V.tensor_scalar(sin, sin, c, None, ALU.add))
                step(V.tensor_tensor(sin, sin, z, ALU.mult))
                step(V.tensor_scalar(cos, zz, -1.0 / 3628800, 1.0 / 40320, ALU.mult, ALU.add))
                for c in (-1.0 / 720, 1.0 / 24, -0.5, 1.0):
                    step(V.tensor_tensor(cos, cos, zz, ALU.mult))
                    step(V.tensor_scalar(cos, cos, c, None, ALU.add))
                for _ in range(2):
                    step(V.tensor_tensor(k, sin, sin, ALU.mult))
                    step(V.tensor_tensor(z, sin, cos, ALU.mult))
                    step(V.tensor_scalar(cos, k, -2.0, 1.0, ALU.mult, ALU.add))
                    step(V.tensor_scalar(sin, z, 2.0, None, ALU.mult))

            dve.wait_ge(s5_in, 16 * 5)
            V.tensor_copy(lam_rows[:, 2, :].rearrange("j (g p) -> j g p", g=2), bc(dt_rows[:], 2, STATE)).then_inc(dt_ok, 1)
            dve.wait_ge(lam_T, 3)
            step(V.tensor_copy(lam[:], ps_v[:, 384:384 + 96].rearrange("p (a j) -> p a j", a=3)))
            T = lambda i: tiny[:, i]
            A = lambda i: ang[:, i]
            exp_of(T(0), lam[:, 2], T(1), T(2), T(3))
            step(V.tensor_tensor(A(0)[:, 0], lam[:, 0], T(0), ALU.mult))
            step(V.tensor_tensor(A(1)[:, 0], lam[:, 1], T(0), ALU.mult))
            step(V.tensor_scalar(A(0)[:, 1], A(0)[:, 0], float(STEP), None, ALU.mult))
            step(V.tensor_scalar(A(1)[:, 1], A(1)[:, 0], float(STEP), None, ALU.mult))
            exp_of(A(2), A(0), A(3), A(4), A(5))
            sincos(A(3), A(4), A(1), A(5), A(6), A(7))
            step(V.memset(powr[:, 0, 0], 1.0))
            step(V.memset(powr[:, 1, 0], 0.0))
            step(V.tensor_tensor(powr[:, 0, 1], A(2)[:, 0], A(3)[:, 0], ALU.mult))
            step(V.tensor_tensor(powr[:, 1, 1], A(2)[:, 0], A(4)[:, 0], ALU.mult))
            for a, b in ((1, 1), (2, 1), (2, 2), (3, 2), (3, 3), (4, 3), (4, 4)):
                n = a + b
                step(V.tensor_tensor(T(4), powr[:, 0, a], powr[:, 0, b], ALU.mult))
                step(V.tensor_tensor(T(5), powr[:, 1, a], powr[:, 1, b], ALU.mult))
                step(V.tensor_tensor(powr[:, 0, n], T(4), T(5), ALU.subtract))
                step(V.tensor_tensor(T(4), powr[:, 0, a], powr[:, 1, b], ALU.mult))
                step(V.tensor_tensor(T(5), powr[:, 1, a], powr[:, 0, b], ALU.mult))
                step(V.tensor_tensor(powr[:, 1, n], T(4), T(5), ALU.add))
            for s in range(STEP):
                ins = V.tensor_copy(prev[:, :, s], powr[:, :, STEP - 1 - s])
            ins.then_inc(pow_ok, 1)
            step(V.tensor_tensor(T(6), lam[:, 0], lam[:, 0], ALU.mult))
            step(V.tensor_tensor(T(7), lam[:, 1], lam[:, 1], ALU.mult))
            step(V.tensor_tensor(T(6), T(6), T(7), ALU.add))
            step(V.reciprocal(T(6), T(6)))
            step(V.tensor_scalar(T(7), powr[:, 0, 1], -1.0, None, ALU.add))
            step(V.tensor_tensor(T(8), T(7), lam[:, 0], ALU.mult))
            step(V.tensor_tensor(T(9), powr[:, 1, 1], lam[:, 1], ALU.mult))
            step(V.tensor_tensor(T(8), T(8), T(9), ALU.add))
            step(V.tensor_tensor(T(8), T(8), T(6), ALU.mult))
            step(V.tensor_tensor(T(9), powr[:, 1, 1], lam[:, 0], ALU.mult))
            step(V.tensor_tensor(T(10), T(7), lam[:, 1], ALU.mult))
            step(V.tensor_tensor(T(9), T(9), T(10), ALU.subtract))
            step(V.tensor_tensor(T(9), T(9), T(6), ALU.mult))
            fr, fi = bc(T(8), 2, CH), bc(T(9), 2, CH)
            w0 = wmat[:].rearrange("p a b c d -> p (a b c d)")[:, 0:512].rearrange("p (j c) -> p j c", j=PAIRS)
            step(V.tensor_tensor(bbar[:, 0], fr, bmat[:, 0], ALU.mult))
            step(V.tensor_tensor(w0, fi, bmat[:, 1], ALU.mult))
            V.tensor_tensor(bbar[:, 0], bbar[:, 0], w0, ALU.subtract).then_inc(bbar_ok, 1)
            dve.wait_ge(bbar_ok, 1)
            step(V.tensor_tensor(bbar[:, 1], fr, bmat[:, 1], ALU.mult))
            step(V.tensor_tensor(w0, fi, bmat[:, 0], ALU.mult))
            V.tensor_tensor(bbar[:, 1], bbar[:, 1], w0, ALU.add).then_inc(bbar_ok, 1)
            for ri in range(2):
                dve.wait_ge(c_mat_T, ri + 1)
                for g in range(2):
                    src = ps_k[64 * g:64 * g + 64].rearrange("p a (j n) -> p (a j) n", n=2 * CH)[:, :, CH * g:CH * g + CH]
                    step(V.tensor_copy(cmat[64 * g:64 * g + 64, ri], src))
                dve.sem_inc(c_mat_copied, 1)
            dve.wait_ge(ident_ok, 1)
            V.tensor_tensor(skip[:], skip[:], bc(ident[0:CH, 0:CH], 1, GROUPS), ALU.mult).then_inc(skip_ok, 1)
            tabs = keep["s5_tabs"]
            step(V.tensor_copy(tabs[:, 0], A(2)[:, 1]))
            step(V.tensor_copy(tabs[:, 1], A(3)[:, 1]))
            step(V.tensor_copy(tabs[:, 2], A(4)[:, 1]))
            step(V.tensor_copy(tabs[:, 3], powr[:, 0, STEP]))
            step(V.tensor_copy(tabs[:, 4], powr[:, 1, STEP]))

            def s5_build(b):
                js = bass.ds(b * PAIR_BATCH, PAIR_BATCH)
                pr = bc(powr[:, 0, :, js].rearrange("p s j -> p j s"), 3, CH)
                pi = bc(powr[:, 1, :, js].rearrange("p s j -> p j s"), 3, CH)
                cr, ci = bc(cmat[:, 0, js], 2, STEP + 1), bc(cmat[:, 1, js], 2, STEP + 1)
                flat = lambda t: t.rearrange("p j t c -> p j (t c)")
                after(dve, k_mm, b)
                dve.sem_inc(passed, 1)
                V.tensor_copy(bslot[:], bbar[:, :, js, :]).then_inc(bslot_ok, 1)
                after(dve, q_out, b * 16)
                V.tensor_tensor(wmat[:, :, 0], pr, cr, ALU.mult).then_inc(w_step, 1)
                V.tensor_tensor(wtmp[:], pi, ci, ALU.mult).then_inc(w_step, 1)
                V.tensor_tensor(wmat[:, :, 1], pi, cr, ALU.mult).then_inc(w_step, 1)
                dve.wait_ge(w_step, b * 5 + 3)
                V.tensor_tensor(wmat[:, :, 0], wmat[:, :, 0], wtmp[:], ALU.subtract).then_inc(w_step, 1)
                dve.wait_ge(w_step, b * 5 + 4)
                V.tensor_tensor(wtmp[:], pr, ci, ALU.mult).then_inc(w_step, 1)
                dve.wait_ge(w_step, b * 5 + 5)
                V.scalar_tensor_tensor(flat(wmat[:, :, 1]), flat(wmat[:, :, 1]), -1.0, flat(wtmp[:]),
                                       ALU.mult, ALU.subtract).then_inc(w_ok, 1)

            def s5_skip(b):
                dve.wait_ge(k_copied, b + 1)
                V.tensor_tensor(taps[:, :, STEP - 1], taps[:, :, STEP - 1],
                                skip[:, bass.ds(b * (2 * PAIR_BATCH), 2 * PAIR_BATCH)], ALU.add).then_inc(taps_ok, 1)

            def keep_modulation(u, T):
                dve.wait_ge(mod_T, T + 1)
                dve.sem_inc(passed, 1)
                V.tensor_tensor(mod[:, bass.ds(T * 4, 4), :], ps_ada[u][:, 0:4 * COND].rearrange("p (b c) -> p b c", b=4),
                                vecT[:, bass.ds(T * 4, 4)].unsqueeze(2).broadcast_to([P, 4, COND]), ALU.add).then_inc(mod_kept, 1)

            keep_modulation(0, 0)
            keep_modulation(1, 1)

            def body(i, u):
                t = i * 2 + u
                copy_x(t * P, t + 1)
                if not (is_(i, 3) and u == 1):
                    normalise(u, t + 2)
                if not (is_(i, 0) and u == 0):
                    s5_skip(t - 1)
                s5_build(t)
                if not is_(i, 3):
                    keep_modulation(u, t + 2)

            turns(dve, body)
            s5_skip(7)
            sc = mod[:, KB:2 * KB]
            dve.wait_ge(mod_kept, KB // 2)
            step(V.tensor_scalar(sc, sc, 1.0, None, ALU.add))
            step(V.tensor_tensor(sc, sc, bc(vecT[:, 48:64], 2, COND), ALU.mult))

        @block.tensor
        def _(pe):
            M, TR = nc.tensor.matmul, nc.tensor.transpose
            pe.wait_ge(ident_ok, 1)
            pe.wait_ge(rows_in, 80)
            for k in range(KB):
                ins = TR(ps_v[:, COND * k:COND * k + COND], crows[:, k * P:k * P + P], ident[0:COND, 0:COND])
            TR(ps_v[:, 256:256 + 72], vrows[:], ident[0:72, 0:72]).then_inc(vec_T, 1)

            def turn_x(slot, n):
                pe.wait_ge(x_scaled, n + 1)
                for g in range(4):
                    after(pe, x_copied[g % 2], n * 2 + g // 2)
                    for k in range(4 * g, 4 * g + 4):
                        ins = TR(ps_x[g % 2][:, (k % 4) * P:(k % 4) * P + P], xs[slot][:, k * P:k * P + P], ident[:])
                    ins.then_inc(x_T, 1)

            def turn_s5_rows():
                pe.wait_ge(dt_ok, 1)
                pe.wait_ge(vec_copied, 1)
                pe.wait_ge(c_copied, 3)
                for a in range(3):
                    TR(ps_v[:, 384 + 32 * a:416 + 32 * a], lam_rows[:, a, :], ident[0:PAIRS, 0:PAIRS]).then_inc(lam_T, 1)

            def turn_c():
                pe.wait_ge(c_in, 16 * 5)
                for ri in range(2):
                    if ri:
                        pe.wait_ge(c_mat_copied, 1)
                    for b in range(8):
                        ins = TR(ps_k[:, b // 4, b % 4 * P:b % 4 * P + P], crow[ri][:, b].rearrange("r g p -> r (g p)"), ident[:])
                    ins.then_inc(c_mat_T, 1)

            def s5_inputs(b):
                pe.wait_ge(p_ok, b * 2 + 2)
                for h in range(2):
                    after(pe, p_copied, b * 2 + h)
                    for q in range(4):
                        j, ri = 2 * h + q // 2, q % 2
                        TR(ps_p[:, q * P:q * P + P], pmat[:, j, ri].rearrange("p s c -> p (s c)"), ident[:]).then_inc(p_T, 1)

            def s5_taps(b):
                pe.wait_ge(w_ok, b + 1)
                pe.sem_inc(passed, 1)
                pe.wait_ge(bslot_ok, b + 1)
                pe.sem_inc(passed, 1)
                after(pe, k_copied, b)
                pe.sem_inc(passed, 1)
                for g in range(2 * PAIR_BATCH):
                    j, half = g // 2, slice(64 * (g % 2), 64 * (g % 2) + 64)
                    for ri in range(2):
                        ins = M(ps_k[0:CH, g % 2, j * P:j * P + P], bslot[half, ri, j, :],
                                wmat[half, j, ri, 0:STEP].rearrange("p t c -> p (t c)"), start=ri == 0, stop=ri == 1)
                ins.then_inc(k_mm, 1)

            def modulate(u, T):
                after(pe, mod_kept, T - 1)
                for k in range(4):
                    for v in range(4):
                        if k == 0:
                            pe.wait_ge(ada_in[v], T * 16 + 16)
                        ins = M(ps_ada[u][32 * v:32 * v + 32, :], cT[:, 4 * v + k, :], wada[v][:, k, :], start=k == 0, stop=k == 3)
                        if k == 3:
                            ins.then_inc(ada_ok[v], 1)

            def turn_modulation(u, T):
                pe.wait_ge(mrows_ok, T + 1)
                pe.sem_inc(passed, 1)
                for c in range(4):
                    ins = M(ps_ada[u][:, COND * c:COND * c + COND], mrows[:, P * c:P * c + P], add4[:, 0:COND], start=True, stop=True)
                ins.then_inc(mod_T, 1)

            def body(i, u):
                t = i * 2 + u
                turn_x((u + 1) % 2, t + 1)
                if not is_(i, 3):
                    modulate(u, t + 2)
                s5_inputs(t)
                if not is_(i, 3):
                    turn_modulation(u, t + 2)
                s5_taps(t)

            turn_x(0, 0)
            pe.wait_ge(c_copied, 3)
            turn_s5_rows()
            modulate(0, 0)
            turn_modulation(0, 0)
            modulate(1, 1)
            turn_modulation(1, 1)
            turn_c()
            turns(pe, body)
CHOSEN, UNSEEN, MASKED = -3.4e38, -3.0e38, -1.0e30
SLICES = [(c, TC) for c in range(0, TOK, TC)]

SEGMENTS = [
    (Q0, 4, False, None), (Q0 + 512, 8, False, 7), (U0, 5, True, 6), (U0 + 640, 5, True, 5),
    (U0 + 1280, 6, True, 4), (ZA0, 4, False, 3), (ZA0 + 512, 4, False, 2),
]


GATE_COLS = 64


def project_in(nc, io, keep, scr):
    cT = keep["cT"]
    ident, mod, xT, maskb = keep["ident"], keep["mod"], keep["xT"], keep["maskb"]
    with ExitStack() as ctx:
        signals = cleared_after(nc, ctx)

        def sb(name, shape, dt=F32):
            return ctx.enter_context(nc.sbuf_tensor(name, shape, dt))

        def sem(name):
            return new_signal(nc, signals, name)

        h_hi = nc.alloc_sbuf_tensor_at("h_hi", [P, KB, TOK], F32R, offset=keep["shared_base"])
        h_lo = nc.alloc_sbuf_tensor_at("h_lo", [P, KB, TOK], F32R, offset=keep["xT_base"])
        w_raw = sb("w_raw", [P, 2, HALF, P])
        w_hi = sb("w_hi", [P, 2, HALF, P], F32R)
        w_lo = sb("w_lo", [P, 2, HALF, P], F32R)
        z_sb = sb("z_sb", [P, TOK])
        iqT = sb("iqT", [P, IDX_HEADS // 2, P])
        ikT = sb("ikT", [P, SEQ])
        rel = sb("rel", [P, 2, 512])
        score = sb("score", [P, SEQ])
        iw = sb("iw", [P, SEQ // P, IDX_HEADS])
        top8 = sb("top8", [P, 8])
        wg = sb("wg", [P, KB, GATE_COLS])
        g_rows = sb("g_rows", [P, GATE_COLS])
        ps_z = [ctx.enter_context(nc.psum_tensor(f"ps_z{i}", [P, 512], F32)) for i in range(NTC)]
        ps_s = [ctx.enter_context(nc.psum_tensor(f"ps_s{i}", [P, 512], F32)) for i in range(4)]
        ps_w = ctx.enter_context(nc.psum_tensor("ps_w", [P, 512], F32))

        affine_ok, affine_s_ok, hi_ok, lo_ok = [sem("affine_ok0"), sem("affine_ok1")], sem("affine_s_ok"), sem("hi_ok"), sem("lo_ok")
        affine_s_step = sem("affine_s_step")
        w_in = [sem("w_in0"), sem("w_in1")]
        w_hi_ok, w_lo_ok, w_used = [sem("w_hi0"), sem("w_hi1")], [sem("w_lo0"), sem("w_lo1")], sem("w_used")
        z_done, z_out = sem("z_done"), sem("z_out")
        z_read = [sem(f"z_read{i}") for i in range(NTC)]
        idx_in, iq_in, iw_T, iw_ok = sem("idx_in"), sem("iq_in"), sem("iw_T"), sem("iw_ok")
        s_mm, s_relu, s_acc, unseen_ok = sem("s_mm"), sem("s_relu"), sem("s_acc"), sem("unseen_ok")
        top, mask_ok, passed = sem("top"), sem("mask_ok"), sem("passed_b")
        g_dma, g_mm, g_copied = sem("gate_dma"), sem("gate_mm_b"), sem("gate_copied")

        wv = io["w_in"][0].rearrange("(k p) n -> p k n", p=P)
        zt = scr["zt"]
        IDX_TILES = [s[3] for s in SEGMENTS if s[3] is not None]

        def width(tile):
            keys = (tile + 1) * P
            return keys, keys if keys <= 512 else keys // 2

        def units(tile):
            keys, w = width(tile)
            return [(hp, h2, c, w) for hp in range(IDX_HEADS // 2) for c in range(0, keys, w) for h2 in range(2)]

        first_unit = {}
        total = 0
        for t in IDX_TILES:
            first_unit[t] = total
            total += len(units(t))
        base_of = []
        g = 9
        for c0, n, perm, tile in SEGMENTS:
            base_of.append(g)
            g += n
        LAST = g - 1
        GATE_UNITS = D_MODEL // GATE_COLS
        assert base_of[-1] - base_of[0] == GATE_UNITS
        gate_cols = lambda U: U * (-GATE_COLS) + (3 * D_MODEL - GATE_COLS)

        block = ctx.enter_context(nc.Block())

        @block.sync
        def _(sp):
            def load(G, col, m=P):
                for h in range(2):
                    sp.wait_ge(w_lo_ok[h], G)
                    sp.dma_start(w_raw[:, h, :, 0:m], wv[:, HALF * h:HALF * h + HALF, bass.ds(col, m)]).then_inc(w_in[h], 16)

            def load_queries(tile):
                sp.dma_start(iqT[:], zt[IQ0:IQ0 + 1024, tile * P:tile * P + P].rearrange("(a q) t -> q a t", q=P)).then_inc(iq_in, 16)

            load(0, IQ0)
            with sp.Fori(1, 8) as i:
                load(i, i * P + IQ0)
            load(8, IK0, 80)
            for (c0, n, perm, tile), g0 in zip(SEGMENTS, base_of):
                if tile is not None:
                    if tile == IDX_TILES[0]:
                        sp.wait_ge(z_out, 16 * 9)
                        for half in range(2):
                            sp.dma_start(ikT[64 * half:64 * half + 64, :], zt[IK0:IK0 + IDX_DIM, 0:SEQ]).then_inc(idx_in, 16)
                        sp.dma_start(score[0:IDX_HEADS, :], zt[IW0:IW0 + IDX_HEADS, 0:SEQ]).then_inc(idx_in, 16)
                    else:
                        sp.wait_ge(s_mm, first_unit[tile])
                    load_queries(tile)
                with sp.Fori(0, n) as i:
                    load(i + g0, i * P + c0)

        @block.scalar
        def _(act):
            def high(h, G, m=P):
                act.wait_ge(w_in[h], (G + 1) * 16)
                if h == 0:
                    act.wait_ge(w_used, G)
                else:
                    act.wait_ge(z_done, G * NTC)
                nc.scalar.activation(w_hi[:, h, :, 0:m], w_raw[:, h, :, 0:m], ACT.Copy).then_inc(w_hi_ok[h], 1)

            def store(G, col, m, perm):
                for i, (c, n) in enumerate(SLICES):
                    if i == 0:
                        act.wait_ge(z_out, G * 16)
                    act.wait_ge(z_done, G * NTC + i + 1)
                    if perm:
                        out = z_sb[0:m, :].rearrange("p (s n) -> p n s", s=STEP)[:, c // STEP:(c + n) // STEP, :]
                        src = ps_z[i][0:m, 0:n].rearrange("p (n s) -> p n s", s=STEP)
                    else:
                        out, src = z_sb[0:m, c:c + n], ps_z[i][0:m, 0:n]
                    nc.scalar.activation(out, src, ACT.Copy).then_inc(z_read[i], 1)
                act.wait_ge(z_read[NTC - 1], G + 1)
                act.dma_start(zt[bass.ds(col, m), :], z_sb[0:m, :]).then_inc(z_out, 16)

            def block_(G, col, perm, m=P, next_m=P):
                high(1, G, m)
                if next_m:
                    high(0, G + 1, next_m)
                store(G, col, m, perm)

            def load_gate(U):
                act.dma_start(wg[:], io["w_ada"][0].rearrange("(k p) n -> p k n", p=P)[:, :, bass.ds(gate_cols(U), GATE_COLS)]).then_inc(g_dma, 16)

            def gate_unit(U):
                act.wait_ge(g_mm, U + 1)
                act.sem_inc(passed, 1)
                nc.scalar.activation(g_rows[:], ps_w[:, 0:GATE_COLS], ACT.Copy).then_inc(g_copied, 1)
                load_gate(U + 1)
                act.wait_ge(g_copied, U + 1)
                act.dma_start(scr["gate_dram"][:, bass.ds(gate_cols(U) - 2 * D_MODEL, GATE_COLS)], g_rows[:]).then_inc(g_dma, 16)

            def relus(tile):
                for u, (hp, h2, c, w) in enumerate(units(tile), first_unit[tile]):
                    act.wait_ge(s_mm, u + 1)
                    if u >= 2:
                        act.wait_ge(s_acc, u - 1)
                    nc.scalar.activation(rel[:, u % 2, 0:w], ps_s[u % 4][:, 0:w], ACT.Relu).then_inc(s_relu, 1)

            high(0, 0)
            high(1, 0)
            def affine_odd(k):
                nc.scalar.activation(xT[:, k, 0:SEQ], xT[:, k, 0:SEQ], ACT.Identity, bias=mod[:, k, 0:1],
                                     scale=mod[:, KB + k, 0:1]).then_inc(affine_ok[1], 1)

            affine_odd(1)
            for k in range(KB):
                if k % 2 == 0 and 0 < k:
                    affine_odd(k + 1)
                act.wait_ge(affine_ok[k % 2], k // 2 + 1)
                act.wait_ge(affine_s_ok, k + 1)
                nc.scalar.activation(h_hi[:, k], xT[:, k], ACT.Copy).then_inc(hi_ok, 1)
            high(0, 1)
            store(0, IQ0, P, False)
            with act.Fori(1, 7) as i:
                block_(i, i * P + IQ0, False)
            block_(7, IQ0 + 7 * P, False, P, 80)
            load_gate(0)
            block_(8, IK0, False, 80, P)
            for (c0, n, perm, tile), g0 in zip(SEGMENTS, base_of):
                if tile is not None:
                    relus(tile)
                last = g0 + n - 1 == LAST
                with act.Fori(0, n - 1 if last else n) as i:
                    block_(i + g0, i * P + c0, perm)
                    if not last:
                        gate_unit(i + (g0 - base_of[0]))
                if last:
                    block_(LAST, c0 + P * (n - 1), perm, P, 0)
            act.wait_ge(z_out, 16 * (LAST + 1))
            act.wait_ge(g_dma, 16 + 32 * GATE_UNITS)

        @block.gpsimd
        def _(pool):
            for k in range(KB):
                s = xT[:, k, SEQ:TOK].rearrange("p (b t) -> p b t", b=DEC_B)
                nc.gpsimd.tensor_tensor(s, s, bc(mod[:, KB + k, 1:COND], 2, DEC_S), ALU.mult).then_inc(affine_s_step, 1)
                pool.wait_ge(affine_s_step, k + 1)
                nc.gpsimd.tensor_tensor(s, s, bc(mod[:, k, 1:COND], 2, DEC_S), ALU.add).then_inc(affine_s_ok, 1)

        @block.vector
        def _(dve):
            V = nc.vector

            def low(h, G, m=P):
                dve.wait_ge(w_hi_ok[h], G + 1)
                V.tensor_tensor(w_lo[:, h, :, 0:m], w_raw[:, h, :, 0:m], w_hi[:, h, :, 0:m].bitcast(F32),
                                ALU.subtract).then_inc(w_lo_ok[h], 1)

            def affine_even(k):
                V.tensor_scalar(xT[:, k, 0:SEQ], xT[:, k, 0:SEQ], mod[:, KB + k, 0:1], mod[:, k, 0:1],
                                ALU.mult, ALU.add).then_inc(affine_ok[0], 1)

            def h_low(k):
                dve.wait_ge(hi_ok, k + 1)
                V.tensor_tensor(h_lo[:, k], xT[:, k], h_hi[:, k].bitcast(F32), ALU.subtract).then_inc(lo_ok, 1)

            def add_scores(tile):
                keys, w_ = width(tile)
                pieces = keys // w_
                if tile != IDX_TILES[0]:
                    dve.wait_ge(mask_ok, 2 + IDX_TILES.index(tile))
                for u, (hp, h2, c, w) in enumerate(units(tile), first_unit[tile]):
                    dve.wait_ge(s_relu, u + 1)
                    wgt = iw[:, tile, 2 * hp + h2:2 * hp + h2 + 1]
                    if hp == 0 and h2 == 0:
                        V.tensor_scalar(score[:, c:c + w], rel[:, u % 2, 0:w], wgt, None, ALU.mult).then_inc(s_acc, 1)
                    else:
                        dve.wait_ge(s_acc, u if h2 else u + 1 - (2 * pieces - 1))
                        V.scalar_tensor_tensor(score[:, c:c + w], rel[:, u % 2, 0:w], wgt, score[:, c:c + w],
                                               ALU.mult, ALU.add).then_inc(s_acc, 1)
                dve.wait_ge(s_acc, first_unit[tile] + len(units(tile)))
                V.memset(score[0:64, keys - CHUNK:keys], UNSEEN).then_inc(unseen_ok, 1)
                dve.wait_ge(unseen_ok, IDX_TILES.index(tile) + 1)

            def rounds(tile, at, n):
                keys = width(tile)[0]
                for r in range(n):
                    dve.wait_ge(top, at + 2 * r)
                    dve.sem_inc(passed, 1)
                    V.max(top8[:], score[:, 0:keys]).then_inc(top, 1)
                    dve.wait_ge(top, at + 2 * r + 1)
                    dve.sem_inc(passed, 1)
                    V.match_replace(score[:, 0:keys], top8[:], score[:, 0:keys], CHOSEN).then_inc(top, 1)

            def block_(G, tile, at, m=P, next_m=P):
                low(1, G, m)
                if tile is not None:
                    rounds(tile, at, 4)
                if next_m:
                    low(0, G + 1, next_m)
                if tile is not None:
                    rounds(tile, at + 8, 4)

            affine_even(0)
            low(0, 0)
            for k in range(KB):
                if k % 2 == 0 and k + 2 < KB:
                    affine_even(k + 2)
                h_low(k)
                if k == 4:
                    low(1, 0)
            low(0, 1)
            with dve.Fori(1, 7) as i:
                block_(i, None, 0)
            block_(7, None, 0, P, 80)
            block_(8, None, 0, 80, P)
            V.memset(maskb[:, 0:3 * P], 0.0).then_inc(mask_ok, 1)
            dve.wait_ge(mask_ok, 1)
            V.memset(maskb[0:64, CHUNK:P], MASKED).then_inc(passed, 1)
            V.memset(maskb[0:64, P + 3 * CHUNK:3 * P], MASKED).then_inc(mask_ok, 1)
            for (c0, n, perm, tile), g0 in zip(SEGMENTS, base_of):
                if tile is None:
                    with dve.Fori(0, n) as i:
                        block_(i + g0, None, 0)
                    dve.wait_ge(iw_T, 1)
                    V.tensor_scalar(iw[:].rearrange("p t h -> p (t h)"), ps_w[:, 0:P], IDX_DIM ** -0.5 * IDX_HEADS ** -0.5, None,
                                    ALU.mult).then_inc(iw_ok, 1)
                    dve.wait_ge(iw_ok, 1)
                    continue
                add_scores(tile)
                k = IDX_TILES.index(tile)
                last = g0 + n - 1 == LAST
                with dve.Fori(0, 3 if last else 4) as i:
                    block_(i + g0, tile, i * 16 + 64 * k)
                if last:
                    block_(LAST, tile, 48 + 64 * k, P, 0)
                elif n > 4:
                    with dve.Fori(4, n) as i:
                        block_(i + g0, None, 0)
                keys = width(tile)[0]
                at = P * (tile * (tile + 1) // 2)
                dve.wait_ge(top, 64 * k + 64)
                V.tensor_scalar(maskb[:, at:at + keys], score[:, 0:keys], (CHOSEN + UNSEEN) / 2, MASKED,
                                ALU.is_gt, ALU.mult).then_inc(mask_ok, 1)

        @block.tensor
        def _(pe):
            M, TR = nc.tensor.matmul, nc.tensor.transpose

            def products(i, c, n, k, h, m):
                kk, cols, out = HALF * h + k, slice(c, c + n), ps_z[i][0:m, 0:n]
                M(out, w_hi[:, h, k, 0:m], h_hi[:, kk, cols], start=kk == 0, stop=False)
                M(out, w_hi[:, h, k, 0:m], h_lo[:, kk, cols], start=False, stop=False)
                return M(out, w_lo[:, h, k, 0:m], h_hi[:, kk, cols], start=False, stop=kk == KB - 1)

            def block_(G, m=P):
                for h in range(2):
                    pe.wait_ge(w_lo_ok[h], G + 1)
                    for i, (c, n) in enumerate(SLICES):
                        if h == 0:
                            pe.wait_ge(z_read[i], G)
                        for k in range(HALF):
                            ins = products(i, c, n, k, h, m)
                        if h == 1:
                            ins.then_inc(z_done, 1)
                    if h == 0:
                        ins.then_inc(w_used, 1)

            def first_block():
                for h in range(2):
                    pe.wait_ge(w_lo_ok[h], 1)
                    for k in range(HALF):
                        pe.wait_ge(lo_ok, HALF * h + k + 1)
                        for i, (c, n) in enumerate(SLICES):
                            ins = products(i, c, n, k, h, P)
                            if h == 1 and k == HALF - 1:
                                ins.then_inc(z_done, 1)
                    if h == 0:
                        ins.then_inc(w_used, 1)

            def scores(tile):
                if tile == IDX_TILES[0]:
                    pe.wait_ge(idx_in, 48)
                    pe.wait_ge(g_copied, SEGMENTS[0][1])
                    for t in range(SEQ // P):
                        ins = TR(ps_w[:, IDX_HEADS * t:IDX_HEADS * t + IDX_HEADS], score[0:IDX_HEADS, t * P:t * P + P],
                                 ident[0:IDX_HEADS, 0:IDX_HEADS])
                    ins.then_inc(iw_T, 1)
                pe.wait_ge(iq_in, 16 * (IDX_TILES.index(tile) + 1))
                for u, (hp, h2, c, w) in enumerate(units(tile), first_unit[tile]):
                    if u >= 4:
                        pe.wait_ge(s_relu, u - 3)
                    half = slice(64 * h2, 64 * h2 + 64)
                    ins = M(ps_s[u % 4][:, 0:w], iqT[half, hp, :], ikT[half, c:c + w], start=True, stop=True)
                    ins.then_inc(s_mm, 1)

            def gate_unit(U):
                pe.wait_ge(g_dma, U * 32 + 16)
                pe.sem_inc(passed, 1)
                for k in range(KB):
                    v = k % 4
                    ins = M(ps_w[32 * v:32 * v + 32, 0:GATE_COLS], cT[:, k, :], wg[:, k, :], start=k < 4, stop=k >= KB - 4)
                ins.then_inc(g_mm, 1)

            first_block()
            with pe.Fori(1, 8) as i:
                block_(i)
            block_(8, 80)
            for (c0, n, perm, tile), g0 in zip(SEGMENTS, base_of):
                if tile is not None:
                    scores(tile)
                    pe.wait_ge(iw_ok, 1)
                with pe.Fori(0, n) as i:
                    block_(i + g0)
                    if g0 != base_of[-1]:
                        gate_unit(i + (g0 - base_of[0]))



def scan_states(nc, io, out, keep, scr):
    tabs, ident = keep["s5_tabs"], keep["ident"]
    with ExitStack() as ctx:
        signals = cleared_after(nc, ctx)

        def sb(name, shape, dt=F32):
            return ctx.enter_context(nc.sbuf_tensor(name, shape, dt))

        def sem(name):
            return new_signal(nc, signals, name)

        uy = sb("uy", [P, GROUPS, NSTEP])
        p_in = sb("p_in", [P, PAIRS, 2, P])
        q_out = sb("q_out", [P, PAIRS, 2, P])
        toep = sb("toep", [P, GROUPS, P])
        rot = sb("rot", [P, 2, PAIRS, PSTEP])
        wide = sb("wide", [P, 2, PAIR_BATCH, PSTEP])
        part = sb("part", [P, 4, PAIR_BATCH, PSTEP])
        hist = sb("hist", [P, 2, 2, PAIR_BATCH, NSTEP])
        dec_b = sb("dec_b", [P, 2, 2, PAIR_BATCH, 2 * DEC_B])
        dec_t = sb("dec_t", [P, 4, PAIR_BATCH, DEC_B])
        state_rows = sb("state_rows", [P, 2, 2, P])
        h0 = sb("h0", [P, 2, DEC_B, PAIRS])
        last = sb("last", [P, 2, DEC_B + 1, PAIRS])
        ps_b = ctx.enter_context(nc.psum_tensor("ps_b", [P, 2, 2, 512], F32))
        ps_y = ctx.enter_context(nc.psum_tensor("ps_y", [P, 4, 512], F32))

        u_in, h0_in = sem("u_in"), sem("h0_in")
        p_land, q_land, t_land = ([sem(f"{n}{q}") for q in range(4)] for n in ("p_land", "q_land", "t_land"))
        rot_dve, rot_pool, rot_ok = sem("rot_dve"), sem("rot_pool"), sem("rot_ok")
        b_mm, b_read, products, turned, scanned = (sem(n) for n in ("b_mm", "b_read", "products", "turned", "scanned"))
        backs, hist_ok, dec_copied, dec_ok, dec_step = (sem(n) for n in ("backs", "hist_ok", "dec_copied", "dec_ok", "dec_step"))
        y_mm, y_copied, y_out, zeroed, h0_T, h0_ok, stepped = (sem(n) for n in ("y_mm", "y_copied", "y_out", "zeroed", "h0_T", "h0_ok", "stepped"))
        last_T, last_copied, state_out = sem("last_T"), sem("last_copied"), sem("state_out")
        zt = scr["zt"]
        block = ctx.enter_context(nc.Block())
        DVE_PAIRS = 22

        def last_rows(ri):
            return part[0:PAIRS, ri, 0, :]

        @block.sync
        def _(sp):
            def matrices(q):
                pairs = slice(8 * q, 8 * q + 8)
                sp.dma_start(p_in[:, pairs], scr["s5_in"][:, pairs]).then_inc(p_land[q], 16)
                sp.dma_start(q_out[:, pairs], scr["s5_out"][:, pairs]).then_inc(q_land[q], 16)

            def quarter(q):
                groups = slice(16 * q, 16 * q + 16)
                if q:
                    matrices(q)
                for s in range(STEP):
                    at = CH * (STEP - 1 - s)
                    sp.dma_start(toep[CH * s:CH * s + CH, groups],
                                 scr["taps"][groups, :, at:at + P].rearrange("g c t -> c g t")).then_inc(t_land[q], 16)

            matrices(0)
            for s in range(STEP):
                sp.dma_start(uy[CH * s:CH * s + CH],
                             zt[U0:U0 + 1024, s * NSTEP:s * NSTEP + NSTEP].rearrange("(g c) n -> c g n", c=CH)).then_inc(u_in, 16)
            for ri, name in enumerate(("state_ssm_re", "state_ssm_im")):
                sp.dma_start(state_rows[:, ri], io[name][0].rearrange("(h b) (j g) p -> (b j) h (g p)", h=2, g=2)).then_inc(h0_in, 16)
            quarter(0)
            sp.wait_ge(rot_ok, 2)
            for q in range(1, 4):
                quarter(q)
            for half in range(2):
                sp.wait_ge(y_copied, 2 * (BATCHES // 2) * (half + 1))
                g = slice(32 * half, 32 * half + 32)
                for s in range(STEP):
                    sp.dma_start(scr["y"].rearrange("(g c) t -> c g t", c=CH)[:, g, s * NSTEP:s * NSTEP + NSTEP],
                                 uy[CH * s:CH * s + CH, g]).then_inc(y_out, 16)
            for ri, (name_d, name_p) in enumerate((("ssm_re_sample", "ssm_re_prompt"), ("ssm_im_sample", "ssm_im_prompt"))):
                sp.wait_ge(last_copied, 2)
                sp.dma_start(out[name_d][0].rearrange("(h b) (j g) p -> (b j) h (g p)", h=2, g=2), state_rows[:, ri]).then_inc(state_out, 16)
                sp.dma_start(out[name_p][0, 0].rearrange("(j g) p -> j (g p)", g=2), last_rows(ri)).then_inc(state_out, 16)
            sp.wait_ge(y_out, 16 * 2 * STEP)
            sp.wait_ge(state_out, 64)

        def rotations(E, eng, done, pairs, work):
            count = [0]

            def step(ins):
                count[0] += 1
                ins.then_inc(done, 1)

            def settle():
                eng.wait_ge(done, count[0])

            r, i = rot[:, 0, pairs], rot[:, 1, pairs]
            n = pairs.stop - pairs.start
            step(E.memset(r[:, :, 0:1], 1.0))
            step(E.memset(i[:, :, 0:1], 0.0))
            step(E.tensor_copy(r[:, :, 1:2], tabs[:, 1, pairs].unsqueeze(2)))
            step(E.tensor_copy(i[:, :, 1:2], tabs[:, 2, pairs].unsqueeze(2)))
            m = 1
            while m < PSTEP:
                settle()
                if m > 1:
                    a, b = r[:, :, m // 2], i[:, :, m // 2]
                    t = [work[:, k, pairs, 0] for k in range(3)]
                    step(E.tensor_tensor(t[0], a, a, ALU.mult))
                    step(E.tensor_tensor(t[1], b, b, ALU.mult))
                    step(E.tensor_tensor(t[2], a, b, ALU.mult))
                    settle()
                    step(E.tensor_tensor(r[:, :, m], t[0], t[1], ALU.subtract))
                    step(E.tensor_tensor(i[:, :, m], t[2], t[2], ALU.add))
                    settle()
                    lo, hi = slice(1, m), slice(m + 1, 2 * m)
                    er, ei = (x[:, :, m:m + 1].broadcast_to([P, n, m - 1]) for x in (r, i))
                    w0, w1 = work[:, 0, pairs, 0:m - 1], work[:, 1, pairs, 0:m - 1]
                    step(E.tensor_tensor(r[:, :, hi], r[:, :, lo], er, ALU.mult))
                    step(E.tensor_tensor(w0, i[:, :, lo], ei, ALU.mult))
                    step(E.tensor_tensor(i[:, :, hi], i[:, :, lo], er, ALU.mult))
                    step(E.tensor_tensor(w1, r[:, :, lo], ei, ALU.mult))
                    settle()
                    step(E.tensor_tensor(r[:, :, hi], r[:, :, hi], w0, ALU.subtract))
                    step(E.tensor_tensor(i[:, :, hi], i[:, :, hi], w1, ALU.add))
                m *= 2
            settle()

        work = p_in[:, 8:].rearrange("p j r n -> p (j r n)")[:, 0:3 * PAIRS * 64].rearrange("p (a j n) -> p a j n", a=3, j=PAIRS)

        @block.gpsimd
        def _(pool):
            G = nc.gpsimd
            rotations(G, pool, rot_pool, slice(DVE_PAIRS, PAIRS), work)
            G.memset(hist[:, :, :, :, 0:1], 0.0).then_inc(zeroed, 1)
            pool.wait_ge(zeroed, 1)
            pool.sem_inc(rot_ok, 1)
            pool.wait_ge(h0_ok, 4)
            n = 0
            for b in range(BATCHES):
                js, s = slice(PAIR_BATCH * b, PAIR_BATCH * b + PAIR_BATCH), b % 2
                ar, ai = (bc(tabs[:, k, js], 2, DEC_B) for k in (3, 4))
                steps = lambda ri, c: hist[:, s, ri, :, PSTEP + c::2]
                xr, xi = (h0[:, ri, :, js].rearrange("p b j -> p j b") for ri in range(2))
                pool.wait_ge(dec_copied, 2 * b + 2)
                if b >= 2:
                    pool.wait_ge(y_mm, b - 1)
                G.tensor_copy(steps(0, 0), xr).then_inc(dec_step, 1)
                G.tensor_copy(steps(1, 0), xi).then_inc(dec_step, 1)
                n += 2
                for c in range(2):
                    t = [dec_t[:, k] for k in range(4)]
                    bu = [dec_b[:, s, ri, :, c::2] for ri in range(2)]
                    if c == 0:
                        to = [steps(0, 1), steps(1, 1)]
                    else:
                        xr, xi = to
                        to = [last[:, ri, 0:DEC_B, js].rearrange("p b j -> p j b") for ri in range(2)]
                    for k, (a, x) in enumerate(((ar, xr), (ai, xi), (ar, xi), (ai, xr))):
                        G.tensor_tensor(t[k], a, x, ALU.mult).then_inc(dec_step, 1)
                    n += 4
                    pool.wait_ge(dec_step, n)
                    G.tensor_tensor(t[0], t[0], t[1], ALU.subtract).then_inc(dec_step, 1)
                    G.tensor_tensor(t[2], t[2], t[3], ALU.add).then_inc(dec_step, 1)
                    n += 2
                    pool.wait_ge(dec_step, n)
                    G.tensor_tensor(to[0], t[0], bu[0], ALU.add).then_inc(dec_step, 1)
                    ins = G.tensor_tensor(to[1], t[2], bu[1], ALU.add)
                    ins.then_inc(dec_step, 1)
                    n += 2
                    pool.wait_ge(dec_step, n)
                pool.sem_inc(dec_ok, 1)

        @block.scalar
        def _(act):
            for b in range(BATCHES):
                act.wait_ge(y_mm, b + 1)
                for e in range(2):
                    dst = uy[:, 8 * b + e:8 * b + 8:2].rearrange("p (a c) n -> p a c n", a=2)
                    src = ps_y[:, 2 * e:2 * e + 2, 0:2 * NSTEP].rearrange("p a (c n) -> p a c n", c=2)
                    nc.scalar.activation(dst, src, ACT.Copy).then_inc(y_copied, 1)
            act.wait_ge(last_T, 2)
            nc.scalar.activation(state_rows[:].rearrange("p r h q -> p (r h q)"), ps_y[:, 0], ACT.Copy).then_inc(last_copied, 1)
            nc.scalar.activation(part[0:PAIRS, 0:2, 0, :], ps_y[0:PAIRS, 1, 0:2 * P].rearrange("p (r q) -> p r q", r=2),
                                 ACT.Copy).then_inc(last_copied, 1)

        @block.vector
        def _(dve):
            V = nc.vector
            rotations(V, dve, rot_dve, slice(0, DVE_PAIRS), work)
            dve.sem_inc(rot_ok, 1)
            dve.wait_ge(h0_T, 1)
            for ri in range(2):
                for h in range(2):
                    V.tensor_copy(h0[:, ri, 4 * h:4 * h + 4].rearrange("p b j -> p (b j)"),
                                  ps_y[:, 0, (2 * ri + h) * P:(2 * ri + h + 1) * P]).then_inc(h0_ok, 1)
            dve.wait_ge(rot_ok, 2)
            for b in range(BATCHES):
                js, s = slice(PAIR_BATCH * b, PAIR_BATCH * b + PAIR_BATCH), b % 2
                er, ei = (rot[:, ri, js].rearrange("p (a c) n -> p a c n", a=2) for ri in range(2))
                br, bi = (ps_b[:, ri, :, 0:2 * NSTEP].rearrange("p a (c n) -> p a c n", c=2) for ri in range(2))
                split = lambda t: t.rearrange("p (a c) n -> p a c n", a=2)
                dve.wait_ge(b_mm, b + 1)
                if b >= 2:
                    dve.wait_ge(dec_ok, b - 1)
                for ri, x in enumerate((br, bi)):
                    V.tensor_copy(split(dec_b[:, s, ri]), x[:, :, :, PSTEP:]).then_inc(dec_copied, 1)
                if b:
                    dve.wait_ge(hist_ok, b)
                V.tensor_tensor(split(wide[:, 0]), er, br[:, :, :, 0:PSTEP], ALU.mult).then_inc(products, 1)
                V.tensor_tensor(split(part[:, 0]), ei, bi[:, :, :, 0:PSTEP], ALU.mult).then_inc(products, 1)
                V.tensor_tensor(split(wide[:, 1]), er, bi[:, :, :, 0:PSTEP], ALU.mult).then_inc(products, 1)
                V.tensor_tensor(split(part[:, 1]), ei, br[:, :, :, 0:PSTEP], ALU.mult).then_inc(b_read, 1)
                dve.wait_ge(products, 3 * b + 3)
                V.tensor_tensor(wide[:, 0], wide[:, 0], part[:, 0], ALU.add).then_inc(turned, 1)
                dve.wait_ge(b_read, b + 1)
                V.tensor_tensor(wide[:, 1], wide[:, 1], part[:, 1], ALU.subtract).then_inc(turned, 1)
                dve.wait_ge(turned, 2 * b + 2)
                for ri in range(2):
                    for j in range(PAIR_BATCH):
                        r = tabs[:, 0, PAIR_BATCH * b + j:PAIR_BATCH * b + j + 1].broadcast_to([P, PSTEP])
                        V.tensor_tensor_scan(wide[:, ri, j], r, wide[:, ri, j], 0.0, ALU.mult, ALU.add).then_inc(scanned, 1)
                dve.wait_ge(scanned, 8 * b + 8)
                E = [rot[:, ri, js] for ri in range(2)]
                for k, (e, x) in enumerate(((0, 0), (1, 1), (0, 1), (1, 0))):
                    V.tensor_tensor(part[:, k], E[e], wide[:, x], ALU.mult).then_inc(backs, 1)
                if b >= 2:
                    dve.wait_ge(y_mm, b - 1)
                dve.wait_ge(backs, 4 * b + 4)
                V.tensor_tensor(last[:, 0, DEC_B, js], part[:, 0, :, PSTEP - 1], part[:, 1, :, PSTEP - 1], ALU.subtract).then_inc(stepped, 1)
                V.tensor_tensor(last[:, 1, DEC_B, js], part[:, 2, :, PSTEP - 1], part[:, 3, :, PSTEP - 1], ALU.add).then_inc(stepped, 1)
                V.tensor_tensor(hist[:, s, 0, :, 1:PSTEP], part[:, 0, :, 0:PSTEP - 1], part[:, 1, :, 0:PSTEP - 1], ALU.subtract).then_inc(stepped, 1)
                V.tensor_tensor(hist[:, s, 1, :, 1:PSTEP], part[:, 2, :, 0:PSTEP - 1], part[:, 3, :, 0:PSTEP - 1], ALU.add).then_inc(hist_ok, 1)

        @block.tensor
        def _(pe):
            M, TR = nc.tensor.matmul, nc.tensor.transpose
            pe.wait_ge(h0_in, 32)
            for ri in range(2):
                for h in range(2):
                    ins = TR(ps_y[:, 0, (2 * ri + h) * P:(2 * ri + h + 1) * P], state_rows[:, ri, h], ident[:])
            ins.then_inc(h0_T, 1)

            def inputs(b):
                if b:
                    pe.wait_ge(b_read, b)
                for j in range(PAIR_BATCH):
                    pair = PAIR_BATCH * b + j
                    for ri in range(2):
                        for g in range(2):
                            ins = M(ps_b[64 * g:64 * g + 64, ri, j // 2, (j % 2) * NSTEP:(j % 2 + 1) * NSTEP],
                                    p_in[:, pair, ri, 64 * g:64 * g + 64], uy[:, 2 * pair + g, :], start=True, stop=True)
                ins.then_inc(b_mm, 1)

            def outputs(b):
                if b:
                    pe.wait_ge(y_copied, 2 * b)
                bank = lambda j, g: ps_y[:, 2 * g + j // 2, (j % 2) * NSTEP:(j % 2 + 1) * NSTEP]
                for g in range(2):
                    for j in range(PAIR_BATCH):
                        group = 2 * (PAIR_BATCH * b + j) + g
                        M(bank(j, g), toep[:, group, :], uy[:, group, :], start=j % 2 == 0, stop=False)
                pe.wait_ge(hist_ok, b + 1)
                pe.wait_ge(dec_ok, b + 1)
                for j in range(PAIR_BATCH):
                    for ri in range(2):
                        for g in range(2):
                            half = slice(64 * g, 64 * g + 64)
                            ins = M(bank(j, g), q_out[half, PAIR_BATCH * b + j, ri, :], hist[half, b % 2, ri, j, :],
                                    start=False, stop=ri == 1 and j % 2 == 1)
                ins.then_inc(y_mm, 1)

            pe.wait_ge(p_land[0], 16)
            pe.wait_ge(u_in, 16 * STEP)
            inputs(0)
            pe.wait_ge(h0_ok, 4)
            for b in range(BATCHES):
                if b + 1 < BATCHES:
                    pe.wait_ge(p_land[(b + 1) // 2], 16)
                    inputs(b + 1)
                pe.wait_ge(t_land[b // 2], 16 * STEP)
                pe.wait_ge(q_land[b // 2], 16)
                outputs(b)
            pe.wait_ge(y_copied, 2 * BATCHES)
            for ri in range(2):
                for h in range(2):
                    ins = TR(ps_y[:, 0, (2 * ri + h) * P:(2 * ri + h + 1) * P],
                             last[:, ri, 4 * h:4 * h + 4].rearrange("p b j -> p (b j)"), ident[:])
            ins.then_inc(last_T, 1)
            for ri in range(2):
                ins = TR(ps_y[0:PAIRS, 1, ri * P:ri * P + P], last[:, ri, DEC_B, :], ident[:])
            ins.then_inc(last_T, 1)


def gate_states(nc, io, out, keep, scr):
    ident = keep["ident"]
    vecT, mix_hi, mix_lo = keep["vecT"], keep["ssm_hi"], keep["ssm_lo"]
    NB = 1024 // P
    QUART = NB // 2
    with ExitStack() as ctx:
        signals = cleared_after(nc, ctx)

        def sb(name, shape, dt=F32):
            return ctx.enter_context(nc.sbuf_tensor(name, shape, dt))

        def sem(name):
            return new_signal(nc, signals, name)

        v_hi, v_lo = sb("v_hi", [P, NB, TOK], F32R), sb("v_lo", [P, NB, TOK], F32R)
        y_in = sb("y_in", [P, 2, TOK])
        w_raw = sb("g_raw", [P, 2, QUART, P])
        w_hi, w_lo = sb("g_hi", [P, 2, QUART, P], F32R), sb("g_lo", [P, 2, QUART, P], F32R)
        zs = sb("zs", [P, TOK])
        s1, s2 = sb("s1", [P, TOK]), sb("s2", [P, TOK])
        ps_z = [ctx.enter_context(nc.psum_tensor(f"ps_g{i}", [P, 512], F32)) for i in range(NTC)]
        W = KV_HEADS * HD
        offset = [keep["ssm_base"]]

        def at(name, shape):
            t = nc.alloc_sbuf_tensor_at(name, shape, F32, offset=offset[0])
            size = 4
            for n in shape[1:]:
                size *= n
            offset[0] += size
            assert offset[0] <= keep["ssm_base"] + 4 * NB * TOK
            return t

        kvT, ikT = at("kvT", [P, 2 * KV_HEADS, TOK]), at("ikT_n", [IDX_DIM, TOK])
        rows, ik_rows = at("kv_rows", [P, 2, 2 * W]), at("ik_rows", [P, 2, IDX_DIM])
        ps_kv = [ctx.enter_context(nc.psum_tensor(f"ps_kv{i}", [P, 512], F32)) for i in range(2)]
        ps_ik = [ctx.enter_context(nc.psum_tensor(f"ps_ik{i}", [P, 512], F32)) for i in range(2)]
        kv_in, kv_T, kv_ok, ik_ok = (sem(n) for n in ("kv_in", "kv_T", "kv_ok", "ik_ok"))
        kv_out = [sem("kv_out0"), sem("kv_out1")]

        def results(t):
            if t < NT - 1:
                part = slice(t * P, t * P + P)
                return (out["k_prompt"][0, 0, part].rearrange("t h d -> t (h d)"),
                        out["v_prompt"][0, 0, part].rearrange("t h d -> t (h d)"), out["idx_k_prompt"][0, 0, part])
            return (out["k_sample"][0].rearrange("b t h d -> (b t) (h d)"),
                    out["v_sample"][0].rearrange("b t h d -> (b t) (h d)"),
                    out["idx_k_sample"][0].rearrange("b t d -> (b t) d"))

        yl = [sem("yl0"), sem("yl1")]
        gelu_ok, v_hi_ok, v_lo_ok = sem("gelu_ok"), sem("v_hi_ok"), sem("v_lo_ok")
        w_in = [sem("gw_in0"), sem("gw_in1")]
        w_hi_ok, w_lo_ok = [sem("gw_hi0"), sem("gw_hi1")], [sem("gw_lo0"), sem("gw_lo1")]
        w_used, z_done, sig_ok, zs_in, zsig_ok = sem("gw_used"), sem("gz_done"), sem("sig_ok"), sem("zs_in"), sem("zsig_ok")
        v_sum, gated, gated_z, zgated, mixed, m_hi, passed = (sem(n) for n in ("v_sum", "gated", "gated_z", "zgated", "mixed", "m_hi", "passed_g"))
        wv = io["w_glu"][0].rearrange("(k p) n -> p k n", p=P)
        zt = scr["zt"]
        block = ctx.enter_context(nc.Block())

        @block.sync
        def _(sp):
            def load_w(i):
                for h in range(2):
                    sp.dma_start(w_raw[:, h], wv[:, QUART * h:QUART * h + QUART, bass.ds(i * P, P)]).then_inc(w_in[h], 16)

            def store_rows(t):
                k, v, ik = results(t)
                sp.wait_ge(kv_ok, t + 1)
                sp.wait_ge(ik_ok, t + 1)
                sp.dma_start(k, rows[:, t % 2, 0:W]).then_inc(kv_out[t % 2], 16)
                sp.dma_start(v, rows[:, t % 2, W:2 * W]).then_inc(kv_out[t % 2], 16)
                sp.dma_start(ik, ik_rows[:, t % 2]).then_inc(kv_out[t % 2], 16)

            sp.dma_start(kvT[:], zt[K0:IQ0].rearrange("(h d) t -> d h t", d=HD)).then_inc(kv_in, 16)
            sp.dma_start(ikT[:], zt[IK0:IW0]).then_inc(kv_in, 16)
            for k in range(NB):
                if k >= 2:
                    sp.wait_ge(gelu_ok, k - 1)
                sp.dma_start(y_in[:, k % 2], scr["y"][k * P:k * P + P, :]).then_inc(yl[k % 2], 16)
                if k == 1:
                    load_w(0)
                if k >= 1:
                    store_rows(k - 1)
            store_rows(NB - 1)
            store_rows(NB)
            sp.dma_start(zs[:], zt[ZS0:ZS0 + P, :]).then_inc(zs_in, 16)
            with sp.Fori(1, NB) as i:
                sp.wait_ge(zgated, i)
                sp.dma_start(zs[:], zt[bass.ds(i * P + ZS0, P), :]).then_inc(zs_in, 16)

        @block.scalar
        def _(act):
            A = nc.scalar.activation

            def load_w(i):
                for h in range(2):
                    act.wait_ge(w_lo_ok[h], i)
                    act.dma_start(w_raw[:, h], wv[:, QUART * h:QUART * h + QUART, bass.ds(i * P, P)]).then_inc(w_in[h], 16)

            def high(h, i):
                act.wait_ge(w_in[h], (i + 1) * 16)
                if h == 0:
                    after(act, w_used, i)
                else:
                    after(act, z_done, i * NTC)
                A(w_hi[:, h], w_raw[:, h], ACT.Copy).then_inc(w_hi_ok[h], 1)

            def copy_rows(t):
                act.wait_ge(kv_T, t + 1)
                if t >= 2:
                    act.wait_ge(kv_out[t % 2], 48 * (t // 2))
                A(rows[:, t % 2], ps_kv[t % 2][:], ACT.Copy).then_inc(kv_ok, 1)

            copy_rows(0)
            for k in range(NB):
                if k == 2:
                    high(0, 0)
                    high(1, 0)
                copy_rows(k + 1)
                act.wait_ge(yl[k % 2], 16 * (k // 2 + 1))
                if k >= 2:
                    act.wait_ge(v_lo_ok, k - 1)
                g = (s1, s2)[k % 2]
                A(g[:], y_in[:, k % 2], ACT.Gelu_apprx_tanh).then_inc(gelu_ok, 1)

            def block_(i, last):
                act.wait_ge(zs_in, i * 16 + 16)
                after(act, zgated, i)
                A(s2[:], zs[:], ACT.Sigmoid).then_inc(zsig_ok, 1)
                if not last:
                    load_w(i + 1)
                    high(0, i + 1)
                for t, (c, n) in enumerate(SLICES):
                    act.wait_ge(z_done, i * NTC + t + 1)
                    if t == 0:
                        after(act, gated, i)
                    act.sem_inc(passed, 1)
                    A(s1[:, c:c + n], ps_z[t][:, 0:n], ACT.Sigmoid, bias=bias(i)).then_inc(sig_ok, 1)
                if not last:
                    high(1, i + 1)
                act.wait_ge(mixed, i + 1)
                if isinstance(i, int) and i == 0:
                    act.wait_ge(kv_out[0], 48 * ((NT + 1) // 2))
                    act.wait_ge(kv_out[1], 48 * (NT // 2))
                act.sem_inc(passed, 1)
                A(mix_hi[:, bass.ds(i, 1)].rearrange("p a t -> p (a t)"), s1[:], ACT.Copy).then_inc(m_hi, 1)

            def bias(i):
                return vecT[:, bass.ds(i + 64, 1)]

            act.wait_ge(v_lo_ok, NB)
            block_(0, False)
            with act.Fori(1, NB - 1) as i:
                block_(i, False)
            block_(NB - 1, True)

        @block.vector
        def _(dve):
            V = nc.vector

            def low(h, i):
                dve.wait_ge(w_hi_ok[h], i + 1)
                V.tensor_tensor(w_lo[:, h], w_raw[:, h], w_hi[:, h].bitcast(F32), ALU.subtract).then_inc(w_lo_ok[h], 1)

            def copy_ik(t):
                dve.wait_ge(kv_T, t + 1)
                if t >= 2:
                    dve.wait_ge(kv_out[t % 2], 48 * (t // 2))
                V.tensor_copy(ik_rows[:, t % 2], ps_ik[t % 2][:, 0:IDX_DIM]).then_inc(ik_ok, 1)

            copy_ik(0)
            for k in range(NB):
                copy_ik(k + 1)
                if k == 2:
                    low(0, 0)
                    low(1, 0)
                dve.wait_ge(gelu_ok, k + 1)
                V.tensor_copy(v_hi[:, k], (s1, s2)[k % 2][:]).then_inc(v_hi_ok, 1)
                dve.wait_ge(v_hi_ok, k + 1)
                V.tensor_tensor(v_lo[:, k], (s1, s2)[k % 2][:], v_hi[:, k].bitcast(F32), ALU.subtract).then_inc(v_lo_ok, 1)

            def block_(i, last):
                row = lambda t: t[:, bass.ds(i, 1)].rearrange("p a t -> p (a t)")
                dve.wait_ge(zsig_ok, i + 1)
                V.tensor_tensor(zs[:], zs[:], s2[:], ALU.mult).then_inc(v_sum, 1)
                if not last:
                    low(0, i + 1)
                dve.wait_ge(v_sum, i * 2 + 1)
                V.tensor_tensor(s2[:], row(v_hi).bitcast(F32), row(v_lo).bitcast(F32), ALU.add).then_inc(v_sum, 1)
                dve.wait_ge(v_sum, i * 2 + 2)
                V.tensor_tensor(zs[:], s2[:], zs[:], ALU.mult).then_inc(gated_z, 1)
                dve.wait_ge(sig_ok, i * NTC + NTC)
                dve.wait_ge(gated_z, i + 1)
                V.tensor_tensor(s1[:], s1[:], zs[:], ALU.mult).then_inc(mixed, 1)
                dve.wait_ge(mixed, i + 1)
                dve.sem_inc(zgated, 1)
                if not last:
                    low(1, i + 1)
                dve.wait_ge(m_hi, i + 1)
                V.tensor_tensor(row(mix_lo), s1[:], row(mix_hi).bitcast(F32), ALU.subtract).then_inc(gated, 1)

            block_(0, False)
            with dve.Fori(1, NB - 1) as i:
                block_(i, False)
            block_(NB - 1, True)

        @block.tensor
        def _(pe):
            M = nc.tensor.matmul

            def block_(i):
                for h in range(2):
                    pe.wait_ge(w_lo_ok[h], i + 1)
                    for t, (c, n) in enumerate(SLICES):
                        if h == 0:
                            pe.wait_ge(sig_ok, i * NTC)
                        for k in range(QUART):
                            kk, cols, o = QUART * h + k, slice(c, c + n), ps_z[t][:, 0:n]
                            M(o, w_hi[:, h, k], v_hi[:, kk, cols], start=kk == 0, stop=False)
                            M(o, w_hi[:, h, k], v_lo[:, kk, cols], start=False, stop=False)
                            ins = M(o, w_lo[:, h, k], v_hi[:, kk, cols], start=False, stop=kk == NB - 1)
                        if h == 1:
                            ins.then_inc(z_done, 1)
                    if h == 0:
                        ins.then_inc(w_used, 1)
            def first_block():
                for h in range(2):
                    pe.wait_ge(w_lo_ok[h], 1)
                    for k in range(QUART):
                        kk = QUART * h + k
                        pe.wait_ge(v_lo_ok, kk + 1)
                        for t, (c, n) in enumerate(SLICES):
                            cols, o = slice(c, c + n), ps_z[t][:, 0:n]
                            M(o, w_hi[:, h, k], v_hi[:, kk, cols], start=kk == 0, stop=False)
                            M(o, w_hi[:, h, k], v_lo[:, kk, cols], start=False, stop=False)
                            ins = M(o, w_lo[:, h, k], v_hi[:, kk, cols], start=False, stop=kk == NB - 1)
                            if kk == NB - 1:
                                ins.then_inc(z_done, 1)
                    if h == 0:
                        ins.then_inc(w_used, 1)

            pe.wait_ge(kv_in, 32)
            for t in range(NT):
                cols = slice(t * P, t * P + P)
                if t >= 2:
                    pe.wait_ge(kv_ok, t - 1)
                    pe.wait_ge(ik_ok, t - 1)
                nc.tensor.transpose(ps_ik[t % 2][:, 0:IDX_DIM], ikT[:, cols], ident[0:IDX_DIM, 0:IDX_DIM])
                for h in range(2 * KV_HEADS):
                    ins = nc.tensor.transpose(ps_kv[t % 2][:, h * HD:h * HD + HD], kvT[:, h, cols], ident[:])
                ins.then_inc(kv_T, 1)
            first_block()
            with pe.Fori(1, NB) as i:
                block_(i)


def attend_prompt(nc, out, keep, scr):
    ident, kT, v_nat, maskb = keep["ident"], keep["kT"], keep["v_nat"], keep["maskb"]
    mix_hi, mix_lo = keep["attn_hi"], keep["attn_lo"]
    SCALE = HD ** -0.5
    TILES = SEQ // P
    units = [(t, h) for t in range(TILES) for h in range(HEADS)]
    N = len(units)
    with ExitStack() as ctx:
        signals = cleared_after(nc, ctx)

        def sb(name, shape, dt=F32):
            return ctx.enter_context(nc.sbuf_tensor(name, shape, dt))

        def sem(name):
            return new_signal(nc, signals, name)

        q = sb("q", [P, 2, HEADS, P])
        za = sb("za", [P, HEADS, P])
        gate = sb("gate", [P, HEADS, P])
        probs = sb("probs", [P, 2, SEQ])
        pT = sb("pT", [P, 2, TILES, P])
        att = sb("att", [P, 2, P])
        stat = sb("row_stat", [P, 4, 2])
        ps_l = [ctx.enter_context(nc.psum_tensor(f"ps_l{i}", [P, 1024], F32)) for i in range(2)]
        ps_t = [ctx.enter_context(nc.psum_tensor(f"ps_t{i}", [P, 512], F32)) for i in range(2)]
        ps_o = [ctx.enter_context(nc.psum_tensor(f"ps_o{i}", [P, 512], F32)) for i in range(2)]

        q_in, za_in = [sem("q_in0"), sem("q_in1")], sem("za_in")
        k_in, v_in = sem("kT_in"), sem("v_nat_in")
        sig_ok, gate_ok, gate_used = sem("asig_ok"), sem("gate_ok"), sem("gate_used")
        logits_mm, logits_ok, bias_ok, exp_ok, recip_ok, probs_ok = (
            sem(n) for n in ("logits_mm", "logits_ok", "bias_ok", "exp_ok", "recip_ok", "probs_ok"))
        turned, turned_read, av_mm, att_ok, hi_ok, lo_ok = (
            sem(n) for n in ("p_turned", "p_turned_read", "av_mm", "att_ok", "att_hi_ok", "att_lo_ok"))
        zt = scr["zt"]
        banks = lambda t: (t + 4) // 4
        before = [sum(banks(t) for t, _ in units[:n]) for n in range(N + 1)]
        fills = [[sum(banks(t) > g for t, _ in units[:n]) for n in range(N + 1)] for g in range(2)]
        block = ctx.enter_context(nc.Block())

        @block.sync
        def _(sp):
            sp.dma_start(kT[:], zt[K0:V0].rearrange("(h d) t -> d h t", d=HD)).then_inc(k_in, 16)
            for t in range(TILES):
                if t >= 2:
                    sp.wait_ge(logits_mm, HEADS * (t - 1))
                cols = slice(t * P, t * P + P)
                sp.dma_start(q[:, t % 2], zt[Q0:K0, cols].rearrange("(h d) t -> d h t", d=HD)).then_inc(q_in[t % 2], 16)
                if t:
                    sp.wait_ge(gate_ok, t)
                sp.dma_start(za[:], zt[ZA0:U0, cols].rearrange("(h d) t -> d h t", d=HD)).then_inc(za_in, 16)
                if t == 0:
                    sp.dma_start(v_nat[:], out["v_prompt"][0, 0].rearrange("(n p) h d -> p n (h d)", p=P)).then_inc(v_in, 16)

        @block.gpsimd
        def _(pool):
            for t in range(TILES):
                pool.wait_ge(sig_ok, t + 1)
                nc.gpsimd.tensor_tensor(gate[:], gate[:], za[:], ALU.mult).then_inc(gate_ok, 1)

        @block.scalar
        def _(act):
            A = nc.scalar.activation

            def exponentials(n):
                t, h = units[n]
                keys = (t + 1) * P
                act.wait_ge(bias_ok, n + 1)
                A(probs[:, n % 2, 0:keys], probs[:, n % 2, 0:keys], ACT.Exp, bias=stat[:, 1, n % 2:n % 2 + 1],
                  scale=SCALE, accum_out=stat[:, 2, n % 2:n % 2 + 1]).then_inc(exp_ok, 1)

            def read_turned(n):
                t, h = units[n]
                if n >= 2:
                    act.wait_ge(av_mm, n - 1)
                for g in range(banks(t)):
                    act.wait_ge(turned, before[n] + g + 1)
                    k = min(4, t + 1 - 4 * g)
                    A(pT[:, n % 2, 4 * g:4 * g + k].rearrange("p b t -> p (b t)"), ps_t[g][:, 0:k * P],
                      ACT.Copy).then_inc(turned_read, 1)

            def high(n):
                t, h = units[n]
                act.wait_ge(att_ok, n + 1)
                out_ = mix_hi[:, h].rearrange("p (s n) -> p n s", s=STEP)[:, 16 * t:16 * t + 16, :]
                A(out_, att[:, n % 2].rearrange("p (n s) -> p n s", s=STEP), ACT.Copy).then_inc(hi_ok, 1)

            def sigmoid(t):
                act.wait_ge(za_in, 16 * (t + 1))
                if t:
                    act.wait_ge(att_ok, HEADS * t)
                A(gate[:], za[:], ACT.Sigmoid).then_inc(sig_ok, 1)

            for n in range(N + 3):
                if n < N:
                    exponentials(n)
                if 1 <= n <= N:
                    read_turned(n - 1)
                if n >= 3:
                    high(n - 3)
                if n == 0:
                    sigmoid(0)
                if n >= 3 and (n - 3) % HEADS == HEADS - 1 and (n - 3) // HEADS + 1 < TILES:
                    sigmoid((n - 3) // HEADS + 1)

        @block.vector
        def _(dve):
            V = nc.vector

            def logits(n):
                t, h = units[n]
                keys, at = (t + 1) * P, P * (t * (t + 1) // 2)
                dve.wait_ge(logits_mm, n + 1)
                if n >= 2:
                    dve.wait_ge(turned, before[n - 1])
                s = n % 2
                V.tensor_tensor_reduce(out=probs[:, s, 0:keys], in0=ps_l[s][:, 0:keys], in1=maskb[:, at:at + keys],
                                       scale=1.0, scalar=-3.0e38, op0=ALU.add, op1=ALU.max,
                                       accum_out=stat[:, 0, s:s + 1]).then_inc(logits_ok, 1)
                dve.wait_ge(logits_ok, n + 1)
                V.tensor_scalar(stat[:, 1, s:s + 1], stat[:, 0, s:s + 1], -SCALE, None, ALU.mult).then_inc(bias_ok, 1)

            def normalise(n):
                t, h = units[n]
                s, keys = n % 2, (t + 1) * P
                dve.wait_ge(exp_ok, n + 1)
                V.reciprocal(stat[:, 3, s:s + 1], stat[:, 2, s:s + 1]).then_inc(recip_ok, 1)
                dve.wait_ge(recip_ok, n + 1)
                V.tensor_scalar(probs[:, s, 0:keys], probs[:, s, 0:keys], stat[:, 3, s:s + 1], None, ALU.mult).then_inc(probs_ok, 1)

            def gate_it(n):
                t, h = units[n]
                dve.wait_ge(av_mm, n + 1)
                dve.wait_ge(gate_ok, t + 1)
                if n >= 2:
                    dve.wait_ge(lo_ok, n - 1)
                V.tensor_tensor(att[:, n % 2], ps_o[n % 2][:, 0:P], gate[:, h], ALU.mult).then_inc(att_ok, 1)

            def low(n):
                t, h = units[n]
                dve.wait_ge(hi_ok, n + 1)
                view = lambda m: m[:, h].rearrange("p (s n) -> p n s", s=STEP)[:, 16 * t:16 * t + 16, :]
                V.tensor_tensor(view(mix_lo), att[:, n % 2].rearrange("p (n s) -> p n s", s=STEP),
                                view(mix_hi).bitcast(F32), ALU.subtract).then_inc(lo_ok, 1)

            for n in range(N + 4):
                if 1 <= n <= N:
                    normalise(n - 1)
                if n < N:
                    logits(n)
                if n >= 4:
                    low(n - 4)
                if 3 <= n < N + 3:
                    gate_it(n - 3)

        @block.tensor
        def _(pe):
            M, TR = nc.tensor.matmul, nc.tensor.transpose

            def logits(n):
                t, h = units[n]
                s, keys = n % 2, (t + 1) * P
                pe.wait_ge(q_in[t % 2], 16 * (t // 2 + 1))
                if n >= 2:
                    pe.wait_ge(logits_ok, n - 1)
                for c in range(0, keys, 512):
                    w = min(512, keys - c)
                    ins = M(ps_l[s][:, c:c + w], q[:, t % 2, h], kT[:, h * KV_HEADS // HEADS, c:c + w], start=True, stop=True)
                ins.then_inc(logits_mm, 1)

            def turn(n):
                t, h = units[n]
                pe.wait_ge(probs_ok, n + 1)
                for g in range(banks(t)):
                    last = max((m for m in range(n) if banks(units[m][0]) > g), default=None)
                    if last is not None:
                        pe.wait_ge(turned_read, before[last] + g + 1)
                    for k in range(4 * g, min(4 * g + 4, t + 1)):
                        ins = TR(ps_t[g][:, (k % 4) * P:(k % 4) * P + P], probs[:, n % 2, k * P:k * P + P], ident[:])
                    ins.then_inc(turned, 1)

            def values(n):
                t, h = units[n]
                kv = h * KV_HEADS // HEADS
                pe.wait_ge(turned_read, before[n + 1])
                if n == 0:
                    pe.wait_ge(v_in, 16)
                if n >= 2:
                    pe.wait_ge(att_ok, n - 1)
                for k in range(t + 1):
                    ins = M(ps_o[n % 2][:, 0:P], v_nat[:, k, kv * HD:kv * HD + HD], pT[:, n % 2, k], start=k == 0, stop=k == t)
                ins.then_inc(av_mm, 1)

            pe.wait_ge(k_in, 16)
            logits(0)
            for n in range(N + 1):
                if n + 1 < N:
                    logits(n + 1)
                if n < N:
                    turn(n)
                if n:
                    values(n - 1)


DUMMY = -3.2e38


def attend_samples(nc, io, out, keep, scr):
    ident, kT = keep["ident"], keep["kT"]
    mix_hi, mix_lo = keep["attn_hi"], keep["attn_lo"]
    SCALE = HD ** -0.5
    HP = IDX_HEADS // 2
    BLK = PAST // P
    W = KV_HEADS * HD
    with ExitStack() as ctx:
        signals = cleared_after(nc, ctx)

        def sb(name, shape, dt=F32):
            return ctx.enter_context(nc.sbuf_tensor(name, shape, dt))

        def sem(name):
            return new_signal(nc, signals, name)

        iq = sb("iq_s", [P, DEC_B, HP * DEC_S])
        q = sb("q_s", [P, DEC_B, HEADS * DEC_S])
        ik_new = sb("ik_new", [P, P])
        w_rows = sb("w_rows", [2 * DEC_B, HP, DEC_S])
        wcol = sb("wcol", [P, 2, DEC_B])
        pick = sb("pick", [P, 240])
        spread = sb("spread", [P, DEC_B, HEADS, DEC_S], BF16)
        ik_rows = sb("ik_cached", [P, 2, BLK, 2, IDX_DIM])
        ikT = sb("ikT_s", [P, 2, DEC_KEYS])
        rel = sb("rel_s", [P, 2, DEC_KEYS])
        score = sb("score_s", [P, DEC_KEYS + 8])
        top8 = sb("top8_s", [P, 8])
        mask = sb("mask_s", [P, DEC_KEYS], BF16)
        gate = sb("gate_s", [P, HEADS, P])
        stage = nc.alloc_sbuf_tensor_at("q_stage", [P, HEADS, P], F32, offset=keep["maskb_base"])
        za = nc.alloc_sbuf_tensor_at("za_s", [P, HEADS, P], F32, offset=keep["maskb_base"] + 4 * HEADS * P)
        k_rows, v_rows = sb("k_cached", [P, 2, BLK, W]), sb("v_cached", [P, 2, BLK, W])
        v_new = sb("v_new", [DEC_S, 2, W])
        kT_s = sb("kT_s", [P, 2, KV_HEADS, DEC_KEYS])
        probs = sb("probs_s", [P, 2, DEC_KEYS])
        pT = sb("pT_s", [P, 2, BLK + 1, P])
        att = ik_rows[:, 0].rearrange("p n a d -> p n (a d)")
        stat = sb("stat_s", [P, 4, 2])
        ps_a = [ctx.enter_context(nc.psum_tensor(f"ps_a{i}", [P, 512], F32)) for i in range(2)]
        ps_k = [ctx.enter_context(nc.psum_tensor(f"ps_ks{i}", [P, 512], F32)) for i in range(2)]
        ps_o = [ctx.enter_context(nc.psum_tensor(f"ps_os{i}", [P, 512], F32)) for i in range(2)]
        ps_p = ctx.enter_context(nc.psum_tensor("ps_pt", [P, 512], F32))
        ps_sum = ctx.enter_context(nc.psum_tensor("ps_sum", [P, 512], F32))

        once_in, w_in_, w_T = sem("once_in"), sem("wcol_in"), sem("wcol_T")
        ik_in, k_in, v_in = ([sem(f"{n}{i}") for i in range(2)] for n in ("ikc_in", "kc_in", "vc_in"))
        once_ok, q_ok = sem("once_ok"), sem("q_s_ok")
        ik_T, ik_ok, s_mm, rel_ok, sum_mm = (sem(n) for n in ("ik_T", "ikT_ok", "si_mm", "rel_ok", "sum_mm"))
        scored, top, mask_ok = sem("scored"), sem("top_s"), sem("mask_s_ok")
        sig_ok, gate_ok = sem("sig_s"), sem("gate_s_ok")
        k_T, k_ok, l_mm, max_ok, bias_ok, exp_ok, recip_ok, probs_ok = (
            sem(n) for n in ("ks_T", "ks_ok", "ls_mm", "max_s", "bias_s", "exp_s", "recip_s", "probs_s_ok"))
        p_T, pT_ok, av_mm, att_ok, hi_ok, lo_ok = (sem(n) for n in ("ps_T", "pTs_ok", "avs_mm", "atts_ok", "his_ok", "los_ok"))
        zt = scr["zt"]
        block = ctx.enter_context(nc.Block())

        @block.sync
        def _(sp):
            def cached_idx(b):
                if b >= 2:
                    sp.wait_ge(ik_T, b - 1)
                src = io["cache_idx_k"][0, b].rearrange("(n p) d -> p n d", p=P)
                for twice in range(2):
                    sp.dma_start(ik_rows[:, b % 2, :, twice], src).then_inc(ik_in[b % 2], 16)

            def cached_keys(b):
                s = b % 2
                if b >= 2:
                    sp.wait_ge(k_T, b - 1)
                sp.dma_start(k_rows[:, s], io["cache_k"][0, b].rearrange("(n p) h d -> p n (h d)", p=P)).then_inc(k_in[s], 16)

            cached_idx(0)
            sp.dma_start(stage[:], zt[IQ0:IK0, SEQ:TOK].rearrange("(a q) t -> q a t", q=P)).then_inc(once_in, 16)
            for half in range(2):
                sp.dma_start(ik_new[64 * half:64 * half + 64, :], zt[IK0:IW0, SEQ:TOK]).then_inc(once_in, 16)
            src = zt[IW0:IW0 + IDX_HEADS, SEQ:TOK].rearrange("(a h) (b t) -> h b a t", h=2, b=DEC_B)
            for h2 in range(2):
                sp.dma_start(w_rows[DEC_B * h2:DEC_B * h2 + DEC_B], src[h2]).then_inc(w_in_, 16)
            cached_idx(1)
            cached_keys(0)
            cached_keys(1)
            sp.wait_ge(q_ok, 1)
            sp.dma_start(stage[:], zt[Q0:K0, SEQ:TOK].rearrange("(h d) t -> d h t", d=HD)).then_inc(once_in, 16)
            sp.dma_start(za[:], zt[ZA0:U0, SEQ:TOK].rearrange("(h d) t -> d h t", d=HD)).then_inc(once_in, 16)
            for b in range(2, DEC_B):
                cached_idx(b)
            for b in range(2, DEC_B):
                cached_keys(b)

        @block.scalar
        def _(act):
            A = nc.scalar.activation

            def idx_keys(b):
                s = b % 2
                act.wait_ge(ik_T, b + 1)
                if b >= 2:
                    act.wait_ge(s_mm, 2 * b - 2)
                if b == 0:
                    act.wait_ge(once_in, 16 * 3)
                A(ikT[:, s, 0:PAST], ps_k[s][:, 0:PAST], ACT.Copy).then_inc(ik_ok, 1)
                A(ikT[:, s, PAST:DEC_KEYS], ik_new[:, DEC_S * b:DEC_S * b + DEC_S], ACT.Copy).then_inc(ik_ok, 1)

            def keys(b):
                s = b % 2
                act.wait_ge(k_T, b + 1)
                if b >= 2:
                    act.wait_ge(l_mm, b - 1)
                A(kT_s[:, s, :, 0:PAST], ps_k[s][:].rearrange("p (h n) -> p h n", h=KV_HEADS), ACT.Copy).then_inc(k_ok, 1)
                A(kT_s[:, s, :, PAST:DEC_KEYS], kT[:, :, SEQ + DEC_S * b:SEQ + DEC_S * b + DEC_S], ACT.Copy).then_inc(k_ok, 1)

            def exponentials(b):
                s = b % 2
                act.wait_ge(bias_ok, b + 1)
                if b >= 2:
                    act.wait_ge(p_T, b - 1)
                A(probs[:, s], ps_a[s][:, 0:DEC_KEYS], ACT.Exp, bias=stat[:, 1, s:s + 1], scale=SCALE,
                  accum_out=stat[:, 2, s:s + 1]).then_inc(exp_ok, 1)

            def turned(b):
                s = b % 2
                act.wait_ge(p_T, b + 1)
                if b >= 2:
                    act.wait_ge(av_mm, b - 1)
                A(pT[:, s, 0:BLK].rearrange("p n t -> p (n t)"), ps_p[:, 0:BLK * P], ACT.Copy).then_inc(pT_ok, 1)
                A(pT[0:DEC_S, s, BLK], ps_p[0:DEC_S, BLK * P:BLK * P + P], ACT.Copy).then_inc(pT_ok, 1)

            def high(b):
                act.wait_ge(att_ok, b + 1)
                view = mix_hi[:].rearrange("p h (s n) -> p h s n", s=STEP)[:, :, :, PSTEP + 2 * b:PSTEP + 2 * b + 2]
                A(view, att[:, b % 2].rearrange("p (h c s) -> p h s c", h=HEADS, c=2), ACT.Copy).then_inc(hi_ok, 1)

            for b in range(DEC_B):
                idx_keys(b)
            act.wait_ge(once_in, 16 * 5)
            A(gate[:], za[:], ACT.Sigmoid).then_inc(sig_ok, 1)
            keys(0)
            for b in range(DEC_B + 2):
                if b + 1 < DEC_B:
                    keys(b + 1)
                if b < DEC_B:
                    exponentials(b)
                if 1 <= b <= DEC_B:
                    turned(b - 1)
                if b >= 2:
                    high(b - 2)

        @block.gpsimd
        def _(pool):
            for n, to in enumerate((iq, q)):
                pool.wait_ge(once_in, 16 * (5 if n else 3))
                nc.gpsimd.tensor_copy(to[:].rearrange("p b (h t) -> p h b t", t=DEC_S),
                                      stage[:].rearrange("p h (b t) -> p h b t", t=DEC_S)).then_inc(q_ok, 1)
            pool.wait_ge(sig_ok, 1)
            nc.gpsimd.tensor_tensor(gate[:], gate[:], za[:], ALU.mult).then_inc(gate_ok, 1)
            for b in range(DEC_B):
                s = b % 2
                if b >= 2:
                    pool.wait_ge(av_mm, b - 1)
                pool.dma_start(v_rows[:, s], io["cache_v"][0, b].rearrange("(n p) h d -> p n (h d)", p=P)).then_inc(v_in[s], 16)
                pool.dma_start(v_new[:, s], out["v_sample"][0, b].rearrange("t h d -> t (h d)")).then_inc(v_in[s], 16)

        @block.vector
        def _(dve):
            V = nc.vector
            V.memset(pick[:], 0.0).then_inc(once_ok, 1)
            dve.wait_ge(once_ok, 1)
            V.tensor_reduce(pick[:, 112:128], ident[:].rearrange("p (h t) -> p t h", t=DEC_S), AX_X, ALU.add).then_inc(once_ok, 1)
            V.tensor_copy(spread[:], bc(ident[:].rearrange("p (b t) -> p b t", t=DEC_S), 2, HEADS)).then_inc(once_ok, 1)
            V.memset(score[:, DEC_KEYS:DEC_KEYS + 8], DUMMY).then_inc(once_ok, 1)
            dve.wait_ge(w_T, 1)
            V.tensor_scalar(wcol[:].rearrange("p h b -> p (h b)"), ps_p[:, 0:2 * DEC_B], IDX_DIM ** -0.5 * IDX_HEADS ** -0.5, None, ALU.mult).then_inc(once_ok, 1)
            dve.wait_ge(once_ok, 5)
            for b in range(DEC_B):
                for h2 in range(2):
                    dve.wait_ge(s_mm, 2 * b + h2 + 1)
                    if b:
                        dve.wait_ge(sum_mm, 2 * b + h2 - 1)
                    V.tensor_scalar(rel[:, h2], ps_a[h2][:, 0:DEC_KEYS], 0.0, wcol[:, h2, b:b + 1],
                                    ALU.max, ALU.mult).then_inc(rel_ok, 1)
            dve.wait_ge(sum_mm, 2 * DEC_B)
            V.tensor_copy(score[:, 0:DEC_KEYS], ps_sum[:, 0:DEC_KEYS]).then_inc(top, 1)
            n = 1
            for r in range(DEC_TOPK // 8 + 1):
                dve.wait_ge(top, n)
                V.max(top8[:], score[:]).then_inc(top, 1)
                dve.wait_ge(top, n + 1)
                n += 2
                if r == DEC_TOPK // 8:
                    V.memset(top8[:, DEC_TOPK % 8:8], DUMMY).then_inc(top, 1)
                    dve.wait_ge(top, n)
                    n += 1
                V.match_replace(score[:], top8[:], score[:], CHOSEN).then_inc(top, 1)
            dve.wait_ge(top, n)
            V.tensor_scalar(mask[:], score[:, 0:DEC_KEYS], (CHOSEN + UNSEEN) / 2, MASKED, ALU.is_gt, ALU.mult).then_inc(mask_ok, 1)

            def largest(b):
                s = b % 2
                dve.wait_ge(l_mm, b + 1)
                V.tensor_reduce(stat[:, 0, s:s + 1], ps_a[s][:, 0:DEC_KEYS], AX_X, ALU.max).then_inc(max_ok, 1)
                dve.wait_ge(max_ok, b + 1)
                V.tensor_scalar(stat[:, 1, s:s + 1], stat[:, 0, s:s + 1], -SCALE, None, ALU.mult).then_inc(bias_ok, 1)

            def normalise(b):
                s = b % 2
                dve.wait_ge(exp_ok, b + 1)
                V.reciprocal(stat[:, 3, s:s + 1], stat[:, 2, s:s + 1]).then_inc(recip_ok, 1)
                dve.wait_ge(recip_ok, b + 1)
                V.tensor_scalar(probs[:, s], probs[:, s], stat[:, 3, s:s + 1], None, ALU.mult).then_inc(probs_ok, 1)

            def gate_it(b):
                s = b % 2
                dve.wait_ge(av_mm, b + 1)
                dve.wait_ge(gate_ok, 1)
                if b >= 2:
                    dve.wait_ge(lo_ok, b - 1)
                V.tensor_tensor(att[:, s].rearrange("p (h t) -> p h t", h=HEADS), ps_o[s][:, 0:P].rearrange("p (h t) -> p h t", h=HEADS),
                                gate[:, :, DEC_S * b:DEC_S * b + DEC_S], ALU.mult).then_inc(att_ok, 1)

            def low(b):
                dve.wait_ge(hi_ok, b + 1)
                view = lambda m: m[:].rearrange("p h (s n) -> p h s n", s=STEP)[:, :, :, PSTEP + 2 * b:PSTEP + 2 * b + 2]
                V.tensor_tensor(view(mix_lo), att[:, b % 2].rearrange("p (h c s) -> p h s c", h=HEADS, c=2),
                                view(mix_hi).bitcast(F32), ALU.subtract).then_inc(lo_ok, 1)

            for b in range(DEC_B + 3):
                if 1 <= b <= DEC_B:
                    normalise(b - 1)
                if b < DEC_B:
                    largest(b)
                if 3 <= b:
                    low(b - 3)
                if 2 <= b < DEC_B + 2:
                    gate_it(b - 2)

        @block.tensor
        def _(pe):
            M, TR = nc.tensor.matmul, nc.tensor.transpose

            def turn_idx(b):
                s = b % 2
                pe.wait_ge(ik_in[s], 32 * (b // 2 + 1))
                if b >= 2:
                    pe.wait_ge(ik_ok, 2 * b - 2)
                for n in range(BLK):
                    ins = TR(ps_k[s][:, n * P:n * P + P], ik_rows[:, s, n].rearrange("p a d -> p (a d)"), ident[:])
                ins.then_inc(ik_T, 1)

            def scores(b):
                pe.wait_ge(ik_ok, 2 * b + 2)
                for h2 in range(2):
                    half = slice(64 * h2, 64 * h2 + 64)
                    if b:
                        pe.wait_ge(rel_ok, 2 * b + h2 - 1)
                    M(ps_a[h2][:, 0:DEC_KEYS], iq[half, b], ikT[half, b % 2],
                      start=True, stop=True).then_inc(s_mm, 1)

            def sums(b):
                for h2 in range(2):
                    pe.wait_ge(rel_ok, 2 * b + h2 + 1)
                    M(ps_sum[:, 0:DEC_KEYS], pick[:, 112 - DEC_S * b:240 - DEC_S * b], rel[:, h2], start=b + h2 == 0,
                      stop=b == DEC_B - 1 and h2 == 1).then_inc(sum_mm, 1)

            turn_idx(0)
            turn_idx(1)
            pe.wait_ge(w_in_, 32)
            TR(ps_p[:, 0:2 * DEC_B], w_rows[:].rearrange("r a t -> r (a t)"), ident[0:2 * DEC_B, 0:2 * DEC_B]).then_inc(w_T, 1)
            pe.wait_ge(q_ok, 1)
            for b in range(DEC_B):
                scores(b)
                if b:
                    sums(b - 1)
                if b + 2 < DEC_B:
                    turn_idx(b + 2)
            sums(DEC_B - 1)

            def turn_keys(b):
                s = b % 2
                pe.wait_ge(k_in[s], 16 * (b // 2 + 1))
                if b < 2:
                    pe.wait_ge(ik_ok, 2 * DEC_B)
                else:
                    pe.wait_ge(k_ok, 2 * b - 2)
                for h in range(KV_HEADS):
                    for n in range(BLK):
                        c = (h * BLK + n) * P
                        ins = TR(ps_k[s][:, c:c + P], k_rows[:, s, n, h * HD:h * HD + HD], ident[:])
                ins.then_inc(k_T, 1)

            def logits(b):
                s = b % 2
                pe.wait_ge(k_ok, 2 * b + 2)
                if b == 0:
                    pe.wait_ge(mask_ok, 1)
                    pe.wait_ge(q_ok, 2)
                if b < 2:
                    pe.wait_ge(rel_ok, 2 * DEC_B)
                else:
                    pe.wait_ge(exp_ok, b - 1)
                M(ps_a[s][:, 0:DEC_KEYS], spread[:, b].rearrange("p h t -> p (h t)"), mask[:], start=True, stop=False)
                for h in range(KV_HEADS):
                    ins = M(ps_a[s][64 * h:64 * h + 64, 0:DEC_KEYS], q[:, b, 64 * h:64 * h + 64],
                            kT_s[:, s, h], start=False, stop=True)
                ins.then_inc(l_mm, 1)

            def turn(b):
                s = b % 2
                pe.wait_ge(probs_ok, b + 1)
                if b:
                    pe.wait_ge(pT_ok, 2 * b)
                for n in range(BLK + 1):
                    w = P if n < BLK else DEC_S
                    ins = TR(ps_p[0:w, n * P:n * P + P], probs[:, s, n * P:n * P + w], ident[:])
                ins.then_inc(p_T, 1)

            def values(b):
                s = b % 2
                pe.wait_ge(pT_ok, 2 * b + 2)
                pe.wait_ge(v_in[s], 32 * (b // 2 + 1))
                if b >= 2:
                    pe.wait_ge(att_ok, b - 1)
                for h in range(KV_HEADS):
                    for n in range(BLK + 1):
                        w = P if n < BLK else DEC_S
                        v = v_rows[:, s, n, h * HD:h * HD + HD] if n < BLK else v_new[:, s, h * HD:h * HD + HD]
                        ins = M(ps_o[s][:, 64 * h:64 * h + 64], v, pT[0:w, s, n, 64 * h:64 * h + 64],
                                start=n == 0 and h == 0, stop=n == BLK and h == KV_HEADS - 1)
                ins.then_inc(av_mm, 1)

            turn_keys(0)
            turn_keys(1)
            logits(0)
            for b in range(DEC_B + 1):
                if b + 1 < DEC_B:
                    logits(b + 1)
                if b < DEC_B:
                    turn(b)
                if b:
                    values(b - 1)
                if b + 2 < DEC_B:
                    turn_keys(b + 2)


OC = 512
NOC = D_MODEL // OC
ROWS = TOK // STEP
GROUP_TILES = ((0, 5), (5, 4))


def gate_rows(nc, io, keep, scr):
    ident, gpost, sel = keep["ident"], keep["gpost"], keep["sel"]
    with ExitStack() as ctx:
        signals = cleared_after(nc, ctx)

        def sb(name, shape, dt=F32):
            return ctx.enter_context(nc.sbuf_tensor(name, shape, dt))

        def sem(name):
            return new_signal(nc, signals, name)

        HALF_D = D_MODEL // 2
        parts = sb("gate_parts", [P, D_MODEL])
        twice = sb("twice", [P, 2, 32])
        ones = sb("sel_f", [P, ROWS + P])
        bias, post = sb("bias_rows", [P, HALF_D]), sb("post_rows", [P, HALF_D])
        full = sb("gate_full", [P, HALF_D])
        low = sb("low_rows", [P, 1])
        ps_g = [ctx.enter_context(nc.psum_tensor(f"ps_gate{i}", [P, 512], F32)) for i in range(NOC)]
        zero_ok, rows_in, parts_in, twice_ok, ones_ok = (sem(n) for n in ("zero_ok", "g_rows_in", "parts_in", "twice_ok", "ones_ok"))
        g_mm, g_step, sel_step = sem("gate_mm"), sem("gate_step"), sem("sel_step")
        block = ctx.enter_context(nc.Block())

        @block.sync
        def _(sp):
            sp.dma_start(parts[:], scr["gate_dram"]).then_inc(parts_in, 16)
            sp.wait_ge(zero_ok, 2)
            for r in range(4):
                cols = slice(HALF_D * (r // 2), HALF_D * (r // 2) + HALF_D)
                bsrc = io["b_ada"][0:1, 2 * D_MODEL:3 * D_MODEL][:, cols]
                sp.dma_start(bias[32 * r:32 * r + COND, :], bsrc.broadcast_to([COND, HALF_D])).then_inc(rows_in, 16)
                sp.dma_start(post[32 * r:32 * r + COND, :], io["g_post"][:, cols].broadcast_to([COND, HALF_D])).then_inc(rows_in, 16)

        @block.gpsimd
        def _(pool):
            G = nc.gpsimd
            G.memset(ones[:], 0.0).then_inc(sel_step, 1)
            pool.wait_ge(sel_step, 1)
            n = 1
            for base in range(0, P, 32):
                for at in (0, ROWS):
                    G.memset(ones[base:base + 1, at:at + PSTEP], 1.0).then_inc(sel_step, 1)
                    n += 1
            for first in (-2, -1):
                pool.wait_ge(sel_step, n)
                for base in range(0, P, 32):
                    part = ones[base:base + COND, PSTEP:ROWS]
                    G.affine_select(out=part, in_=part, compare_op=ALU.not_equal, fill=1.0, base=first,
                                    pattern=[[-1, ROWS - PSTEP]], channel_multiplier=2).then_inc(sel_step, 1)
                    n += 1
            pool.wait_ge(sel_step, n)
            G.tensor_copy(sel[:], ones[:]).then_inc(ones_ok, 1)

        @block.vector
        def _(dve):
            V = nc.vector
            V.memset(bias[:], 0.0).then_inc(zero_ok, 1)
            V.memset(post[:], 0.0).then_inc(zero_ok, 1)
            for i in range(2):
                V.tensor_reduce(twice[:, i], ident[:].rearrange("p (a c) -> p c a", a=4), AX_X, ALU.add).then_inc(twice_ok, 1)
            V.memset(low[:], 0.0).then_inc(g_step, 1)
            dve.wait_ge(g_step, 1)
            for r in (32, 96):
                V.memset(low[r:r + 32, :], -1.0).then_inc(g_step, 1)
            dve.wait_ge(rows_in, 16 * 8)
            n = 3
            for c in range(NOC):
                rows = slice(64 * (c // 2), 64 * (c // 2) + 64)
                cols = slice(OC * (c % 2), OC * (c % 2) + OC)
                dve.wait_ge(g_mm, c + 1)
                V.tensor_tensor(full[rows, cols], ps_g[c][rows, :], bias[rows, cols], ALU.add).then_inc(g_step, 1)
                dve.wait_ge(g_step, n + 1)
                V.tensor_tensor(full[rows, cols], full[rows, cols], post[rows, cols], ALU.mult).then_inc(g_step, 1)
                n += 2
            dve.wait_ge(g_step, n)
            V.tensor_copy(gpost[:], full[:]).then_inc(g_step, 1)
            dve.wait_ge(g_step, n + 1)
            V.scalar_tensor_tensor(bias[:], gpost[:].bitcast(F32), low[:], full[:], ALU.mult, ALU.add).then_inc(g_step, 1)
            dve.wait_ge(g_step, n + 2)
            V.tensor_copy(gpost[:], bias[:]).then_inc(g_step, 1)

        @block.tensor
        def _(pe):
            pe.wait_ge(parts_in, 16)
            pe.wait_ge(twice_ok, 2)
            for c in range(NOC):
                rows = slice(64 * (c // 2), 64 * (c // 2) + 64)
                nc.tensor.matmul(ps_g[c][rows, :], twice[:].rearrange("p a c -> p (a c)"), parts[:, OC * c:OC * c + OC],
                                 start=True, stop=True).then_inc(g_mm, 1)


def project_out(nc, io, out, keep, scr):
    gpost, sel = keep["gpost"], keep["sel"]
    MIX_HI, MIX_LO = (keep["attn_hi"], keep["ssm_hi"]), (keep["attn_lo"], keep["ssm_lo"])
    NB = KB // 2
    with ExitStack() as ctx:
        signals = cleared_after(nc, ctx)

        def sb(name, shape, dt=F32):
            return ctx.enter_context(nc.sbuf_tensor(name, shape, dt))

        def sem(name):
            return new_signal(nc, signals, name)

        rows = [nc.alloc_sbuf_tensor_at("out_rows0", [P, D_MODEL], F32, offset=keep["maskb_base"])]
        square = nc.alloc_sbuf_tensor_at("out_square", [P, OC], BF16, offset=keep["maskb_base"] + 4 * D_MODEL)
        rows += [sb(f"out_rows{i}", [P, D_MODEL]) for i in range(1, 5)]
        w_raw = sb("o_raw", [P, 2, OC])
        w_hi, w_lo = sb("o_hi", [P, 2, OC], F32R), sb("o_lo", [P, 2, OC], F32R)
        xs = sb("x_add", [P, 2, OC])
        ssq = sb("ssq", [P, 5, NOC])
        stat = sb("out_stat", [P, 5, 5])
        ps_o = [ctx.enter_context(nc.psum_tensor(f"ps_out{i}", [P, 512], F32)) for i in range(5)]
        ps_g = [ctx.enter_context(nc.psum_tensor(f"ps_gt{i}", [P, 512], F32)) for i in range(2)]

        w_in = [sem("ow_in0"), sem("ow_in1")]
        x_in = [[sem(f"x_quarter_in{i}") for i in range(2)], [sem(f"x_half_in{i}") for i in range(3)]]
        w_hi_ok, w_lo_ok, w_used = sem("ow_hi"), sem("ow_lo"), sem("ow_used")
        out_mm, out_read, squared = sem("out_mm"), sem("out_read"), sem("out_sq")
        rstd_step, root_ok, g_mm, scaled = (sem(n) for n in ("rstd_step", "o_root", "g_copied", "scaled"))
        y_ok = [sem("y_ok0"), sem("y_ok1")]
        y_out = [sem(f"y_out{i}") for i in range(5)]
        passed, passed_v, ssq_ready = sem("passed_o"), sem("passed_v"), sem("ssq_ready")
        block = ctx.enter_context(nc.Block())
        wv = io["w_out"][0].rearrange("(k p) n -> p k n", p=P)

        def pieces(tile, dram_p, dram_s):
            found = []
            c = P * tile
            while c < P * tile + P:
                s, m = divmod(c, ROWS)
                end = min(P * tile + P, ROWS * s + (PSTEP if m < PSTEP else ROWS))
                dram, m = (dram_p, m) if m < PSTEP else (dram_s, m - PSTEP)
                v = dram.rearrange("(m s) d -> s m d", s=STEP)[s, m:m + end - c]
                found.append((c - P * tile, end - c, v))
                c = end
            return found

        xv = (io["x_prompt"].rearrange("b t d -> (b t) d"), io["x_sample"].rearrange("b t d -> (b t) d"))
        yv = (out["y_prompt"].rearrange("b t d -> (b t) d"), out["y_sample"].rearrange("b t d -> (b t) d"))
        finals = [[(i, q) for i in range(n) for q in range(NOC)] for _, n in GROUP_TILES]
        before = (0, len(finals[0]))
        PIECES = KB * NOC

        def y_left(g, i):
            return sum(16 * 2 * len(pieces(t0 + i, *yv)) for gg, (t0, n) in enumerate(GROUP_TILES) if gg <= g and i < n)

        HALF_D = D_MODEL // 2
        x_slots = ([xs[:, 0], xs[:, 1]], [rows[4][:, 0:HALF_D], rows[4][:, HALF_D:], xs[:].rearrange("p a c -> p (a c)")])
        XW = (OC, HALF_D)
        halves = [2 * n for _, n in GROUP_TILES]

        def x_landed(g, k):
            per_tile, slots = D_MODEL // XW[g], len(x_slots[g])
            return sum(16 * len(pieces(GROUP_TILES[g][0] + h // per_tile, *xv)) for h in range(k % slots, k + 1, slots))

        def half_added(eng, g, H):
            for n in (before[g] + 2 * H, before[g] + 2 * H + 1):
                eng.wait_ge(y_ok[n % 2], n // 2 + 1)

        def load_x(eng, g, k):
            per_tile, slot = D_MODEL // XW[g], k % len(x_slots[g])
            cols = slice(XW[g] * (k % per_tile), XW[g] * (k % per_tile) + XW[g])
            for p0, m, v in pieces(GROUP_TILES[g][0] + k // per_tile, *xv):
                eng.dma_start(x_slots[g][slot][p0:p0 + m], v[:, cols]).then_inc(x_in[g][slot], 16)

        def x_piece(g, f):
            k = f if g == 0 else f // 2
            slot = k % len(x_slots[g])
            c0 = 0 if g == 0 else OC * (f % 2)
            return k, slot, x_slots[g][slot][:, c0:c0 + OC]

        def store_half(eng, g, H):
            half_added(eng, g, H)
            cols = slice(HALF_D * (H % 2), HALF_D * (H % 2) + HALF_D)
            for p0, m, v in pieces(GROUP_TILES[g][0] + H // 2, *yv):
                eng.dma_start(v[:, cols], rows[H // 2][p0:p0 + m, cols]).then_inc(y_out[H // 2], 16)

        def tiles_before(g, c):
            return c * GROUP_TILES[g][1] + (NOC * GROUP_TILES[0][1] if g else 0)

        def half_at(g, c, kb):
            if g == 0 or not isinstance(c, int) or c:
                return []
            return [H for H in range(halves[0]) if 1 + 7 * H // 5 == kb]

        def finals_at(g, c, kb):
            return [f for H in half_at(g, c, kb) for f in (2 * H, 2 * H + 1)]

        def chunks(eng, body):
            for g in range(2):
                body(g, 0)
                with eng.Fori(1, NOC - 1) as c:
                    body(g, c)
                body(g, NOC - 1)

        @block.sync
        def _(sp):
            def send(g, c, kb):
                for f in finals_at(g, c, kb - 2):
                    if f >= 2:
                        sp.wait_ge(y_ok[f % 2], f // 2)
                    load_x(sp, 0, f)
                for H in half_at(g, c, kb - 4):
                    store_half(sp, 0, H)

            def body(g, c):
                for kb in range(KB):
                    if g or kb >= 2 or not isinstance(c, int) or c:
                        sp.wait_ge(w_lo_ok, c * KB + (g * PIECES + kb - 1))
                    sp.dma_start(w_raw[:, kb % 2], wv[:, kb, bass.ds(c * OC, OC)]).then_inc(w_in[kb % 2], 16)
                    send(g, c, kb)
                for kb in (KB, KB + 1):
                    send(g, c, kb)

            chunks(sp, body)
            sp.wait_ge(y_out[4], y_left(0, 4))
            for H in range(halves[1]):
                if H == 2:
                    half_added(sp, 0, halves[0] - 1)
                elif H > 2:
                    half_added(sp, 1, H - 3)
                load_x(sp, 1, H)
            for i in range(5):
                sp.wait_ge(y_out[i], y_left(1, i))

        @block.gpsimd
        def _(pool):
            for g in range(2):
                for f, (i, q) in enumerate(finals[g]):
                    n = before[g] + f
                    if g and n % 2:
                        continue
                    part = rows[i][:, OC * q:OC * q + OC]
                    k, slot, x = x_piece(g, f)
                    pool.wait_ge(x_in[g][slot], x_landed(g, k))
                    pool.wait_ge(scaled, n + 1)
                    nc.gpsimd.tensor_tensor(part, part, x, ALU.add).then_inc(y_ok[n % 2], 1)

        @block.scalar
        def _(act):
            A = nc.scalar.activation

            def high(g, c, kb):
                act.wait_ge(w_in[kb % 2], c * (8 * KB) + 16 * (g * PIECES // 2 + kb // 2 + 1))
                if kb == 1:
                    if g or not isinstance(c, int) or c:
                        act.wait_ge(out_mm, tiles_before(g, c))
                elif not (g == 0 and isinstance(c, int) and c == 0 and kb == 0):
                    act.wait_ge(w_used, c * (KB - 1) + (g * NOC * (KB - 1) + max(kb - 1, 0)))
                A(w_hi[:, kb % 2], w_raw[:, kb % 2], ACT.Copy).then_inc(w_hi_ok, 1)

            def body(g, c):
                for kb in range(1, KB):
                    high(g, c, kb)
                last = isinstance(c, int) and c == NOC - 1
                if not last:
                    high(g, c + 1, 0)
                elif g == 0:
                    high(1, 0, 0)
                for i in range(GROUP_TILES[g][1]):
                    if g and isinstance(c, int) and c == 0:
                        act.wait_ge(y_out[i], y_left(0, i))
                    act.wait_ge(out_mm, tiles_before(g, c) + (i + 1))
                    if g or i or not isinstance(c, int) or c:
                        act.wait_ge(squared, tiles_before(g, c) + i)
                    act.sem_inc(passed, 1)
                    A(square[:], ps_o[i][:], ACT.Square, accum_out=ssq[:, i, bass.ds(c, 1)]).then_inc(squared, 1)
                    A(rows[i][:, bass.ds(c * OC, OC)], ps_o[i][:], ACT.Copy).then_inc(out_read, 1)
                if last:
                    act.wait_ge(rstd_step, 8 * g + 2)
                    A(stat[:, 2], stat[:, 1], ACT.Sqrt).then_inc(root_ok, 1)

            act.wait_ge(ssq_ready, 1)
            high(0, 0, 0)
            chunks(act, body)
            for H in range(halves[1]):
                store_half(act, 1, H)

        @block.vector
        def _(dve):
            V = nc.vector

            def low(g, c, kb):
                dve.wait_ge(w_hi_ok, c * KB + (g * PIECES + kb + 1))
                V.tensor_tensor(w_lo[:, kb % 2], w_raw[:, kb % 2], w_hi[:, kb % 2].bitcast(F32), ALU.subtract).then_inc(w_lo_ok, 1)

            def scale(g, f):
                i, q = finals[g][f]
                part = rows[i][:, OC * q:OC * q + OC]
                dve.wait_ge(g_mm, before[g] + f + 1)
                V.scalar_tensor_tensor(part, part, stat[:, 4, i:i + 1], ps_g[(before[g] + f) % 2][:], ALU.mult, ALU.mult).then_inc(scaled, 1)

            def rstd(g):
                n = 8 * g
                dve.wait_ge(squared, tiles_before(g, NOC))
                V.tensor_reduce(stat[:, 0], ssq[:], AX_X, ALU.add).then_inc(rstd_step, 1)
                dve.wait_ge(rstd_step, n + 1)
                V.tensor_scalar(stat[:, 1], stat[:, 0], 1.0 / D_MODEL, EPS, ALU.mult, ALU.add).then_inc(rstd_step, 1)
                dve.wait_ge(root_ok, g + 1)
                V.reciprocal(stat[:, 3], stat[:, 2]).then_inc(rstd_step, 1)
                dve.wait_ge(rstd_step, n + 3)
                V.tensor_tensor(stat[:, 4], stat[:, 3], stat[:, 3], ALU.mult).then_inc(rstd_step, 1)
                dve.wait_ge(rstd_step, n + 4)
                V.tensor_tensor(stat[:, 4], stat[:, 4], stat[:, 1], ALU.mult).then_inc(rstd_step, 1)
                dve.wait_ge(rstd_step, n + 5)
                V.tensor_scalar(stat[:, 4], stat[:, 4], -0.5, 1.5, ALU.mult, ALU.add).then_inc(rstd_step, 1)
                dve.wait_ge(rstd_step, n + 6)
                V.tensor_tensor(stat[:, 4], stat[:, 4], stat[:, 3], ALU.mult).then_inc(rstd_step, 1)
                dve.wait_ge(rstd_step, n + 7)
                dve.sem_inc(rstd_step, 1)

            def body(g, c):
                last = isinstance(c, int) and c == NOC - 1
                for kb in range(1, KB):
                    low(g, c, kb)
                    for f in finals_at(g, c, kb - 1):
                        scale(0, f)
                if not last:
                    low(g, c + 1, 0)
                elif g == 0:
                    low(1, 0, 0)
                if last:
                    rstd(g)

            V.memset(ssq[:], 1.0).then_inc(passed_v, 1)
            dve.wait_ge(passed_v, 1)
            dve.sem_inc(ssq_ready, 1)
            low(0, 0, 0)
            chunks(dve, body)
            for f, (i, q) in enumerate(finals[1]):
                scale(1, f)
                n = before[1] + f
                if n % 2:
                    part = rows[i][:, OC * q:OC * q + OC]
                    dve.wait_ge(scaled, n + 1)
                    k, slot, x = x_piece(1, f)
                    dve.wait_ge(x_in[1][slot], x_landed(1, k))
                    V.tensor_tensor(part, part, x, ALU.add).then_inc(y_ok[n % 2], 1)

        @block.tensor
        def _(pe):
            M = nc.tensor.matmul

            def gates(g, f):
                i, q = finals[g][f]
                n = before[g] + f
                half = slice(64 * (q // 2), 64 * (q // 2) + 64)
                c0 = P * (GROUP_TILES[g][0] + i) % ROWS
                if n >= 2:
                    pe.wait_ge(scaled, n - 1)
                M(ps_g[n % 2][:], sel[half, c0:c0 + P], gpost[half, OC * (q % 2):OC * (q % 2) + OC],
                  start=True, stop=True).then_inc(g_mm, 1)

            def body(g, c):
                t0, tiles = GROUP_TILES[g]
                for kb in range(KB):
                    hi, lo = MIX_HI[kb // NB], MIX_LO[kb // NB]
                    pe.wait_ge(w_lo_ok, c * KB + (g * PIECES + kb + 1))
                    for i in range(tiles):
                        if kb == 0 and (g or not isinstance(c, int) or c):
                            first = isinstance(c, int) and c == 0
                            pe.wait_ge(out_read, tiles_before(g, c) + (i + 1 - GROUP_TILES[0 if first else g][1]))
                            pe.wait_ge(squared, tiles_before(g, c) + (i + 1 - GROUP_TILES[0 if first else g][1]))
                        cols = slice(P * (t0 + i), P * (t0 + i) + P)
                        M(ps_o[i][:], hi[:, kb % NB, cols], w_hi[:, kb % 2], start=kb == 0, stop=False)
                        M(ps_o[i][:], hi[:, kb % NB, cols], w_lo[:, kb % 2], start=False, stop=False)
                        ins = M(ps_o[i][:], lo[:, kb % NB, cols], w_hi[:, kb % 2], start=False, stop=kb == KB - 1)
                        if kb == KB - 1:
                            ins.then_inc(out_mm, 1)
                    if kb < KB - 1:
                        ins.then_inc(w_used, 1)
                    for f in finals_at(g, c, kb):
                        gates(0, f)

            chunks(pe, body)
            for f in range(len(finals[1])):
                gates(1, f)


_INS = ("x_prompt", "x_sample", "c_prompt", "c_sample", "cache_k", "cache_v", "cache_idx_k", "state_ssm_re",
        "state_ssm_im", "w_ada", "b_ada", "g_pre", "g_post", "w_in", "lambda_re", "lambda_im", "log_dt", "b_re",
        "b_im", "c_re", "c_im", "d_skip", "w_glu", "b_glu", "w_out")
_OUTS = (
    ("y_prompt", (1, SEQ, D_MODEL)), ("y_sample", (DEC_B, DEC_S, D_MODEL)),
    ("k_prompt", (1, 1, SEQ, KV_HEADS, HD)), ("v_prompt", (1, 1, SEQ, KV_HEADS, HD)), ("idx_k_prompt", (1, 1, SEQ, IDX_DIM)),
    ("ssm_re_prompt", (1, 1, GROUPS, STATE)), ("ssm_im_prompt", (1, 1, GROUPS, STATE)),
    ("k_sample", (1, DEC_B, DEC_S, KV_HEADS, HD)), ("v_sample", (1, DEC_B, DEC_S, KV_HEADS, HD)),
    ("idx_k_sample", (1, DEC_B, DEC_S, IDX_DIM)),
    ("ssm_re_sample", (1, DEC_B, GROUPS, STATE)), ("ssm_im_sample", (1, DEC_B, GROUPS, STATE)),
)


def hybrid_layer(nc, io, out):
    scr = {name: nc.dram_tensor(name, shape, F32, kind="Internal").ap() for name, shape in (
        ("zt", [COLS, TOK]), ("s5_in", [P, PAIRS, 2, P]), ("s5_out", [P, PAIRS, 2, P]),
        ("taps", [GROUPS, CH, TAPS * CH]), ("y", [1024, TOK]), ("gate_dram", [P, D_MODEL]))}
    with ExitStack() as ctx:
        def sb(name, shape, dt=F32):
            return ctx.enter_context(nc.sbuf_tensor(name, shape, dt))

        keep = {"ident": sb("ident", [P, P]), "vecT": sb("vecT", [P, 72])}
        mod_base = nc.sbuf_base
        keep["mod"] = sb("mod", [P, 2 * KB, COND])
        keep["s5_tabs"] = sb("s5_tabs", [P, 5, PAIRS])
        keep["maskb_base"] = nc.sbuf_base
        keep["maskb"] = sb("maskb", [P, P * (NT - 1) * NT // 2], BF16)
        with ExitStack() as early:
            keep["cT"] = early.enter_context(nc.sbuf_tensor("cT", [P, KB, 32], F32))
            keep["xT_base"] = (nc.sbuf_base + 31) // 32 * 32
            keep["xT"] = early.enter_context(nc.sbuf_tensor("xT", [P, KB, TOK], F32))
            keep["shared_base"] = (nc.sbuf_base + 31) // 32 * 32
            early.enter_context(nc.sbuf_tensor("beside_xT", [P, KB, TOK], F32))
            prepare(nc, io, keep, scr)
            project_in(nc, io, keep, scr)
        scan_states(nc, io, out, keep, scr)
        keep["ssm_base"] = (nc.sbuf_base + 31) // 32 * 32
        keep["ssm_hi"], keep["ssm_lo"] = sb("ssm_hi", [P, 8, TOK], F32R), sb("ssm_lo", [P, 8, TOK], F32R)
        gate_states(nc, io, out, keep, scr)
        keep["attn_hi"], keep["attn_lo"] = sb("attn_hi", [P, 8, TOK], F32R), sb("attn_lo", [P, 8, TOK], F32R)
        with nc.sbuf_tensor("kT", [P, KV_HEADS, TOK], F32) as kT:
            keep["kT"] = kT
            with nc.sbuf_tensor("v_nat", [P, SEQ // P, KV_HEADS * HD], F32) as v_nat:
                keep["v_nat"] = v_nat
                attend_prompt(nc, out, keep, scr)
            attend_samples(nc, io, out, keep, scr)
        keep["gpost"] = sb("gpost", [P, D_MODEL // 2], F32R)
        keep["sel"] = nc.alloc_sbuf_tensor_at("sel", [P, ROWS + P], F32R, offset=mod_base)
        gate_rows(nc, io, keep, scr)
        project_out(nc, io, out, keep, scr)


def kernel(**inputs):
    import numpy as _np
    import concourse.bacc as _bacc
    from concourse.bass_utils import run_bass_kernel_spmd as _run

    nc = _bacc.Bacc("TRN2", target_bir_lowering=False, num_devices=1)
    arrays, io = {}, {}
    for name in _INS:
        a = _np.ascontiguousarray(inputs[name])
        arrays[f"in_{name}"] = a
        io[name] = nc.dram_tensor(f"in_{name}", a.shape, mybir.dt.from_np(a.dtype), kind="ExternalInput").ap()
    out = {name: nc.dram_tensor(f"out_{name}", list(shape), F32, kind="ExternalOutput").ap() for name, shape in _OUTS}
    hybrid_layer(nc, io, out)
    r = _run(nc, [arrays], core_ids=[0])
    return tuple(r.results[0][f"out_{name}"] for name, _ in _OUTS)
```
